# Optimizing a Trainium2 kernel written in Bass

```python
import jax, jax.numpy as jnp
from jax import lax
import numpy as np

D_MODEL = 1024
BATCH = 1
SEQ = 512
DEPTH = 2

DN_HEAD_DIM = 128
DN_HEADS = D_MODEL // (2 * DN_HEAD_DIM)
DN_WIDTH = DN_HEADS * DN_HEAD_DIM
DN_CONV = 5
DN_CHUNK = 64
HG_EXPAND = 128
HG_HEAD_DIM = 128
HG_HEADS = D_MODEL // (2 * HG_HEAD_DIM)
HG_KEY_WIDTH = HG_HEADS * HG_EXPAND
HG_VAL_WIDTH = HG_HEADS * HG_HEAD_DIM
HG_CHUNK = 32
D_FF = 2816
FFN_CONV = 3
EPS = 1e-6

IN_SIZES = (3 * DN_WIDTH, DN_WIDTH, 2 * DN_HEADS, 2 * DN_HEADS,
            HG_KEY_WIDTH, HG_KEY_WIDTH, HG_KEY_WIDTH, HG_VAL_WIDTH, HG_VAL_WIDTH,
            D_MODEL, D_MODEL)
IN_COLS = 4 * DN_WIDTH + 4 * DN_HEADS + 3 * HG_KEY_WIDTH + 2 * HG_VAL_WIDTH + 2 * D_MODEL


def _split(x, sizes):
    idx = np.cumsum(np.array(sizes))[:-1].tolist()
    return jnp.split(x, idx, axis=-1)

def _rmsnorm(x, w):
    xf = x.astype(jnp.float32)
    y = xf * lax.rsqrt(jnp.mean(xf * xf, axis=-1, keepdims=True) + EPS)
    return (y * w.astype(jnp.float32)).astype(x.dtype)

def _gated_rmsnorm(o, z, w):
    y = o * lax.rsqrt(jnp.mean(o * o, axis=-1, keepdims=True) + EPS)
    return y * w.astype(jnp.float32) * jax.nn.silu(z)

def _l2norm(x):
    return x * lax.rsqrt(jnp.sum(x * x, axis=-1, keepdims=True) + EPS)

def _dwconv(x, w):
    return lax.conv_general_dilated(x, w[:, None, :].astype(x.dtype), window_strides=(1,),
                                    padding='SAME', dimension_numbers=('NWC', 'WIO', 'NWC'),
                                    feature_group_count=x.shape[-1])

def _to_heads(x, n):
    b, s, _ = x.shape
    return x.reshape(b, s, n, -1).transpose(0, 2, 1, 3)

def _gated_delta_rule(q, k, v, beta, g):
    b, h, s, dk = q.shape
    dv = v.shape[-1]
    c = DN_CHUNK
    n = s // c
    q = q.reshape(b, h, n, c, dk)
    k = k.reshape(b, h, n, c, dk)
    v = v.reshape(b, h, n, c, dv)
    beta = beta.reshape(b, h, n, c)
    gc = jnp.cumsum(g.reshape(b, h, n, c), axis=-1)
    incl = jnp.tril(jnp.ones((c, c), dtype=bool))
    strict = jnp.tril(jnp.ones((c, c), dtype=bool), k=-1)
    decay = jnp.exp(jnp.where(incl, gc[..., :, None] - gc[..., None, :], -jnp.inf))
    kb = k * beta[..., None]
    a = jnp.where(strict, jnp.einsum('bhntd,bhnsd->bhnts', kb, k) * decay, 0.0)
    eye = jnp.eye(c, dtype=q.dtype)
    t_inv = lax.linalg.triangular_solve(a + eye, jnp.broadcast_to(eye, a.shape),
                                        left_side=True, lower=True, unit_diagonal=True)
    u = jnp.einsum('bhnts,bhnsv->bhntv', t_inv, v * beta[..., None])
    w = jnp.einsum('bhnts,bhnsd->bhntd', t_inv, kb * jnp.exp(gc)[..., None])
    qk = jnp.einsum('bhntd,bhnsd->bhnts', q, k) * decay
    qg = q * jnp.exp(gc)[..., None]
    kd = k * jnp.exp(gc[..., -1:] - gc)[..., None]
    gl = jnp.exp(gc[..., -1])
    xs = (jnp.moveaxis(u, 2, 0), jnp.moveaxis(w, 2, 0), jnp.moveaxis(qk, 2, 0),
          jnp.moveaxis(qg, 2, 0), jnp.moveaxis(kd, 2, 0), jnp.moveaxis(gl, 2, 0))

    def step(state, inp):
        u_n, w_n, qk_n, qg_n, kd_n, gl_n = inp
        v_new = u_n - jnp.einsum('bhtd,bhdv->bhtv', w_n, state)
        o = jnp.einsum('bhtd,bhdv->bhtv', qg_n, state) + jnp.einsum('bhts,bhsv->bhtv', qk_n, v_new)
        state = state * gl_n[..., None, None] + jnp.einsum('bhsd,bhsv->bhdv', kd_n, v_new)
        return state, o

    state0 = jnp.zeros((b, h, dk, dv), dtype=q.dtype)
    _, o = lax.scan(step, state0, xs)
    return jnp.moveaxis(o, 0, 2).reshape(b, h, s, dv)

def _hgrn2_scan(q, k, i, logf):
    b, h, s, dk = q.shape
    dv = i.shape[-1]
    c = HG_CHUNK
    n = s // c
    q = jnp.moveaxis(q.reshape(b, h, n, c, dk), 2, 0)
    k = jnp.moveaxis(k.reshape(b, h, n, c, dk), 2, 0)
    i = jnp.moveaxis(i.reshape(b, h, n, c, dv), 2, 0)
    bc = jnp.moveaxis(jnp.cumsum(logf.reshape(b, h, n, c, dk), axis=-2), 2, 0)
    incl = jnp.tril(jnp.ones((c, c), dtype=bool))[:, :, None]

    def step(state, inp):
        q_n, k_n, i_n, b_n = inp
        dec = jnp.exp(jnp.where(incl, b_n[:, :, :, None, :] - b_n[:, :, None, :, :], -jnp.inf))
        att = jnp.einsum('bhtd,bhsd,bhtsd->bhts', q_n, k_n, dec)
        o = (jnp.einsum('bhtd,bhdv->bhtv', q_n * jnp.exp(b_n), state)
             + jnp.einsum('bhts,bhsv->bhtv', att, i_n))
        last = b_n[:, :, -1:, :]
        state = (state * jnp.exp(last[:, :, 0, :])[..., None]
                 + jnp.einsum('bhsd,bhsv->bhdv', k_n * jnp.exp(last - b_n), i_n))
        return state, o

    state0 = jnp.zeros((b, h, dk, dv), dtype=q.dtype)
    _, o = lax.scan(step, state0, (q, k, i, bc))
    return jnp.moveaxis(o, 0, 2).reshape(b, h, s, dv)

def _flip(t):
    return jnp.flip(t, axis=2)

def _mixer(h, w_in, dn_conv, dn_a_log, dn_dt_bias, dn_norm, lb, hg_norm, w_branch_dn, w_branch_hg, w_out):
    b, s, _ = h.shape
    f32 = jnp.float32
    p = h @ w_in
    (qkv, z, beta_r, a_r, hq, hf_fwd, hf_bwd, hi, hgate, gate_dn, gate_hg) = _split(p, IN_SIZES)

    qkv = jax.nn.silu(_dwconv(qkv, dn_conv)).astype(f32)
    q, k, v = _split(qkv, (DN_WIDTH, DN_WIDTH, DN_WIDTH))
    q = _l2norm(_to_heads(q, DN_HEADS)) * (DN_HEAD_DIM ** -0.5)
    k = _l2norm(_to_heads(k, DN_HEADS))
    v = _to_heads(v, DN_HEADS)
    beta = jax.nn.sigmoid(beta_r.astype(f32)).reshape(b, s, 2, DN_HEADS).transpose(2, 0, 3, 1)
    g = (-jnp.exp(dn_a_log.astype(f32))
         * jax.nn.softplus(a_r.astype(f32).reshape(b, s, 2, DN_HEADS) + dn_dt_bias.astype(f32)))
    g = g.transpose(2, 0, 3, 1)
    o_f = _gated_delta_rule(q, k, v, beta[0], g[0])
    o_b = _flip(_gated_delta_rule(_flip(q), _flip(k), _flip(v), _flip(beta[1]), _flip(g[1])))
    o_dn = (o_f + o_b).transpose(0, 2, 1, 3)
    o_dn = _gated_rmsnorm(o_dn, z.astype(f32).reshape(b, s, DN_HEADS, DN_HEAD_DIM), dn_norm)
    o_dn = o_dn.reshape(b, s, DN_WIDTH).astype(h.dtype)

    lb = lb.astype(f32)
    qh = _to_heads(jax.nn.silu(hq.astype(f32)), HG_HEADS) * (HG_EXPAND ** -0.5)
    ih = _to_heads(hi.astype(f32), HG_HEADS)
    outs = []
    for d, fr in enumerate((hf_fwd, hf_bwd)):
        fr = fr.astype(f32)
        logf = jax.nn.log_sigmoid(fr) + jnp.log1p(lb[d] * jnp.exp(-fr))
        kk = (1.0 - lb[d]) * jax.nn.sigmoid(-fr)
        outs.append((_to_heads(kk, HG_HEADS), _to_heads(logf, HG_HEADS)))
    o_hf = _hgrn2_scan(qh, outs[0][0], ih, outs[0][1])
    o_hb = _flip(_hgrn2_scan(_flip(qh), _flip(outs[1][0]), _flip(ih), _flip(outs[1][1])))
    o_hg = (o_hf + o_hb).transpose(0, 2, 1, 3)
    o_hg = _gated_rmsnorm(o_hg, hgate.astype(f32).reshape(b, s, HG_HEADS, HG_HEAD_DIM), hg_norm)
    o_hg = o_hg.reshape(b, s, HG_VAL_WIDTH).astype(h.dtype)

    merged = (jax.nn.sigmoid(gate_dn) * (o_dn @ w_branch_dn)
              + jax.nn.sigmoid(gate_hg) * (o_hg @ w_branch_hg))
    return merged @ w_out

def _conv_ffn(h, w_up, ffn_conv, ffn_conv_bias, w_down):
    gate, up = _split(h @ w_up, (D_FF, D_FF))
    gate = _dwconv(gate, ffn_conv) + ffn_conv_bias
    return (jax.nn.silu(gate) * up) @ w_down

def _log(v):
    return float(np.log(v))

def first_inputs(seed: int = 0) -> dict:
    key = jax.random.key(seed)
    ks = jax.random.split(key, 20)
    f32 = jnp.float32
    nrm = lambda k, shape, scale: jax.random.normal(k, shape, f32) * scale
    dt = jnp.exp(jax.random.uniform(ks[5], (DEPTH, 2, DN_HEADS), f32)
                 * (_log(0.1) - _log(0.001)) + _log(0.001))
    return {
        'x': nrm(ks[0], (BATCH, SEQ, D_MODEL), 1.0),
        'mix_norm': 1.0 + nrm(ks[1], (DEPTH, D_MODEL), 0.02),
        'w_in': nrm(ks[2], (DEPTH, D_MODEL, IN_COLS), D_MODEL ** -0.5),
        'dn_conv': nrm(ks[3], (DEPTH, DN_CONV, 3 * DN_WIDTH), DN_CONV ** -0.5),
        'dn_a_log': jnp.log(jax.random.uniform(ks[4], (DEPTH, 2, DN_HEADS), f32, 1.0, 16.0)),
        'dn_dt_bias': dt + jnp.log(-jnp.expm1(-dt)),
        'dn_norm': 1.0 + nrm(ks[6], (DEPTH, DN_HEAD_DIM), 0.02),
        'hg_lb_logits': nrm(ks[7], (DEPTH, 2, HG_KEY_WIDTH), 1.0),
        'hg_norm': 1.0 + nrm(ks[8], (DEPTH, HG_HEAD_DIM), 0.02),
        'w_branch_dn': nrm(ks[9], (DEPTH, DN_WIDTH, D_MODEL), DN_WIDTH ** -0.5),
        'w_branch_hg': nrm(ks[10], (DEPTH, HG_VAL_WIDTH, D_MODEL), HG_VAL_WIDTH ** -0.5),
        'w_out': nrm(ks[11], (DEPTH, D_MODEL, D_MODEL), D_MODEL ** -0.5),
        'ffn_norm': 1.0 + nrm(ks[12], (DEPTH, D_MODEL), 0.02),
        'w_up': nrm(ks[13], (DEPTH, D_MODEL, 2 * D_FF), D_MODEL ** -0.5),
        'ffn_conv': nrm(ks[14], (DEPTH, FFN_CONV, D_FF), FFN_CONV ** -0.5),
        'ffn_conv_bias': nrm(ks[15], (DEPTH, D_FF), 0.02),
        'w_down': nrm(ks[16], (DEPTH, D_FF, D_MODEL), D_FF ** -0.5),
        'final_norm': 1.0 + nrm(ks[17], (D_MODEL,), 0.02),
    }

def first_block(x, mix_norm, w_in, dn_conv, dn_a_log, dn_dt_bias, dn_norm, hg_lb_logits, hg_norm,
              w_branch_dn, w_branch_hg, w_out, ffn_norm, w_up, ffn_conv, ffn_conv_bias, w_down, final_norm):
    sm = jax.nn.softmax(hg_lb_logits.astype(jnp.float32), axis=0)
    lb_all = jnp.clip(jnp.cumsum(sm, axis=0) - sm[0:1], 0.0, 1.0)
    for l in range(DEPTH):
        h = _rmsnorm(x, mix_norm[l])
        x = x + _mixer(h, w_in[l], dn_conv[l], dn_a_log[l], dn_dt_bias[l], dn_norm[l], lb_all[l],
                       hg_norm[l], w_branch_dn[l], w_branch_hg[l], w_out[l])
        h = _rmsnorm(x, ffn_norm[l])
        x = x + _conv_ffn(h, w_up[l], ffn_conv[l], ffn_conv_bias[l], w_down[l])
    return _rmsnorm(x, final_norm)


DEPTH_2 = 1

N_MIXERS = 4
MIX_W = D_MODEL // N_MIXERS
HEAD_DIM = 64
N_Q_HEADS = MIX_W // HEAD_DIM
N_KV_HEADS = 2
Q_PER_KV = N_Q_HEADS // N_KV_HEADS
KV_W = N_KV_HEADS * HEAD_DIM
GMLP_GROUPS = 4
GMLP_CHUNK = 128
CMP_LEN = 32
CMP_STRIDE = 16
CMP_HIDDEN = 128
SEL_BLOCK = 64
SEL_TOPK = 8
N_LOCAL_BLOCKS = 2
WINDOW = 512
Q_BLOCK = 128
CONF_KERNEL = 31
SCONV_KERNEL = 3
D_FF_2 = 4 * D_MODEL
NSA_GATE_W = N_Q_HEADS * 3
IN_WIDTHS = (MIX_W, MIX_W, MIX_W, KV_W, KV_W, KV_W, KV_W, KV_W, KV_W, NSA_GATE_W, MIX_W, MIX_W, MIX_W, MIX_W, MIX_W)
IN_COLS_2 = sum(IN_WIDTHS)
NEG_INF = -1e30


def _rms(x, g, eps=1e-6):
    xf = x.astype(jnp.float32)
    y = xf * lax.rsqrt(jnp.mean(xf * xf, axis=-1, keepdims=True) + eps)
    return (y * g.astype(jnp.float32)).astype(x.dtype)

def _layernorm(x, g, b, eps=1e-5):
    xf = x.astype(jnp.float32)
    mu = jnp.mean(xf, axis=-1, keepdims=True)
    var = jnp.mean(jnp.square(xf - mu), axis=-1, keepdims=True)
    return ((xf - mu) * lax.rsqrt(var + eps) * g.astype(jnp.float32) + b.astype(jnp.float32)).astype(x.dtype)

def _causal_depthwise_conv(x, w):
    k = w.shape[0]
    return lax.conv_general_dilated(x, w[:, None, :].astype(x.dtype), window_strides=(1,),
                                    padding=[(k - 1, 0)], dimension_numbers=('NWC', 'WIO', 'NWC'),
                                    feature_group_count=x.shape[-1])

def _gmlp_spatial_gate(u, v, ln_g, ln_b, ws, bs):
    B, S, _ = v.shape
    nc = S // GMLP_CHUNK
    v = _layernorm(v, ln_g, ln_b).reshape(B, nc, GMLP_CHUNK, GMLP_GROUPS, MIX_W // GMLP_GROUPS)
    mask = np.tril(np.ones((GMLP_CHUNK, GMLP_CHUNK), dtype=bool))
    wsm = jnp.where(mask, ws, 0).astype(v.dtype)
    mixed = jnp.einsum('gts,bnsgc->bntgc', wsm, v) + bs.T[None, None, :, :, None].astype(v.dtype)
    return u * mixed.reshape(B, S, MIX_W)

def _overlap_matrix(n_cmp, n_sel):
    cs = np.arange(n_cmp) * CMP_STRIDE
    ce = cs + CMP_LEN
    ss = np.arange(n_sel) * SEL_BLOCK
    se = ss + SEL_BLOCK
    return ((cs[:, None] < se[None, :]) & (ce[:, None] > ss[None, :])).astype(np.float32)

def _nsa(q, kc, vc, ks, vs, kw, vw, gate_logits, q_g, k_g, cmp_pe, cmp_w1, cmp_w2):
    B, S, _ = q.shape
    T = Q_BLOCK
    nqb = S // T
    pos = jnp.arange(S)
    scale = HEAD_DIM ** -0.5
    heads = lambda t: t.reshape(B, S, N_KV_HEADS, HEAD_DIM)
    q = _rms(q.reshape(B, S, N_KV_HEADS, Q_PER_KV, HEAD_DIM), q_g)

    n_cmp = (S - CMP_LEN) // CMP_STRIDE + 1
    cmp_idx = np.arange(n_cmp)[:, None] * CMP_STRIDE + np.arange(CMP_LEN)[None, :]

    def compress(t, pe, w1, w2):
        blk = jnp.take(heads(t), cmp_idx, axis=1) + pe[None, None, :, None, :]
        blk = jnp.swapaxes(blk, 2, 3).reshape(B, n_cmp, N_KV_HEADS, CMP_LEN * HEAD_DIM)
        hid = jax.nn.gelu(jnp.einsum('bnhf,fe->bnhe', blk, w1))
        return jnp.einsum('bnhe,ed->bnhd', hid, w2)

    k_cmp = _rms(compress(kc, cmp_pe[0], cmp_w1[0], cmp_w2[0]), k_g[0])
    v_cmp = compress(vc, cmp_pe[1], cmp_w1[1], cmp_w2[1])
    cmp_valid = cmp_idx[:, -1][None, :] <= np.arange(S)[:, None]
    s = jnp.einsum('bshgd,bnhd->bhgsn', q, k_cmp).astype(jnp.float32) * scale
    p_cmp = jnp.where(cmp_valid, jax.nn.softmax(jnp.where(cmp_valid, s, NEG_INF), axis=-1), 0.0)
    o_cmp = jnp.einsum('bhgsn,bnhd->bshgd', p_cmp.astype(v_cmp.dtype), v_cmp)

    n_sel = S // SEL_BLOCK
    k_top = min(SEL_TOPK, n_sel)
    p_slc = jnp.einsum('bhgsn,nj->bhsj', p_cmp, jnp.asarray(_overlap_matrix(n_cmp, n_sel)))
    blk = np.arange(n_sel)[None, :]
    cur = (np.arange(S) // SEL_BLOCK)[:, None]
    forced = (blk == 0) | ((cur - blk >= 0) & (cur - blk < N_LOCAL_BLOCKS))
    causal = blk <= cur
    score = jnp.where(forced, jnp.inf, jnp.where(causal, p_slc, -jnp.inf))
    sel_idx = lax.top_k(score, k_top)[1]

    ks_h = jnp.swapaxes(_rms(heads(ks), k_g[1]), 1, 2)
    vs_h = jnp.swapaxes(heads(vs), 1, 2)
    gather = jax.vmap(jax.vmap(lambda a, i: a[i]))
    tok_off = jnp.arange(SEL_BLOCK)

    def sel_block(args):
        qb, ib, pb = args
        tok = (ib[..., None] * SEL_BLOCK + tok_off).reshape(B, N_KV_HEADS, T, k_top * SEL_BLOCK)
        flat = tok.reshape(B, N_KV_HEADS, -1)
        kg = gather(ks_h, flat).reshape(B, N_KV_HEADS, T, k_top * SEL_BLOCK, HEAD_DIM)
        vg = gather(vs_h, flat).reshape(B, N_KV_HEADS, T, k_top * SEL_BLOCK, HEAD_DIM)
        sb = jnp.einsum('bthgd,bhtkd->bhgtk', qb, kg).astype(jnp.float32) * scale
        m = (tok <= pb[:, None])[:, :, None]
        pr = jax.nn.softmax(jnp.where(m, sb, NEG_INF), axis=-1).astype(vg.dtype)
        return jnp.einsum('bhgtk,bhtkd->bthgd', pr, vg)

    q_blocks = jnp.moveaxis(q.reshape(B, nqb, T, N_KV_HEADS, Q_PER_KV, HEAD_DIM), 1, 0)
    i_blocks = jnp.moveaxis(sel_idx.reshape(B, N_KV_HEADS, nqb, T, k_top), 2, 0)
    p_blocks = pos.reshape(nqb, T)
    o_sel = jnp.moveaxis(lax.map(sel_block, (q_blocks, i_blocks, p_blocks)), 0, 1)
    o_sel = o_sel.reshape(B, S, N_KV_HEADS, Q_PER_KV, HEAD_DIM)

    kw_h = _rms(heads(kw), k_g[2])
    vw_h = heads(vw)
    win_idx = np.arange(nqb)[:, None] * T + np.arange(WINDOW + T)[None, :]
    kpos = (win_idx - WINDOW)[:, None, :]
    qpos = np.arange(S).reshape(nqb, T)[:, :, None]
    wmask = (kpos <= qpos) & (kpos > qpos - WINDOW) & (kpos >= 0)
    pad = ((0, 0), (WINDOW, 0), (0, 0), (0, 0))
    kb = jnp.take(jnp.pad(kw_h, pad), win_idx, axis=1)
    vb = jnp.take(jnp.pad(vw_h, pad), win_idx, axis=1)
    qb = q.reshape(B, nqb, T, N_KV_HEADS, Q_PER_KV, HEAD_DIM)
    sw = jnp.einsum('bnthgd,bnmhd->bnhgtm', qb, kb).astype(jnp.float32) * scale
    pw = jax.nn.softmax(jnp.where(wmask[:, None, None], sw, NEG_INF), axis=-1).astype(vb.dtype)
    o_win = jnp.einsum('bnhgtm,bnmhd->bnthgd', pw, vb).reshape(B, S, N_KV_HEADS, Q_PER_KV, HEAD_DIM)

    g = jax.nn.sigmoid(gate_logits.reshape(B, S, N_KV_HEADS, Q_PER_KV, 3))
    o = g[..., 0:1] * o_cmp + g[..., 1:2] * o_sel + g[..., 2:3] * o_win
    return o.reshape(B, S, MIX_W)

def second_inputs(seed: int = 0) -> dict:
    key = jax.random.key(seed)
    ks = jax.random.split(key, 26)
    L = DEPTH_2
    nrm = lambda k, shape, sc: jax.random.normal(k, shape, jnp.float32) * sc
    res_sc = (2.0 * DEPTH_2) ** -0.5
    return {
        "x": nrm(ks[0], (BATCH, SEQ, D_MODEL), 1.0),
        "norm1_g": 1.0 + nrm(ks[1], (L, D_MODEL), 0.02),
        "w_in": nrm(ks[2], (L, D_MODEL, IN_COLS_2), D_MODEL ** -0.5),
        "gmlp_ln_g": 1.0 + nrm(ks[3], (L, MIX_W), 0.02),
        "gmlp_ln_b": nrm(ks[4], (L, MIX_W), 0.02),
        "gmlp_ws": nrm(ks[5], (L, GMLP_GROUPS, GMLP_CHUNK, GMLP_CHUNK), GMLP_CHUNK ** -0.5),
        "gmlp_bs": 1.0 + nrm(ks[6], (L, GMLP_GROUPS, GMLP_CHUNK), 0.02),
        "nsa_q_norm_g": 1.0 + nrm(ks[7], (L, HEAD_DIM), 0.02),
        "nsa_k_norm_g": 1.0 + nrm(ks[8], (L, 3, HEAD_DIM), 0.02),
        "nsa_cmp_pe": nrm(ks[9], (L, 2, CMP_LEN, HEAD_DIM), 0.02),
        "nsa_cmp_w1": nrm(ks[10], (L, 2, CMP_LEN * HEAD_DIM, CMP_HIDDEN), (CMP_LEN * HEAD_DIM) ** -0.5),
        "nsa_cmp_w2": nrm(ks[11], (L, 2, CMP_HIDDEN, HEAD_DIM), CMP_HIDDEN ** -0.5),
        "conf_conv_w": nrm(ks[12], (L, CONF_KERNEL, MIX_W), CONF_KERNEL ** -0.5),
        "conf_conv_b": nrm(ks[13], (L, MIX_W), 0.02),
        "conf_ln_g": 1.0 + nrm(ks[14], (L, MIX_W), 0.02),
        "conf_ln_b": nrm(ks[15], (L, MIX_W), 0.02),
        "sconv_w": nrm(ks[16], (L, SCONV_KERNEL, MIX_W), SCONV_KERNEL ** -0.5),
        "w_branch": nrm(ks[17], (L, N_MIXERS, MIX_W, D_MODEL), MIX_W ** -0.5),
        "w_gate": nrm(ks[18], (L, D_MODEL, N_MIXERS * D_MODEL), D_MODEL ** -0.5),
        "b_gate": nrm(ks[19], (L, N_MIXERS * D_MODEL), 0.02),
        "w_out": nrm(ks[20], (L, D_MODEL, D_MODEL), D_MODEL ** -0.5 * res_sc),
        "norm2_g": 1.0 + nrm(ks[21], (L, D_MODEL), 0.02),
        "w_mlp1": nrm(ks[22], (L, D_MODEL, D_FF_2), D_MODEL ** -0.5),
        "w_mlp2": nrm(ks[23], (L, D_FF_2, D_MODEL), D_FF_2 ** -0.5 * res_sc),
    }

def second_block(x, norm1_g, w_in, gmlp_ln_g, gmlp_ln_b, gmlp_ws, gmlp_bs, nsa_q_norm_g, nsa_k_norm_g,
              nsa_cmp_pe, nsa_cmp_w1, nsa_cmp_w2, conf_conv_w, conf_conv_b, conf_ln_g, conf_ln_b,
              sconv_w, w_branch, w_gate, b_gate, w_out, norm2_g, w_mlp1, w_mlp2):
    B, S, D = x.shape
    split_points = np.cumsum(IN_WIDTHS)[:-1].tolist()
    for l in range(DEPTH_2):
        xn = _rms(x, norm1_g[l])
        (gu, gv, q, kc, vc, ks_, vs_, kw, vw, ng, ca, cb, sB, sC, sh) = jnp.split(
            jnp.einsum('bsd,de->bse', xn, w_in[l]), split_points, axis=-1)
        y_a = _gmlp_spatial_gate(jax.nn.gelu(gu), jax.nn.gelu(gv), gmlp_ln_g[l], gmlp_ln_b[l], gmlp_ws[l], gmlp_bs[l])
        y_b = _nsa(q, kc, vc, ks_, vs_, kw, vw, ng, nsa_q_norm_g[l], nsa_k_norm_g[l],
                   nsa_cmp_pe[l], nsa_cmp_w1[l], nsa_cmp_w2[l])
        z = ca * jax.nn.sigmoid(cb)
        z = _causal_depthwise_conv(z, conf_conv_w[l]) + conf_conv_b[l]
        y_c = jax.nn.silu(_layernorm(z, conf_ln_g[l], conf_ln_b[l]))
        y_d = sB * _causal_depthwise_conv(sC * sh, sconv_w[l])
        ys = jnp.stack([y_a, y_b, y_c, y_d], axis=2)
        proj = jnp.einsum('bsnc,ncd->bsnd', ys, w_branch[l])
        gates = jax.nn.sigmoid(jnp.einsum('bsd,de->bse', xn, w_gate[l]) + b_gate[l]).reshape(B, S, N_MIXERS, D)
        mixed = jnp.sum(gates * proj, axis=2)
        x = x + jnp.einsum('bsd,de->bse', mixed, w_out[l])
        hn = _rms(x, norm2_g[l])
        hid = jnp.square(jax.nn.relu(jnp.einsum('bsd,df->bsf', hn, w_mlp1[l])))
        x = x + jnp.einsum('bsf,fd->bsd', hid, w_mlp2[l])
    return x


_first_inputs = second_inputs


def second_inputs(seed=0):
    import zlib

    import numpy as np

    out = dict(_first_inputs(seed))
    spreads = {}
    factors = {'norm1_g': 3.39,
     'gmlp_ln_g': 200.0,
     'gmlp_ln_b': 200.0,
     'gmlp_bs': 172.139,
     'nsa_q_norm_g': 200.0,
     'nsa_k_norm_g': 200.0,
     'nsa_cmp_pe': 200.0,
     'conf_conv_b': 39.482,
     'conf_ln_g': 200.0,
     'conf_ln_b': 200.0,
     'b_gate': 8.0,
     'norm2_g': 16.994,
     'nsa_cmp_w1': 5.939,
     'nsa_cmp_w2': 5.422}
    for name, (base, spread) in spreads.items():
        noise = np.random.default_rng([zlib.crc32(name.encode()), seed]).standard_normal(out[name].shape)
        drawn = base * np.exp(spread * noise) if base else spread * noise
        out[name] = __import__('jax').numpy.asarray(drawn.astype(out[name].dtype))
    for name, factor in factors.items():
        out[name] = (out[name] * factor).astype(out[name].dtype)
    return out


_narrow_inputs = second_inputs


def second_inputs(seed=0):

    out = dict(_narrow_inputs(seed))
    wider = {'gmlp_ln_g': 5.26,
     'gmlp_ln_b': 5.43,
     'gmlp_bs': 3.84,
     'nsa_q_norm_g': 4.58,
     'nsa_k_norm_g': 4.35,
     'conf_ln_g': 11.66,
     'conf_ln_b': 11.64,
     'norm2_g': 3.73}
    for name, times in wider.items():
        mean = out[name].mean()
        out[name] = (mean + times * (out[name] - mean)).astype(out[name].dtype)
    return out


def setup_inputs(seed=0):
    out = dict(first_inputs(seed))
    for name, value in second_inputs(seed + 1).items():
        if name != "x":
            out[name + "_2"] = value
    return out


def reference(
    x, mix_norm, w_in, dn_conv, dn_a_log, dn_dt_bias, dn_norm, hg_lb_logits, hg_norm,
    w_branch_dn, w_branch_hg, w_out, ffn_norm, w_up, ffn_conv, ffn_conv_bias, w_down,
    final_norm, norm1_g_2, w_in_2, gmlp_ln_g_2, gmlp_ln_b_2, gmlp_ws_2, gmlp_bs_2,
    nsa_q_norm_g_2, nsa_k_norm_g_2, nsa_cmp_pe_2, nsa_cmp_w1_2, nsa_cmp_w2_2, conf_conv_w_2,
    conf_conv_b_2, conf_ln_g_2, conf_ln_b_2, sconv_w_2, w_branch_2, w_gate_2, b_gate_2, w_out_2,
    norm2_g_2, w_mlp1_2, w_mlp2_2,
):
    x = first_block(
        x, mix_norm, w_in, dn_conv, dn_a_log, dn_dt_bias, dn_norm, hg_lb_logits, hg_norm,
        w_branch_dn, w_branch_hg, w_out, ffn_norm, w_up, ffn_conv, ffn_conv_bias, w_down,
        final_norm,
    )
    return second_block(
        x, norm1_g_2, w_in_2, gmlp_ln_g_2, gmlp_ln_b_2, gmlp_ws_2, gmlp_bs_2, nsa_q_norm_g_2,
        nsa_k_norm_g_2, nsa_cmp_pe_2, nsa_cmp_w1_2, nsa_cmp_w2_2, conf_conv_w_2, conf_conv_b_2,
        conf_ln_g_2, conf_ln_b_2, sconv_w_2, w_branch_2, w_gate_2, b_gate_2, w_out_2, norm2_g_2,
        w_mlp1_2, w_mlp2_2,
    )


_drawn_inputs = setup_inputs


def setup_inputs(seed=0):
    import zlib

    import numpy as np

    out = dict(_drawn_inputs(seed))
    spreads = {}
    factors = {'dn_norm': 2.882, 'hg_norm': 3.344, 'ffn_conv_bias': 3.022}
    for name, (base, spread) in spreads.items():
        noise = np.random.default_rng([zlib.crc32(name.encode()), seed]).standard_normal(out[name].shape)
        drawn = base * np.exp(spread * noise) if base else spread * noise
        out[name] = __import__('jax').numpy.asarray(drawn.astype(out[name].dtype))
    for name, factor in factors.items():
        out[name] = (out[name] * factor).astype(out[name].dtype)
    return out
```

```python
from contextlib import ExitStack, contextmanager

import numpy as np
import concourse.bass as bass
from concourse import mybir

P = 128
F32 = mybir.dt.float32
I32 = mybir.dt.int32
ALU = mybir.AluOpType
ACT = mybir.ActivationFunctionType
AX = mybir.AxisListType.X
ds = bass.ds
LEVELS = 7
UNIT = 256

IDENT, ONES, INCL, AFTER, REACH, PAIR = 0, 1, 2, 4, 6, 6 + 2 * LEVELS
BLOCK64, CAUSAL, CMP_ADD, CMP_OK, N_CONST = 6 + 4 * LEVELS, 7 + 4 * LEVELS, 8 + 4 * LEVELS, 9 + 4 * LEVELS, 10 + 4 * LEVELS


def constant_table(n_cmp, cmp_len, cmp_stride):
    r = np.arange(P)
    s, t = r[:, None], r[None, :]
    c = np.zeros((P, N_CONST, P), np.float32)
    c[:, IDENT] = s == t
    c[:, ONES] = 1
    for lane in (0, 1):
        a, b = (s, t) if lane == 0 else (P - 1 - s, P - 1 - t)
        c[:, INCL + lane] = a <= b
        c[:, AFTER + lane] = a > b
        for n in range(LEVELS):
            half = 1 << n
            same = a // (2 * half) == b // (2 * half)
            second_a, second_b = a // half % 2 == 1, b // half % 2 == 1
            c[:, REACH + lane * LEVELS + n] = same & np.where(second_b, second_a & (a <= b), ~second_a & (a > b))
            c[:, PAIR + lane * LEVELS + n] = same & ~second_a & second_b
    c[:, BLOCK64] = s // 64 == t // 64
    c[:, CAUSAL] = np.where(t <= s, 0.0, -1e30)
    for chunk in range(4):
        for n in range(n_cmp):
            ok = n * cmp_stride + cmp_len - 1 <= chunk * P + r
            c[:, CMP_OK, chunk * 32 + n] = ok
            c[:, CMP_ADD, chunk * 32 + n] = np.where(ok, 0.0, -1e30)
    return c


class Steps:

    def __init__(self, sem, names):
        self.sem, self.per = sem, len(names)
        self.place = {n: k + 1 for k, n in enumerate(names)}
        self.names, self.given = list(names), 0

    def open(self, e):
        e.sem_inc(self.sem, self.per)

    def done(self, instruction, name):
        assert self.names[self.given % self.per] == name, (name, self.names[self.given % self.per])
        self.given += 1
        return instruction.then_inc(self.sem, 1)

    def wait(self, e, turn, name):
        e.wait_ge(self.sem, turn * self.per + self.per + self.place[name])

    def wait_before(self, e, turn, name):
        e.wait_ge(self.sem, turn * self.per + self.place[name])


@contextmanager
def stage(nc, *names):
    with ExitStack() as ctx:
        sems = [ctx.enter_context(nc.semaphore(n)) for n in names]
        yield sems
        for s in sems:
            nc.gpsimd.sem_clear(s)
        nc.all_engine_barrier()


def pass_waits(e, passed):
    e.sem_inc(passed, 1)


def wide(ap, n):
    return ap.unsqueeze(2).broadcast_to((ap.shape[0], ap.shape[1], n))


def heads(ap, n):
    return ap.unsqueeze(1).broadcast_to((ap.shape[0], n, ap.shape[1]))


def contract(e, out, pairs):
    for n, (lhsT, rhs) in enumerate(pairs):
        last = e.matmul(out, lhsT, rhs, start=n == 0, stop=n == len(pairs) - 1)
    return last


def load_norm_stage(nc, PS, C, x, X, H):
    S = X.shape[2]
    D = x.shape[1]
    T, K = S // P, D // P
    with stage(nc, "x_in", "turned", "x_kept") as (x_in, turned_s, kept_s):
        turned = Steps(turned_s, [f"tile{k}" for k in range(K)])
        kept = Steps(kept_s, [f"tile{k}" for k in range(K)])
        rows = H[:, :, :].rearrange("p k n -> p (k n)").rearrange("p (c f) -> p c f", c=T)
        with nc.Block() as block:

            @block.sync
            def _(sp):
                sp.dma_start(rows, x.rearrange("(c p) f -> p c f", p=P)).then_inc(x_in, 16)

            @block.tensor
            def _(pe):
                pe.wait_ge(x_in, 16)
                for k in range(K):
                    for c in range(T):
                        last = pe.transpose(PS[:, k, c * P:(c + 1) * P], rows[:, c, k * P:(k + 1) * P], C[:, IDENT, :])
                    turned.done(last, f"tile{k}")

            @block.vector
            def _(dve):
                for k in range(K):
                    dve.wait_ge(turned.sem, k + 1)
                    kept.done(dve.tensor_copy(X[:, k, :], PS[:, k, :]), f"tile{k}")


def rms_stage(nc, PS, C, X, out, weight, scratch, RS, eps):
    K = X.shape[1]
    with stage(nc, "squares", "sums", "vector_steps", "root") as (sq_s, sum_s, dve_s, root_s):
        with nc.Block() as block:

            @block.scalar
            def _(act):
                for k in range(K):
                    act.activation(scratch[:, k, :], X[:, k, :], ACT.Square).then_inc(sq_s, 1)
                act.wait_ge(dve_s, 2)
                act.activation(RS[:, :], RS[:, :], ACT.Sqrt).then_inc(root_s, 1)

            @block.tensor
            def _(pe):
                for k in range(K):
                    pe.wait_ge(sq_s, k + 1)
                    last = pe.matmul(PS[:, 0, :], C[:, ONES, :], scratch[:, k, :], start=k == 0, stop=k == K - 1)
                last.then_inc(sum_s, 1)

            @block.vector
            def _(dve):
                dve.wait_ge(sum_s, 1)
                dve.tensor_scalar(RS[:, :], PS[:, 0, :], 1.0 / (K * P), eps, ALU.mult, ALU.add).then_inc(dve_s, 1)
                dve.wait_ge(dve_s, 1)
                dve.reciprocal(RS[:, :], RS[:, :]).then_inc(dve_s, 1)
                dve.wait_ge(root_s, 1)
                for k in range(K):
                    dve.scalar_tensor_tensor(out[:, k, :], X[:, k, :], weight[:, k:k + 1], RS[:, :], ALU.mult, ALU.mult).then_inc(dve_s, 1)


def k_tiles(w):
    return w.rearrange("(k p) n -> p k n", p=P)


def slab_stage(nc, PS, w, source, X, slab_buf):
    K = source.shape[1]
    rows = w.rearrange("(k p) n -> k p n", p=P)
    N = 4
    groups = K // N
    tail = K - groups * N
    with stage(nc, *[f"slab{n}_in" for n in range(N)], "slabs_used", "added") as sems:
        slab_in, used_s, added = sems[:N], sems[N], sems[N + 1]
        used = Steps(used_s, [f"slab{n}" for n in range(N)])
        with nc.Block() as block:

            def load(sp, g, n):
                used.wait_before(sp, g, f"slab{n}")
                k = g * N + n
                src = rows[k] if isinstance(k, int) else rows[ds(k, 1)].rearrange("k p n -> (k p) n")
                sp.dma_start(slab_buf[:, n, :], src).then_inc(slab_in[n], 16)

            @block.sync
            def _(sp):
                with sp.Fori(0, groups) as g:
                    for n in range(N):
                        load(sp, g, n)
                for n in range(tail):
                    load(sp, groups, n)

            @block.tensor
            def _(pe):
                used.open(pe)

                def use(g, n, first, final):
                    pe.wait_ge(slab_in[n], 16 * (g + 1))
                    k = g * N + n
                    src = source[:, k, :] if isinstance(k, int) else source[:, ds(k, 1), :].rearrange("p a n -> p (a n)")
                    for m in range(X.shape[1]):
                        last = pe.matmul(PS[:, m, :], slab_buf[:, n, m * P:(m + 1) * P], src, start=first, stop=final)
                    used.done(last, f"slab{n}")

                for n in range(N):
                    use(0, n, n == 0, False)
                if groups - (not tail) > 1:
                    with pe.Fori(1, groups - (not tail)) as g:
                        for n in range(N):
                            use(g, n, False, False)
                left = groups if tail else groups - 1
                for n in range(tail or N):
                    use(left, n, False, n == (tail or N) - 1)

            @block.vector
            def _(dve):
                dve.wait_ge(used.sem, used.per + K)
                for m in range(X.shape[1]):
                    dve.tensor_tensor(X[:, m, :], X[:, m, :], PS[:, m, :], ALU.add).then_inc(added, 1)


def tile(buf, k):
    return buf[:, k, :] if isinstance(k, int) else buf[:, ds(k, 1), :].rearrange("p a n -> p (a n)")


def qkv_stage(nc, PS, C, A, l, w_in, H, QKV, CONV, Z, WBA, BA, W, PAR):
    T = 4
    names = [f"tile{j}" for j in range(4)]
    with stage(nc, "w0_in", "w1_in", "wba_in", "projected", "vector_steps", "silu_done", "ba_done", "ba_kept") as (
            w0, w1, wba_in, proj_s, dve_s, silu_s, ba_done, ba_kept):
        w_loaded = (w0, w1)
        proj = Steps(proj_s, names)
        dve_st = Steps(dve_s, [f"{a}{j}" for j in range(4) for a in ("kept", "tap0_", "tap1_", "tap2_", "tap3_", "tap4_")])
        silu = Steps(silu_s, names)
        wl = w_in[ds(l, 1)].rearrange("l (k p) n -> p (l k) n", p=P)
        with nc.Block() as block:

            @block.sync
            def _(sp):
                def load(g, s):
                    proj.wait_before(sp, g, f"tile{2 * s + 1}")
                    sp.dma_start(W[:, s], wl[:, :, ds(g * 2 * UNIT + s * UNIT, UNIT)]).then_inc(w_loaded[s], 16)

                with sp.Fori(0, 4) as g:
                    for s in range(2):
                        load(g, s)
                sp.dma_start(WBA[:, :, :], wl[:, :, ds(4 * 512, 16)]).then_inc(wba_in, 16)

            @block.tensor
            def _(pe):
                proj.open(pe)

                def group(g, free):
                    for j in range(4):
                        s, m = divmod(j, 2)
                        if m == 0:
                            pe.wait_ge(w_loaded[s], 16 * (g + 1))
                        free(g, j)
                        last = contract(pe, PS[:, j, :], [(W[:, s, k, m * P:(m + 1) * P], H[:, k, :]) for k in range(8)])
                        proj.done(last, f"tile{j}")

                with pe.Fori(0, 3) as g:
                    group(g, lambda g, j: dve_st.wait_before(pe, g, f"kept{j}"))
                group(3, lambda g, j: dve_st.wait_before(pe, g, f"kept{j}"))
                pe.wait_ge(wba_in, 16)
                for c in range(T):
                    last = contract(pe, PS[:, 4, c * 16:(c + 1) * 16],
                                    [(H[:, k, c * P:(c + 1) * P], WBA[:, k, :]) for k in range(8)])
                last.then_inc(ba_done, 1)

            @block.vector
            def _(dve):
                dve_st.open(dve)
                dve.memset(QKV[:, :, 0:2], 0.0)
                dve.memset(QKV[:, :, 514:516], 0.0)
                with dve.Fori(0, 3) as g:
                    for j in range(4):
                        t = g * 4 + j
                        proj.wait(dve, g, f"tile{j}")
                        row = QKV[:, ds(t, 1), :].rearrange("p a n -> p (a n)")
                        dve_st.done(dve.tensor_copy(QKV[:, ds(t, 1), 2:514].rearrange("p a n -> p (a n)"), PS[:, j, :]), f"kept{j}")
                        dve_st.wait(dve, g, f"kept{j}")
                        if j >= 2:
                            silu.wait(dve, g, f"tile{j - 2}")
                        else:
                            silu.wait_before(dve, g, f"tile{j + 2}")
                        acc = CONV[:, j % 2, :]
                        for tap in range(5):
                            x_tap = QKV[:, ds(t, 1), tap:tap + 512].rearrange("p a n -> p (a n)")
                            w_tap = PAR[:, ds(t + tap * 12, 1)]
                            if tap == 0:
                                ins = dve.tensor_scalar(acc, x_tap, w_tap, None, ALU.mult)
                            else:
                                dve_st.wait(dve, g, f"tap{tap - 1}_{j}")
                                ins = dve.scalar_tensor_tensor(acc, x_tap, w_tap, acc, ALU.mult, ALU.add)
                            dve_st.done(ins, f"tap{tap}_{j}")
                dve.wait_ge(ba_done, 1)
                dve.tensor_copy(BA[:, :, :].rearrange("p c n -> p (c n)"), PS[:, 4, 0:64]).then_inc(ba_kept, 1)

            @block.scalar
            def _(act):
                silu.open(act)
                with act.Fori(0, 3) as g:
                    for j in range(4):
                        dve_st.wait(act, g, f"tap4_{j}")
                        silu.done(act.activation(QKV[:, ds(g * 4 + j, 1), 2:514].rearrange("p a n -> p (a n)"), CONV[:, j % 2, :], ACT.Silu), f"tile{j}")
                for j in range(4):
                    proj.wait(act, 3, f"tile{j}")
                    silu.done(act.activation(Z[:, j, :], PS[:, j, :], ACT.Silu), f"tile{j}")


def delta_prep_stage(nc, PS, C, l, QKV, BA, SMALL, KTOK, VTOK, SQ, RS, KS, VS, BETA, G, TMP):
    with stage(nc, "squares", "sums", "vector_steps", "scalar_steps", "staged", "turned", "gate_steps", "waits_passed") as (
            sq_s, sum_s, dve_s, act_s, pool_s, turn_s, gate_s, passed):
        sums = Steps(sum_s, ["q", "k"])
        dve_st = Steps(dve_s, ["mean_q", "inv_q", "mean_k", "inv_k", "q", "k"])
        act_st = Steps(act_s, ["sq_q", "sq_k", "root_q", "root_k", "k_back", "k_tok", "v_tok"])
        pool_st = Steps(pool_s, ["v"])
        turned = Steps(turn_s, ["k", "v"])
        gate = Steps(gate_s, ["eb", "ea", "eb1", "beta", "a", "nabs", "exp", "relu", "ln", "sum", "g"])

        def body(h):
            return (QKV[:, ds(h, 1), 2:514].rearrange("p a n -> p (a n)"), QKV[:, ds(h + 4, 1), 2:514].rearrange("p a n -> p (a n)"))

        with nc.Block() as block:

            @block.scalar
            def _(act):
                act_st.open(act)
                with act.Fori(0, 4) as h:
                    for n, (name, src) in enumerate(zip("qk", body(h))):
                        sums.wait_before(act, h, name)
                        act_st.done(act.activation(SQ[:, n, :], src, ACT.Square), f"sq_{name}")
                    for n, name in enumerate("qk"):
                        dve_st.wait(act, h, f"inv_{name}")
                        act_st.done(act.activation(RS[:, n, :], RS[:, n, :], ACT.Sqrt), f"root_{name}")
                    dve_st.wait(act, h, "k")
                    pass_waits(act, passed)
                    act_st.done(act.copy(body(h)[1], KS[:, :]), "k_back")
                    turned.wait(act, h, "k")
                    act_st.done(act.copy(KTOK[:, :, ds(h * P, P)], PS[:, 2, :].rearrange("p (c d) -> p c d", d=P)), "k_tok")
                    turned.wait(act, h, "v")
                    pass_waits(act, passed)
                    act_st.done(act.copy(VTOK[:, :, ds(h * P, P)], PS[:, 3, :].rearrange("p (c d) -> p c d", d=P)), "v_tok")
                a_log, dt = SMALL[:, 0:8], SMALL[:, 8:16]
                gate.done(act.activation(BETA[:, :, :], BA[:, :, 0:8], ACT.Exp, scale=-1.0), "eb")
                gate.done(act.activation(TMP[:, 0, 0:8], a_log, ACT.Exp), "ea")
                act.wait_ge(gate.sem, gate.place["nabs"])
                act.activation(G[:, :, :], TMP[:, 2, :].rearrange("p (c n) -> p c n", n=8), ACT.Exp).then_inc(gate.sem, 1)
                act.wait_ge(gate.sem, gate.place["relu"])
                act.activation(G[:, :, :], G[:, :, :], ACT.Ln, bias=1.0).then_inc(gate.sem, 1)

            @block.gpsimd
            def _(pool):
                pool_st.open(pool)
                with pool.Fori(0, 4) as h:
                    turned.wait_before(pool, h, "v")
                    pool_st.done(pool.tensor_copy(VS[:, :], QKV[:, ds(h + 8, 1), 2:514].rearrange("p a n -> p (a n)")), "v")

            @block.tensor
            def _(pe):
                sums.open(pe)
                turned.open(pe)
                with pe.Fori(0, 4) as h:
                    for n, name in enumerate("qk"):
                        act_st.wait(pe, h, f"sq_{name}")
                        dve_st.wait_before(pe, h, f"mean_{name}")
                        sums.done(pe.matmul(PS[:, n, :], C[:, ONES, :], SQ[:, n, :], start=True, stop=True), name)
                    for n, name in enumerate("kv"):
                        if name == "k":
                            dve_st.wait(pe, h, "k")
                        else:
                            pool_st.wait(pe, h, "v")
                        act_st.wait_before(pe, h, f"{name}_tok")
                        src = KS if name == "k" else VS
                        for c in range(4):
                            last = pe.transpose(PS[:, 2 + n, c * P:(c + 1) * P], src[:, c * P:(c + 1) * P], C[:, IDENT, :])
                        turned.done(last, name)

            @block.vector
            def _(dve):
                dve_st.open(dve)
                with dve.Fori(0, 4) as h:
                    for n, name in enumerate("qk"):
                        sums.wait(dve, h, name)
                        dve_st.done(dve.tensor_scalar(RS[:, n, :], PS[:, n, :], 1e-6, None, ALU.add), f"mean_{name}")
                        dve_st.wait(dve, h, f"mean_{name}")
                        dve_st.done(dve.reciprocal(RS[:, n, :], RS[:, n, :]), f"inv_{name}")
                    q, k = body(h)
                    act_st.wait(dve, h, "root_q")
                    dve_st.done(dve.scalar_tensor_tensor(q, q, P ** -0.5, RS[:, 0, :], ALU.mult, ALU.mult), "q")
                    act_st.wait(dve, h, "root_k")
                    turned.wait_before(dve, h, "k")
                    act_st.wait_before(dve, h, "k_back")
                    dve_st.done(dve.tensor_tensor(KS[:, :], k, RS[:, 1, :], ALU.mult), "k")
                a = TMP[:, 1, :]
                dve.wait_ge(gate.sem, gate.place["ea"])
                dve.tensor_scalar(BETA[:, :, :], BETA[:, :, :], 1.0, None, ALU.add).then_inc(gate.sem, 1)
                dve.wait_ge(gate.sem, gate.place["eb1"])
                dve.reciprocal(BETA[:, :, :], BETA[:, :, :]).then_inc(gate.sem, 1)
                dve.tensor_tensor(a.rearrange("p (c n) -> p c n", n=8), BA[:, :, 8:16], heads(SMALL[:, 8:16], 4), ALU.add).then_inc(gate.sem, 1)
                dve.wait_ge(gate.sem, gate.place["a"])
                dve.scalar_tensor_tensor(TMP[:, 2, :], a, -1.0, a, ALU.mult, ALU.min).then_inc(gate.sem, 1)
                dve.wait_ge(gate.sem, gate.place["exp"])
                dve.tensor_scalar(a, a, 0.0, None, ALU.max).then_inc(gate.sem, 1)
                dve.wait_ge(gate.sem, gate.place["ln"])
                dve.tensor_tensor(a.rearrange("p (c n) -> p c n", n=8), a.rearrange("p (c n) -> p c n", n=8), G[:, :, :], ALU.add).then_inc(gate.sem, 1)
                dve.wait_ge(gate.sem, gate.place["sum"])
                dve.scalar_tensor_tensor(G[:, :, :], a.rearrange("p (c n) -> p c n", n=8), -1.0, heads(TMP[:, 0, 0:8], 4), ALU.mult, ALU.mult).then_inc(gate.sem, 1)


def per_head(bank):
    return bank.rearrange("p (h n) -> p h n", h=4)


def delta_stage(nc, PS, C, QKV, KTOK, VTOK, BETA, G, O2, new):
    lanes = (0, 1)
    B = [{n: new(f"{n}{d}", [P, 4, P]) for n in
          ("GB", "BB", "KT", "EG", "DM", "AT", "LB", "T", "TT", "PP", "QK", "VB", "KBG", "KD", "WT", "VN", "QG", "ST")} for d in lanes]
    for d in lanes:
        B[d].update({n: new(f"{n}{d}", [P, 4]) for n in ("GCS", "EGS", "LD", "BE")})
    last_col = (P - 1, 0)
    pool_names = ["gb", "bb", "kt", "vb", "kd", "kbg"]
    pe_names = ["gc", "bg", "qk"] + [f"{a}{n}" for n in range(LEVELS) for a in "pd"] + ["wt", "vn", "o", "st"]
    act_names = ["eg", "dm", "egs", "ld"] + [f"p{n}" for n in range(LEVELS)] + ["wt", "o"]
    dve_names = (["gcs"] + [f"dif{h}" for h in range(4)] + ["be", "ldif", "mask", "at", "atb", "qk", "t", "tt", "qg"]
                 + [f"{a}{n}" for n in range(LEVELS) for a in ("lb", "t", "tt")][:-3] + [f"lb{LEVELS - 1}", f"tt{LEVELS - 1}", "vn"]
                 + [f"st{h}" for h in range(4)])
    with stage(nc, *[f"{e}{d}" for d in lanes for e in ("delta_pe", "delta_act", "delta_dve", "delta_pool")], "waits_passed") as sems:
        pe_st = [Steps(sems[4 * d], pe_names) for d in lanes]
        act_st = [Steps(sems[4 * d + 1], act_names) for d in lanes]
        dve_st = [Steps(sems[4 * d + 2], dve_names) for d in lanes]
        pool_st = [Steps(sems[4 * d + 3], pool_names) for d in lanes]

        def chunk(i, d):
            return i if d == 0 else i * -1 + 3

        def bank(d, n):
            return PS[:, 4 * d + n, :]

        with nc.Block() as block:

            @block.gpsimd
            def _(pool):
                for d in lanes:
                    pool_st[d].open(pool)
                with pool.Fori(0, 4) as i:
                    for d in lanes:
                        b, c, st = B[d], chunk(i, d), pool_st[d]
                        pe_st[d].wait_before(pool, i, "bg")
                        g_c = G[:, ds(c, 1), 4 * d:4 * d + 4].rearrange("p a n -> p (a n)")
                        b_c = BETA[:, ds(c, 1), 4 * d:4 * d + 4].rearrange("p a n -> p (a n)")
                        st.done(pool.tensor_copy(b["GB"][:, :, :], wide(g_c, P)), "gb")
                        st.done(pool.tensor_copy(b["BB"][:, :, :], wide(b_c, P)), "bb")
                        pe_st[d].wait_before(pool, i, "qk")
                        st.done(pool.tensor_copy(b["KT"][:, :, :], QKV[:, 4:8, ds(c * P + 2, P)]), "kt")
                    for d in lanes:
                        b, c, st = B[d], chunk(i, d), pool_st[d]
                        pe_st[d].wait_before(pool, i, "st")
                        b_c = BETA[:, ds(c, 1), 4 * d:4 * d + 4].rearrange("p a n -> p (a n)")
                        k_c, v_c = (x[:, ds(c, 1), :].rearrange("p a (h n) -> p (a h) n", h=4) for x in (KTOK, VTOK))
                        st.done(pool.tensor_tensor(b["VB"][:, :, :], v_c, wide(b_c, P), ALU.mult), "vb")
                        act_st[d].wait(pool, i, "ld")
                        pass_waits(pool, sems[8])
                        st.done(pool.tensor_tensor(b["KD"][:, :, :], k_c, wide(b["LD"][:, :], P), ALU.mult), "kd")
                        dve_st[d].wait(pool, i, "be")
                        pass_waits(pool, sems[8])
                        st.done(pool.tensor_tensor(b["KBG"][:, :, :], k_c, wide(b["BE"][:, :], P), ALU.mult), "kbg")

            @block.tensor
            def _(pe):
                for d in lanes:
                    pe_st[d].open(pe)

                def each_head(d, n, lhsT, rhs):
                    for h in range(4):
                        last = pe.matmul(bank(d, n)[:, h * P:(h + 1) * P], lhsT(h), rhs(h), start=True, stop=True)
                    return last

                with pe.Fori(0, 4) as i:
                    for d in lanes:
                        b, c, st = B[d], chunk(i, d), pe_st[d]
                        pool_st[d].wait(pe, i, "bb")
                        act_st[d].wait_before(pe, i, "wt")
                        dve_st[d].wait_before(pe, i, "vn")
                        pe.matmul(bank(d, 3)[:, 0:4], C[:, INCL + d, :], G[:, ds(c, 1), 4 * d:4 * d + 4].rearrange("p a n -> p (a n)"), start=True, stop=True)
                        st.done(each_head(d, 0, lambda h: b["GB"][:, h, :], lambda h: C[:, INCL + d, :]), "gc")
                        act_st[d].wait_before(pe, i, "o")
                        dve_st[d].wait_before(pe, i, "st3")
                        pool_st[d].wait(pe, i, "kt")
                        each_head(d, 1, lambda h: b["BB"][:, h, :], lambda h: C[:, IDENT, :])
                        st.done(each_head(d, 2, lambda h: b["KT"][:, h, :], lambda h: QKV[:, 4 + h, ds(c * P + 2, P)]), "bg")
                        dve_st[d].wait(pe, i, "gcs")
                        st.done(each_head(d, 3, lambda h: b["KT"][:, h, :], lambda h: QKV[:, h, ds(c * P + 2, P)]), "qk")
                    for n in range(LEVELS):
                        for d in lanes:
                            b, st = B[d], pe_st[d]
                            dve_st[d].wait(pe, i, f"lb{n}")
                            if n == 0:
                                act_st[d].wait(pe, i, "eg")
                            else:
                                act_st[d].wait(pe, i, f"p{n - 1}")
                            st.done(each_head(d, 0, lambda h: b["LB"][:, h, :], lambda h: b["T"][:, h, :]), f"p{n}")
                        for d in lanes:
                            b, st = B[d], pe_st[d]
                            act_st[d].wait(pe, i, f"p{n}")
                            dve_st[d].wait(pe, i, "qg" if n == 0 else f"tt{n - 1}")
                            if n < LEVELS - 1:
                                each_head(d, 1, lambda h: b["TT"][:, h, :], lambda h: b["PP"][:, h, :])
                            st.done(each_head(d, 2, lambda h: b["PP"][:, h, :], lambda h: b["TT"][:, h, :]), f"d{n}")
                    for d in lanes:
                        b, st = B[d], pe_st[d]
                        dve_st[d].wait(pe, i, f"tt{LEVELS - 1}")
                        pool_st[d].wait(pe, i, "kbg")
                        st.done(each_head(d, 3, lambda h: b["KBG"][:, h, :], lambda h: b["TT"][:, h, :]), "wt")
                    for d in lanes:
                        b, st = B[d], pe_st[d]
                        act_st[d].wait(pe, i, "wt")
                        dve_st[d].wait_before(pe, i, "st3")
                        for h in range(4):
                            last = contract(pe, bank(d, 0)[:, h * P:(h + 1) * P],
                                            [(b["TT"][:, h, :], b["VB"][:, h, :]), (b["WT"][:, h, :], b["ST"][:, h, :])])
                        st.done(last, "vn")
                    for d in lanes:
                        b, st = B[d], pe_st[d]
                        dve_st[d].wait(pe, i, "vn")
                        for h in range(4):
                            last = contract(pe, bank(d, 1)[:, h * P:(h + 1) * P],
                                            [(b["ST"][:, h, :], b["QG"][:, h, :]), (b["VN"][:, h, :], b["QK"][:, h, :])])
                        st.done(last, "o")
                        st.done(each_head(d, 2, lambda h: b["KD"][:, h, :], lambda h: b["VN"][:, h, :]), "st")

            @block.scalar
            def _(act):
                for d in lanes:
                    act_st[d].open(act)
                with act.Fori(0, 4) as i:
                    for d in lanes:
                        b, st = B[d], act_st[d]
                        pe_st[d].wait(act, i, "gc")
                        dve_st[d].wait_before(act, i, "st3")
                        st.done(act.activation(b["EG"][:, :, :], per_head(bank(d, 0)), ACT.Exp), "eg")
                        dve_st[d].wait(act, i, "dif3")
                        st.done(act.activation(b["DM"][:, :, :], b["DM"][:, :, :], ACT.Exp), "dm")
                        st.done(act.activation(b["EGS"][:, :], b["GCS"][:, :], ACT.Exp), "egs")
                        dve_st[d].wait(act, i, "ldif")
                        st.done(act.activation(b["LD"][:, :], b["LD"][:, :], ACT.Exp), "ld")
                    for n in range(LEVELS):
                        for d in lanes:
                            pe_st[d].wait(act, i, f"p{n}")
                            act_st[d].done(act.copy(B[d]["PP"][:, :, :], per_head(bank(d, 0))), f"p{n}")
                    for d in lanes:
                        pe_st[d].wait(act, i, "wt")
                        act_st[d].done(act.mul(B[d]["WT"][:, :, :], per_head(bank(d, 3)), -1.0), "wt")
                    for d in lanes:
                        pe_st[d].wait(act, i, "o")
                        act_st[d].done(act.copy(O2[:, 4 * d:4 * d + 4, ds(chunk(i, d) * P, P)], per_head(bank(d, 1))), "o")

            @block.vector
            def _(dve):
                for d in lanes:
                    dve_st[d].open(dve)
                    dve.memset(B[d]["ST"][:, :, :], 0.0)
                with dve.Fori(0, 4) as i:
                    for d in lanes:
                        b, c, st = B[d], chunk(i, d), dve_st[d]
                        gcb = per_head(bank(d, 0))
                        pe_st[d].wait(dve, i, "gc")
                        act_st[d].wait_before(dve, i, "egs")
                        st.done(dve.tensor_copy(b["GCS"][:, :], bank(d, 3)[:, 0:4]), "gcs")
                        st.wait(dve, i, "gcs")
                        act_st[d].wait(dve, i, "eg")
                        for h in range(4):
                            st.done(dve.tensor_scalar(b["DM"][:, h, :], gcb[:, h, :], b["GCS"][:, h:h + 1], 0.0, ALU.subtract, ALU.min), f"dif{h}")
                        act_st[d].wait(dve, i, "egs")
                        pool_st[d].wait_before(dve, i, "kbg")
                        b_c = BETA[:, ds(c, 1), 4 * d:4 * d + 4].rearrange("p a n -> p (a n)")
                        st.done(dve.tensor_tensor(b["BE"][:, :], b_c, b["EGS"][:, :], ALU.mult), "be")
                        pool_st[d].wait_before(dve, i, "kd")
                        st.done(dve.tensor_tensor(b["LD"][:, :], gcb[:, :, last_col[d]], b["GCS"][:, :], ALU.subtract), "ldif")
                        act_st[d].wait(dve, i, "dm")
                        st.done(dve.tensor_tensor(b["DM"][:, :, :], b["DM"][:, :, :], heads(C[:, INCL + d, :], 4), ALU.mult), "mask")
                        pe_st[d].wait(dve, i, "bg")
                        st.wait(dve, i, "mask")
                        st.done(dve.tensor_tensor(b["AT"][:, :, :], per_head(bank(d, 2)), b["DM"][:, :, :], ALU.mult), "at")
                        st.wait(dve, i, "at")
                        st.done(dve.tensor_tensor(b["AT"][:, :, :], per_head(bank(d, 1)), b["AT"][:, :, :], ALU.mult), "atb")
                        pe_st[d].wait(dve, i, "qk")
                        st.done(dve.tensor_tensor(b["QK"][:, :, :], per_head(bank(d, 3)), b["DM"][:, :, :], ALU.mult), "qk")
                        st.done(dve.tensor_copy(b["T"][:, :, :], heads(C[:, IDENT, :], 4)), "t")
                        st.done(dve.tensor_copy(b["TT"][:, :, :], heads(C[:, IDENT, :], 4)), "tt")
                        act_st[d].wait(dve, i, "eg")
                        st.done(dve.tensor_tensor(b["QG"][:, :, :], QKV[:, 0:4, ds(c * P + 2, P)], b["EG"][:, :, :], ALU.mult), "qg")
                    for d in lanes:
                        b, st = B[d], dve_st[d]
                        st.wait(dve, i, "atb")
                        st.done(dve.tensor_tensor(b["LB"][:, :, :], b["AT"][:, :, :], heads(C[:, PAIR + d * LEVELS, :], 4), ALU.mult), "lb0")
                    for n in range(LEVELS):
                        for d in lanes:
                            b, st = B[d], dve_st[d]
                            pe_st[d].wait(dve, i, f"d{n}")
                            if n < LEVELS - 1:
                                st.done(dve.tensor_tensor(b["T"][:, :, :], b["T"][:, :, :], per_head(bank(d, 1)), ALU.subtract), f"t{n}")
                            st.done(dve.tensor_tensor(b["TT"][:, :, :], b["TT"][:, :, :], per_head(bank(d, 2)), ALU.subtract), f"tt{n}")
                            if n < LEVELS - 1:
                                st.done(dve.tensor_tensor(b["LB"][:, :, :], b["AT"][:, :, :], heads(C[:, PAIR + d * LEVELS + n + 1, :], 4), ALU.mult), f"lb{n + 1}")
                    for d in lanes:
                        pe_st[d].wait(dve, i, "vn")
                        dve_st[d].done(dve.tensor_copy(B[d]["VN"][:, :, :], per_head(bank(d, 0))), "vn")
                    for d in lanes:
                        b, st = B[d], dve_st[d]
                        pe_st[d].wait(dve, i, "st")
                        for h in range(4):
                            st.done(dve.scalar_tensor_tensor(b["ST"][:, h, :], b["ST"][:, h, :], b["EG"][:, h, last_col[d]:last_col[d] + 1],
                                                             bank(d, 2)[:, h * P:(h + 1) * P], ALU.mult, ALU.add), f"st{h}")


def head_norm_stage(nc, PS, C, O2, Z, weight, out, SQ, RS):
    with stage(nc, "vector_steps", "squares", "roots", "sums") as (dve_s, sq_s, root_s, sum_s):
        dve_st = Steps(dve_s, ["add", "mean", "inv", "norm", "out"])
        sq, root, sums = Steps(sq_s, ["sq"]), Steps(root_s, ["root"]), Steps(sum_s, ["sum"])
        with nc.Block() as block:

            @block.vector
            def _(dve):
                dve_st.open(dve)
                with dve.Fori(0, 4) as h:
                    o = tile(out, h)
                    dve_st.done(dve.tensor_tensor(o, tile(O2, h), tile(O2, h + 4), ALU.add), "add")
                    sums.wait(dve, h, "sum")
                    dve_st.done(dve.tensor_scalar(RS[:, 0, :], PS[:, 0, :], 1.0 / P, 1e-6, ALU.mult, ALU.add), "mean")
                    dve_st.wait(dve, h, "mean")
                    dve_st.done(dve.reciprocal(RS[:, 0, :], RS[:, 0, :]), "inv")
                    root.wait(dve, h, "root")
                    dve_st.done(dve.scalar_tensor_tensor(o, o, weight, RS[:, 0, :], ALU.mult, ALU.mult), "norm")
                    dve_st.wait(dve, h, "norm")
                    dve_st.done(dve.tensor_tensor(o, o, tile(Z, h), ALU.mult), "out")

            @block.scalar
            def _(act):
                sq.open(act)
                root.open(act)
                with act.Fori(0, 4) as h:
                    dve_st.wait(act, h, "add")
                    sums.wait_before(act, h, "sum")
                    sq.done(act.activation(SQ[:, 0, :], tile(out, h), ACT.Square), "sq")
                    dve_st.wait(act, h, "inv")
                    root.done(act.activation(RS[:, 0, :], RS[:, 0, :], ACT.Sqrt), "root")

            @block.tensor
            def _(pe):
                sums.open(pe)
                with pe.Fori(0, 4) as h:
                    sq.wait(pe, h, "sq")
                    dve_st.wait_before(pe, h, "mean")
                    sums.done(pe.matmul(PS[:, 0, :], C[:, ONES, :], SQ[:, 0, :], start=True, stop=True), "sum")


def lower_bound_stage(nc, A, SMALL, LB, OM, PAIRB):
    lg = A["hg_lb_logits"]
    with stage(nc, "logits_in", "steps") as (logits_in, steps):
        with nc.Block() as block:

            @block.sync
            def _(sp):
                for n in range(2):
                    sp.dma_start(PAIRB[:, n, :], lg[n].rearrange("d n -> (d n)").partition_broadcast(P)).then_inc(logits_in, 16)

            @block.vector
            def _(dve):
                dve.wait_ge(logits_in, 32)
                dve.tensor_tensor(LB[:, :], PAIRB[:, 0, :], PAIRB[:, 1, :], ALU.subtract).then_inc(steps, 1)
                dve.wait_ge(steps, 2)
                dve.tensor_scalar(LB[:, :], LB[:, :], 1.0, None, ALU.add).then_inc(steps, 1)
                dve.wait_ge(steps, 3)
                dve.reciprocal(LB[:, :], LB[:, :]).then_inc(steps, 1)
                dve.wait_ge(steps, 4)
                dve.tensor_scalar(LB[:, :], LB[:, :], SMALL[:, 16:17], None, ALU.mult).then_inc(steps, 1)
                dve.wait_ge(steps, 5)
                dve.tensor_scalar(OM[:, :], LB[:, :], -1.0, 1.0, ALU.mult, ALU.add).then_inc(steps, 1)

            @block.scalar
            def _(act):
                act.wait_ge(steps, 1)
                act.activation(LB[:, :], LB[:, :], ACT.Exp).then_inc(steps, 1)


def hgrn_proj_stage(nc, PS, l, w_in, H, W, LB, OM, LF, KK, HI, HQ, HG, E0, E1):
    col0 = 4 * 512 + 16
    order = (1, 2, 3, 0, 4)
    with stage(nc, "w0_in", "w1_in", "projected", "vector_steps", "scalar_steps") as (w0, w1, proj_s, dve_s, act_s):
        w_loaded = (w0, w1)
        pnames = []
        for g in range(5):
            pnames += [f"unit{g}_0", f"unit{g}_1"] if g < 3 else [f"unit{g}_{m}" for m in range(4)]
        proj = Steps(proj_s, pnames)
        act_st = Steps(act_s, [f"{a}{g}_{c}" for g in range(2) for c in range(4) for a in ("e", "ln1", "lnb")]
                       + [f"hi{c}" for c in range(4)] + [f"silu{g}_{m}" for g in (3, 4) for m in range(4)])
        dve_st = Steps(dve_s, [f"{a}{g}_{c}" for g in range(2) for c in range(4) for a in ("lbe", "e1", "inv", "er", "kk", "lf")]
                       + [f"q{m}" for m in range(4)])
        wl = w_in[ds(l, 1)].rearrange("l (k p) n -> p (l k) n", p=P)
        with nc.Block() as block:

            @block.sync
            def _(sp):
                for g in range(5):
                    for s in range(2):
                        if g:
                            name = f"unit{g - 1}_{s}" if g <= 3 else f"unit{g - 1}_{2 * s + 1}"
                            sp.wait_ge(proj.sem, proj.place[name])
                        sp.dma_start(W[:, s], wl[:, :, ds(col0 + order[g] * 512 + s * UNIT, UNIT)]).then_inc(w_loaded[s], 16)

            @block.tensor
            def _(pe):
                def free(g, c):
                    if 1 <= g <= 2:
                        pe.wait_ge(act_st.sem, act_st.place[f"e{g - 1}_{c}"])
                    if g == 3:
                        pe.wait_ge(act_st.sem, act_st.place[f"hi{c}"])
                    if g == 4:
                        pe.wait_ge(act_st.sem, act_st.place[f"silu3_{c}"])

                for g in range(3):
                    for s in range(2):
                        pe.wait_ge(w_loaded[s], 16 * (g + 1))
                        for c in range(4):
                            if s == 0:
                                free(g, c)
                            last = contract(pe, PS[:, c, s * UNIT:(s + 1) * UNIT],
                                            [(H[:, k, c * P:(c + 1) * P], W[:, s, k, :]) for k in range(8)])
                        proj.done(last, f"unit{g}_{s}")
                for g in (3, 4):
                    for m in range(4):
                        s, half = divmod(m, 2)
                        if half == 0:
                            pe.wait_ge(w_loaded[s], 16 * (g + 1))
                        free(g, m)
                        last = contract(pe, PS[:, m, :], [(W[:, s, k, half * P:(half + 1) * P], H[:, k, :]) for k in range(8)])
                        proj.done(last, f"unit{g}_{m}")

            @block.scalar
            def _(act):
                for g in range(2):
                    act.wait_ge(proj.sem, proj.place[f"unit{g}_1"])
                    for c in range(4):
                        if g or c >= 2:
                            gg, cc = (g, c - 2) if c >= 2 else (g - 1, c + 2)
                            act.wait_ge(dve_st.sem, dve_st.place[f"lf{gg}_{cc}"])
                        act_st.done(act.activation(E0[:, c % 2, :], PS[:, c, :], ACT.Exp, scale=-1.0), f"e{g}_{c}")
                        act.wait_ge(act_st.sem, act_st.place[f"e{g}_{c}"])
                        act_st.done(act.activation(E1[:, c % 2, :], E0[:, c % 2, :], ACT.Ln, bias=1.0), f"ln1{g}_{c}")
                        act.wait_ge(dve_st.sem, dve_st.place[f"lbe{g}_{c}"])
                        act_st.done(act.activation(LF[:, g * 4 + c, :], LF[:, g * 4 + c, :], ACT.Ln, bias=1.0), f"lnb{g}_{c}")
                act.wait_ge(proj.sem, proj.place["unit2_1"])
                for c in range(4):
                    act_st.done(act.copy(HI[:, c, :], PS[:, c, :]), f"hi{c}")
                for g, dst in ((3, HQ), (4, HG)):
                    for m in range(4):
                        act.wait_ge(proj.sem, proj.place[f"unit{g}_{m}"])
                        act_st.done(act.activation(dst[:, m, :], PS[:, m, :], ACT.Silu), f"silu{g}_{m}")

            @block.vector
            def _(dve):
                for g in range(2):
                    cols = slice(g * 512, (g + 1) * 512)
                    for c in range(4):
                        lf, kk = LF[:, g * 4 + c, :], KK[:, g * 4 + c, :]
                        own = lambda name: dve.wait_ge(dve_st.sem, dve_st.place[f"{name}{g}_{c}"])
                        dve.wait_ge(act_st.sem, act_st.place[f"e{g}_{c}"])
                        dve_st.done(dve.tensor_tensor(lf, E0[:, c % 2, :], LB[:, cols], ALU.mult), f"lbe{g}_{c}")
                        dve_st.done(dve.tensor_scalar(kk, E0[:, c % 2, :], 1.0, None, ALU.add), f"e1{g}_{c}")
                        own("e1")
                        dve_st.done(dve.reciprocal(kk, kk), f"inv{g}_{c}")
                        own("inv")
                        dve_st.done(dve.tensor_tensor(kk, kk, E0[:, c % 2, :], ALU.mult), f"er{g}_{c}")
                        own("er")
                        dve_st.done(dve.tensor_tensor(kk, kk, OM[:, cols], ALU.mult), f"kk{g}_{c}")
                        dve.wait_ge(act_st.sem, act_st.place[f"lnb{g}_{c}"])
                        dve_st.done(dve.tensor_tensor(lf, lf, E1[:, c % 2, :], ALU.subtract), f"lf{g}_{c}")
                for m in range(4):
                    dve.wait_ge(act_st.sem, act_st.place[f"silu3_{m}"])
                    dve_st.done(dve.tensor_scalar(HQ[:, m, :], HQ[:, m, :], P ** -0.5, None, ALU.mult), f"q{m}")


def hgrn_stage(nc, PS, C, LF, KK, HI, HQ, O2, new):
    lanes = (0, 1)
    B = [{n: new(f"h{n}{d}", [P, 4, P]) for n in ("LFS", "KS", "IS", "KT", "EC", "ES", "QE", "KD", "AT", "ST", "X0", "X1", "E0", "E1")} for d in lanes]
    last_col = (P - 1, 0)
    pool_names = ["lf", "k", "i", "kd"]
    pe_names = ["kt", "cum", "suf", "dia", "e0"]
    for n in range(LEVELS):
        if n + 1 < LEVELS:
            pe_names.append(f"e{n + 1}")
        pe_names.append(f"a{n}")
    pe_names += ["o", "st"]
    act_names = ["kt", "cum", "suf"] + [f"e{n}" for n in range(LEVELS)] + ["o"]
    dve_names = ["zero", "dia", "qe"]
    for n in range(LEVELS):
        dve_names += [f"xq{n}", f"xk{n}"]
        if n:
            dve_names.append(f"a{n - 1}")
    dve_names += [f"a{LEVELS - 1}"] + [f"st{h}" for h in range(4)]
    with stage(nc, *[f"{e}{d}" for d in lanes for e in ("hgrn_pe", "hgrn_act", "hgrn_dve", "hgrn_pool")], "waits_passed") as sems:
        pe_st = [Steps(sems[4 * d], pe_names) for d in lanes]
        act_st = [Steps(sems[4 * d + 1], act_names) for d in lanes]
        dve_st = [Steps(sems[4 * d + 2], dve_names) for d in lanes]
        pool_st = [Steps(sems[4 * d + 3], pool_names) for d in lanes]

        def chunk(i, d):
            return i if d == 0 else i * -1 + 3

        def bank(d, n):
            return PS[:, 4 * d + n, :]

        def halves(ap, n, second):
            v = ap.rearrange("p h (b two a) -> p (h b) two a", two=2, a=1 << n)
            return v[:, :, 1 if second else 0, :]

        with nc.Block() as block:

            @block.gpsimd
            def _(pool):
                for d in lanes:
                    pool_st[d].open(pool)
                with pool.Fori(0, 4) as i:
                    for d in lanes:
                        b, st = B[d], pool_st[d]
                        row = ds(chunk(i, d) + 4 * d, 1)
                        f = lambda t: t[:, :, :].rearrange("p h n -> p (h n)")
                        pe_st[d].wait_before(pool, i, f"e{LEVELS - 1}")
                        st.done(pool.tensor_copy(f(b["LFS"]), LF[:, row, :].rearrange("p a n -> p (a n)")), "lf")
                        st.wait_before(pool, i, "kd")
                        st.done(pool.tensor_copy(f(b["KS"]), KK[:, row, :].rearrange("p a n -> p (a n)")), "k")
                        pe_st[d].wait_before(pool, i, "st")
                        st.done(pool.tensor_copy(f(b["IS"]), HI[:, ds(chunk(i, d), 1), :].rearrange("p a n -> p (a n)")), "i")
                    for d in lanes:
                        b, st = B[d], pool_st[d]
                        act_st[d].wait(pool, i, "suf")
                        st.done(pool.tensor_tensor(b["KD"][:, :, :], b["KS"][:, :, :], b["ES"][:, :, :], ALU.mult), "kd")

            @block.tensor
            def _(pe):
                for d in lanes:
                    pe_st[d].open(pe)

                def each_head(d, n, lhsT, rhs):
                    for h in range(4):
                        last = pe.matmul(bank(d, n)[:, h * P:(h + 1) * P], lhsT(h), rhs(h), start=True, stop=True)
                    return last

                def exponents(i, d, n):
                    b, st = B[d], pe_st[d]
                    if n >= 2:
                        act_st[d].wait(pe, i, f"e{n - 2}")
                    else:
                        act_st[d].wait(pe, i, ("cum", "suf")[n])
                    st.done(each_head(d, n % 2, lambda h: b["LFS"][:, h, :], lambda h: C[:, REACH + d * LEVELS + n, :]), f"e{n}")

                with pe.Fori(0, 4) as i:
                    for d in lanes:
                        b, c, st = B[d], chunk(i, d), pe_st[d]
                        pool_st[d].wait(pe, i, "k")
                        dve_st[d].wait_before(pe, i, "st3")
                        for h in range(4):
                            last = pe.transpose(bank(d, 2)[:, h * P:(h + 1) * P], b["KS"][:, h, :], C[:, IDENT, :])
                        st.done(last, "kt")
                        act_st[d].wait_before(pe, i, f"e{LEVELS - 1}")
                        st.done(each_head(d, 0, lambda h: b["LFS"][:, h, :], lambda h: C[:, INCL + d, :]), "cum")
                        st.done(pe.matmul(bank(d, 1), C[:, AFTER + d, :], b["LFS"][:, :, :].rearrange("p h n -> p (h n)"), start=True, stop=True), "suf")
                        act_st[d].wait(pe, i, "kt")
                        st.done(each_head(d, 3, lambda h: b["KT"][:, h, :], lambda h: HQ[:, h, ds(c * P, P)]), "dia")
                    for d in lanes:
                        exponents(i, d, 0)
                    for n in range(LEVELS):
                        for d in lanes:
                            b, st = B[d], pe_st[d]
                            if n + 1 < LEVELS:
                                exponents(i, d, n + 1)
                            if n == 0:
                                act_st[d].wait(pe, i, "kt")
                            dve_st[d].wait(pe, i, f"xk{n}")
                            x = b[f"X{n % 2}"]
                            st.done(each_head(d, 2 + n % 2, lambda h: x[:, h, :], lambda h: x[:, h, :]), f"a{n}")
                    for d in lanes:
                        b, st = B[d], pe_st[d]
                        dve_st[d].wait(pe, i, f"a{LEVELS - 1}")
                        pool_st[d].wait(pe, i, "kd")
                        for h in range(4):
                            last = contract(pe, bank(d, 3)[:, h * P:(h + 1) * P],
                                            [(b["ST"][:, h, :], b["QE"][:, h, :]), (b["IS"][:, h, :], b["AT"][:, h, :])])
                        st.done(last, "o")
                        st.done(each_head(d, 2, lambda h: b["KD"][:, h, :], lambda h: b["IS"][:, h, :]), "st")

            @block.scalar
            def _(act):
                for d in lanes:
                    act_st[d].open(act)
                with act.Fori(0, 4) as i:
                    for d in lanes:
                        b, st = B[d], act_st[d]
                        pe_st[d].wait(act, i, "kt")
                        dve_st[d].wait_before(act, i, f"xk{LEVELS - 1}")
                        st.done(act.copy(b["KT"][:, :, :], per_head(bank(d, 2))), "kt")
                        pe_st[d].wait(act, i, "cum")
                        dve_st[d].wait_before(act, i, "st3")
                        st.done(act.activation(b["EC"][:, :, :], per_head(bank(d, 0)), ACT.Exp), "cum")
                        pe_st[d].wait(act, i, "suf")
                        pool_st[d].wait_before(act, i, "kd")
                        st.done(act.activation(b["ES"][:, :, :], per_head(bank(d, 1)), ACT.Exp), "suf")
                    for n in range(LEVELS):
                        for d in lanes:
                            b, st = B[d], act_st[d]
                            pe_st[d].wait(act, i, f"e{n}")
                            if n >= 2:
                                dve_st[d].wait(act, i, f"xk{n - 2}")
                            else:
                                dve_st[d].wait_before(act, i, f"xk{LEVELS - 1}")
                            st.done(act.activation(b[f"E{n % 2}"][:, :, :], per_head(bank(d, n % 2)), ACT.Exp), f"e{n}")
                    for d in lanes:
                        pe_st[d].wait(act, i, "o")
                        act_st[d].done(act.copy(O2[:, 4 * d:4 * d + 4, ds(chunk(i, d) * P, P)], per_head(bank(d, 3))), "o")

            @block.vector
            def _(dve):
                for d in lanes:
                    dve_st[d].open(dve)
                    dve.memset(B[d]["ST"][:, :, :], 0.0)
                mask = lambda n: heads(C[:, n, :], 4).bitcast(I32)
                with dve.Fori(0, 4) as i:
                    for d in lanes:
                        b, c, st = B[d], chunk(i, d), dve_st[d]
                        pe_st[d].wait_before(dve, i, "o")
                        st.done(dve.memset(b["AT"][:, :, :], 0.0), "zero")
                        pe_st[d].wait(dve, i, "dia")
                        st.wait(dve, i, "zero")
                        pass_waits(dve, sems[8])
                        st.done(dve.copy_predicated(b["AT"][:, :, :], mask(IDENT), per_head(bank(d, 3))), "dia")
                        act_st[d].wait(dve, i, "cum")
                        st.done(dve.tensor_tensor(b["QE"][:, :, :], HQ[:, :, ds(c * P, P)], b["EC"][:, :, :], ALU.mult), "qe")
                    for n in range(LEVELS):
                        for d in lanes:
                            b, c, st = B[d], chunk(i, d), dve_st[d]
                            act_st[d].wait(dve, i, f"e{n}")
                            if n >= 2:
                                pe_st[d].wait(dve, i, f"a{n - 2}")
                            x, e = b[f"X{n % 2}"][:, :, :], b[f"E{n % 2}"][:, :, :]
                            later = d == 0
                            q = HQ[:, :, ds(c * P, P)]
                            qv = q.rearrange("p h (b two a) -> p h b two a", two=2, a=1 << n)[:, :, :, int(later), :]
                            xv = x.rearrange("p h (b two a) -> p h b two a", two=2, a=1 << n)[:, :, :, int(later), :]
                            ev = e.rearrange("p h (b two a) -> p h b two a", two=2, a=1 << n)[:, :, :, int(later), :]
                            st.done(dve.tensor_tensor(xv, qv, ev, ALU.mult), f"xq{n}")
                            st.done(dve.tensor_tensor(halves(x, n, not later), halves(b["KT"][:, :, :], n, not later), halves(e, n, not later), ALU.mult), f"xk{n}")
                            if n:
                                pe_st[d].wait(dve, i, f"a{n - 1}")
                                st.wait(dve, i, f"a{n - 2}" if n > 1 else "dia")
                                pass_waits(dve, sems[8])
                                st.done(dve.copy_predicated(b["AT"][:, :, :], mask(PAIR + d * LEVELS + n - 1), per_head(bank(d, 2 + (n - 1) % 2))), f"a{n - 1}")
                    for d in lanes:
                        b, st, n = B[d], dve_st[d], LEVELS - 1
                        pe_st[d].wait(dve, i, f"a{n}")
                        st.wait(dve, i, f"a{n - 1}")
                        pass_waits(dve, sems[8])
                        st.done(dve.copy_predicated(b["AT"][:, :, :], mask(PAIR + d * LEVELS + n), per_head(bank(d, 2 + n % 2))), f"a{n}")
                    for d in lanes:
                        b, st = B[d], dve_st[d]
                        pe_st[d].wait(dve, i, "st")
                        for h in range(4):
                            st.done(dve.scalar_tensor_tensor(b["ST"][:, h, :], b["ST"][:, h, :], b["EC"][:, h, last_col[d]:last_col[d] + 1],
                                                             bank(d, 2)[:, h * P:(h + 1) * P], ALU.mult, ALU.add), f"st{h}")


def branch_stage(nc, PS, l, A, H, ODN, OHG, M, WG, WB, SG, TMP):
    D = M.shape[1] * P
    col0 = A["w_in"].shape[2] - 2 * D
    with stage(nc, "wg0_in", "wg1_in", "wb0_in", "wb1_in", "projected", "sigmoid_done", "vector_steps") as (
            g0, g1, b0, b1, proj_s, sig_s, dve_s):
        gate_in, branch_in = (g0, g1), (b0, b1)
        proj = Steps(proj_s, [f"{a}{j}" for j in range(4) for a in "gb"])
        sig = Steps(sig_s, [f"tile{j}" for j in range(4)])
        dve_st = Steps(dve_s, ["dn0", "dn1", "hg0", "sum0", "hg1", "sum1"])
        gl = A["w_in"][ds(l, 1)].rearrange("l (k p) n -> p (l k) n", p=P)
        bl = [A[n][ds(l, 1)].rearrange("l (k p) n -> p (l k) n", p=P) for n in ("w_branch_dn", "w_branch_hg")]
        with nc.Block() as block:

            @block.sync
            def _(sp):
                with sp.Fori(0, D // UNIT) as g:
                    for r in range(2):
                        proj.wait_before(sp, g, f"b{2 * r + 1}")
                        sp.dma_start(WG[:, r], gl[:, :, ds(g * UNIT + col0 + r * D, UNIT)]).then_inc(gate_in[r], 16)
                        sp.dma_start(WB[:, r], bl[r][:, :, ds(g * UNIT, UNIT)]).then_inc(branch_in[r], 16)

            @block.tensor
            def _(pe):
                proj.open(pe)
                with pe.Fori(0, D // UNIT) as g:
                    for r, o in enumerate((ODN, OHG)):
                        pe.wait_ge(gate_in[r], 16 * (g + 1))
                        for m in range(2):
                            j = 2 * r + m
                            sig.wait_before(pe, g, f"tile{j}")
                            last = contract(pe, PS[:, j, :], [(WG[:, r, k, m * P:(m + 1) * P], H[:, k, :]) for k in range(8)])
                            proj.done(last, f"g{j}")
                            if m == 0:
                                pe.wait_ge(branch_in[r], 16 * (g + 1))
                            dve_st.wait_before(pe, g, ("dn0", "dn1", "hg0", "hg1")[j])
                            last = contract(pe, PS[:, 4 + j, :], [(WB[:, r, k, m * P:(m + 1) * P], o[:, k, :]) for k in range(4)])
                            proj.done(last, f"b{j}")

            @block.scalar
            def _(act):
                sig.open(act)
                with act.Fori(0, D // UNIT) as g:
                    for j in range(4):
                        proj.wait(act, g, f"g{j}")
                        dve_st.wait_before(act, g, ("dn0", "dn1", "hg0", "hg1")[j])
                        sig.done(act.activation(SG[:, j, :], PS[:, j, :], ACT.Sigmoid), f"tile{j}")

            @block.vector
            def _(dve):
                dve_st.open(dve)
                with dve.Fori(0, D // UNIT) as g:
                    for m in range(2):
                        sig.wait(dve, g, f"tile{m}")
                        proj.wait(dve, g, f"b{m}")
                        dve_st.done(dve.tensor_tensor(tile(M, g * 2 + m), SG[:, m, :], PS[:, 4 + m, :], ALU.mult), f"dn{m}")
                    for m in range(2):
                        sig.wait(dve, g, f"tile{2 + m}")
                        proj.wait(dve, g, f"b{2 + m}")
                        dve_st.done(dve.tensor_tensor(TMP[:, m, :], SG[:, 2 + m, :], PS[:, 6 + m, :], ALU.mult), f"hg{m}")
                        dve_st.wait(dve, g, f"hg{m}")
                        dve_st.done(dve.tensor_tensor(tile(M, g * 2 + m), tile(M, g * 2 + m), TMP[:, m, :], ALU.add), f"sum{m}")


def ffn_up_stage(nc, PS, l, A, H, PAR, HID, W, GP, ACC):
    F = A["w_down"].shape[1]
    with stage(nc, "wg_in", "wu_in", "projected", "vector_steps", "silu_done") as (wg, wu, proj_s, dve_s, silu_s):
        w_loaded = (wg, wu)
        proj = Steps(proj_s, [f"tile{j}" for j in range(4)])
        dve_st = Steps(dve_s, [f"{a}{m}" for m in range(2) for a in ("kept", "tap0_", "tap1_", "tap2_")] + ["hid0", "hid1"])
        silu = Steps(silu_s, ["tile0", "tile1"])
        wl = A["w_up"][ds(l, 1)].rearrange("l (k p) n -> p (l k) n", p=P)
        with nc.Block() as block:

            @block.sync
            def _(sp):
                with sp.Fori(0, F // UNIT) as g:
                    for s in range(2):
                        proj.wait_before(sp, g, f"tile{2 * s + 1}")
                        sp.dma_start(W[:, s], wl[:, :, ds(g * UNIT + s * F, UNIT)]).then_inc(w_loaded[s], 16)

            @block.tensor
            def _(pe):
                proj.open(pe)
                with pe.Fori(0, F // UNIT) as g:
                    for j in range(4):
                        s, m = divmod(j, 2)
                        if m == 0:
                            pe.wait_ge(w_loaded[s], 16 * (g + 1))
                        dve_st.wait_before(pe, g, f"kept{m}" if s == 0 else f"hid{m}")
                        last = contract(pe, PS[:, j, :], [(W[:, s, k, m * P:(m + 1) * P], H[:, k, :]) for k in range(8)])
                        proj.done(last, f"tile{j}")

            @block.vector
            def _(dve):
                dve_st.open(dve)
                dve.memset(GP[:, :, 0:1], 0.0)
                dve.memset(GP[:, :, 513:514], 0.0)
                with dve.Fori(0, F // UNIT) as g:
                    for m in range(2):
                        proj.wait(dve, g, f"tile{m}")
                        dve_st.done(dve.tensor_copy(GP[:, m, 1:513], PS[:, m, :]), f"kept{m}")
                        dve_st.wait(dve, g, f"kept{m}")
                        w = lambda tap: PAR[:, ds(g * 2 + (m + tap * 22), 1)]
                        silu.wait_before(dve, g, f"tile{m}")
                        dve_st.done(dve.tensor_scalar(ACC[:, m, :], GP[:, m, 0:512], w(0), w(3), ALU.mult, ALU.add), f"tap0_{m}")
                        for tap in (1, 2):
                            dve_st.wait(dve, g, f"tap{tap - 1}_{m}")
                            dve_st.done(dve.scalar_tensor_tensor(ACC[:, m, :], GP[:, m, tap:tap + 512], w(tap), ACC[:, m, :], ALU.mult, ALU.add), f"tap{tap}_{m}")
                    for m in range(2):
                        silu.wait(dve, g, f"tile{m}")
                        proj.wait(dve, g, f"tile{2 + m}")
                        t = tile(HID, g * 2 + m)
                        dve_st.done(dve.tensor_tensor(t, t, PS[:, 2 + m, :], ALU.mult), f"hid{m}")

            @block.scalar
            def _(act):
                silu.open(act)
                with act.Fori(0, F // UNIT) as g:
                    for m in range(2):
                        dve_st.wait(act, g, f"tap2_{m}")
                        silu.done(act.activation(tile(HID, g * 2 + m), ACC[:, m, :], ACT.Silu), f"tile{m}")


GU, GV_, Q_, KC_, VC_, KS_, VS_, KW_, VW_, NG_, CA_, CB_, SB_, SC_, SH_ = (
    0, 256, 512, 768, 896, 1024, 1152, 1280, 1408, 1536, 1548, 1804, 2060, 2316, 2572)
KV, D_HEAD, N_CMP = 2, 64, 31
FINAL, NORM1, NORM2, BGATE, SCONV, CONFB, CLNG, CLNB, QG, KG, PE_ = 0, 8, 16, 24, 56, 62, 64, 66, 68, 69, 72


def second_proj_stage(nc, PS, A, H, W, WNG, b):
    whole = lambda col: [(0, col, UNIT)]
    twice = lambda col: [(0, col, 64), (64, col, 64), (P, col + 64, 64), (P + 64, col + 64, 64)]
    units = [whole(GU), whole(GV_), [(0, Q_, 64), (64, Q_ + P, 64), (P, Q_ + 64, 64), (P + 64, Q_ + P + 64, 64)],
             twice(KC_), twice(VC_), whole(KS_), whole(KW_), whole(CB_), whole(CA_), whole(SC_), whole(SH_), whole(SB_)]
    landed = [16 * sum(len(units[v]) for v in range(u % 2, u + 1, 2)) for u in range(len(units))]

    products = ([(0, "act", f"gu{m}") for m in range(2)] + [(1, "act", f"gv{c}") for c in range(4)]
                + [(2, "dve", f"q{g}") for g in range(2)]
                + [(3, "dve", f"kc{h}") for h in range(2)] + [(4, "dve", f"vc{h}") for h in range(2)]
                + [(5, "dve", "ks"), (5, "dve", "vs"), (6, "dve", "kw"), (6, "dve", "vw")]
                + [(7, "act", f"cb{m}") for m in range(2)] + [(8, "dve", f"ca{m}") for m in range(2)]
                + [(9, "dve", f"sc{m}") for m in range(2)] + [(10, "dve", f"sh{m}") for m in range(2)]
                + [(11, "dve", f"sb{m}") for m in range(2)] + [(12, "act", "ng")])
    engine_of = {name: e for _, e, name in products}
    with stage(nc, "w0_in", "w1_in", "wng_in", "projected", "emptied_act", "emptied_dve") as (w0, w1, wng_in, proj_s, act_s, dve_s):
        w_loaded = (w0, w1)
        proj = Steps(proj_s, [name for _, _, name in products])
        out_st = {"act": Steps(act_s, [n for _, e, n in products if e == "act"]),
                  "dve": Steps(dve_s, [n for _, e, n in products if e == "dve"])}
        wl = k_tiles(A["w_in_2"][0])
        bank_of = {name: n % 8 for n, (_, _, name) in enumerate(products)}
        last_of_unit = {u: name for u, _, name in products}
        with nc.Block() as block:

            @block.sync
            def _(sp):
                for u, pieces in enumerate(units):
                    if u >= 2:
                        sp.wait_ge(proj.sem, proj.place[last_of_unit[u - 2]])
                    for at, col, n in pieces:
                        sp.dma_start(W[:, u % 2, :, at:at + n], wl[:, :, col:col + n]).then_inc(w_loaded[u % 2], 16)
                sp.dma_start(WNG[:, :, :], wl[:, :, NG_:NG_ + 12]).then_inc(wng_in, 16)

            @block.tensor
            def _(pe):
                for n, (u, _, name) in enumerate(products):
                    s = u % 2
                    if n == 0 or products[n - 1][0] != u:
                        if u == len(units):
                            pe.wait_ge(wng_in, 16)
                        else:
                            pe.wait_ge(w_loaded[s], landed[u])
                    if n >= 8:
                        before = products[n - 8][2]
                        st = out_st[engine_of[before]]
                        pe.wait_ge(st.sem, st.place[before])
                    bank = PS[:, bank_of[name], :]
                    tokens = lambda k, c: H[:, k, c * P:(c + 1) * P]
                    if name[:2] == "gv":
                        c = int(name[2])
                        last = contract(pe, bank[:, 0:UNIT], [(tokens(k, c), W[:, s, k, :]) for k in range(8)])
                    elif name in ("vs", "vw"):
                        for c in range(4):
                            last = contract(pe, bank[:, c * P:(c + 1) * P], [(tokens(k, c), W[:, s, k, P:2 * P]) for k in range(8)])
                    elif name == "ng":
                        for c in range(4):
                            last = contract(pe, bank[:, c * 12:(c + 1) * 12], [(tokens(k, c), WNG[:, k, :]) for k in range(8)])
                    else:
                        m = int(name[-1]) if name[-1].isdigit() else 0
                        last = contract(pe, bank, [(W[:, s, k, m * P:(m + 1) * P], H[:, k, :]) for k in range(8)])
                    proj.done(last, name)

            def source(e, name):
                e.wait_ge(proj.sem, proj.place[name])
                return PS[:, bank_of[name], :]

            @block.scalar
            def _(act):
                for name in out_st["act"].names:
                    ps = source(act, name)
                    n = int(name[2]) if len(name) == 3 else 0
                    if name[:2] == "gu":
                        ins = act.activation(b["GU"][:, n, :], ps, ACT.Gelu_apprx_tanh)
                    elif name[:2] == "gv":
                        ins = act.activation(b["GV"][:, n, :], ps[:, 0:UNIT], ACT.Gelu_apprx_tanh)
                    elif name[:2] == "cb":
                        ins = act.activation(b["CB"][:, n, :], ps, ACT.Sigmoid)
                    else:
                        ins = act.activation(b["NG"][:, :, :].rearrange("p c n -> p (c n)"), ps[:, 0:48], ACT.Sigmoid)
                    out_st["act"].done(ins, name)

            @block.vector
            def _(dve):
                st = out_st["dve"]
                dve.memset(b["ZP"][:, :, 0:30], 0.0)
                dve.memset(b["SP"][:, :, 0:2], 0.0)
                for name in st.names:
                    ps = source(dve, name)
                    n = int(name[-1]) if name[-1].isdigit() else 0
                    if name[0] == "q":
                        ins = dve.tensor_copy(b["Q"][:, n, :], ps)
                    elif name[:2] in ("kc", "vc"):
                        dst = b["KC"][:, 2 * (name[0] == "v") + n, :]
                        dve.tensor_copy(dst[0:64, :], ps[0:64, :])
                        ins = dve.tensor_copy(dst[64:P, 0:511], ps[64:P, 1:512])
                    elif name in ("ks", "kw"):
                        ins = dve.tensor_copy(b["K"][:, int(name == "kw"), :], ps)
                    elif name in ("vs", "vw"):
                        ins = dve.tensor_copy(b["V"][:, int(name == "vw"), :], ps)
                    elif name[:2] == "ca":
                        dve.wait_ge(out_st["act"].sem, out_st["act"].place[f"cb{n}"])
                        ins = dve.tensor_tensor(b["ZP"][:, n, 30:542], b["CB"][:, n, :], ps, ALU.mult)
                    elif name[:2] == "sc":
                        ins = dve.tensor_copy(b["SC"][:, n, :], ps)
                    elif name[:2] == "sh":
                        if n == 0:
                            dve.wait_ge(st.sem, st.place["sc1"])
                        ins = dve.tensor_tensor(b["SP"][:, n, 2:514], b["SC"][:, n, :], ps, ALU.mult)
                    else:
                        ins = dve.tensor_copy(b["SBB"][:, n, :], ps)
                    st.done(ins, name)


def gmlp_stage(nc, PS, C, A, b, Y, new):
    WS, WST, BS, LG, LNB = new("WS", [P, 4, P]), new("WST", [P, 4, P]), new("BS", [1, 512]), new("LG", [P, UNIT]), new("LNB", [P, UNIT])
    ST, SQ = new("STAT", [P, 4, 4]), new("GSQ", [P, 4, UNIT])
    GV = b["GV"]
    with stage(nc, "ws_in", "bs_in", "ln_in", "vector_steps", "squares", "root", "turned", "mixed") as (
            ws_in, bs_in, ln_in, dve_s, sq_s, root_s, turn_s, mix_s):
        st = Steps(dve_s, ["mask", "sum", "mean"] + [f"cent{c}" for c in range(4)] + ["var", "eps", "inv", "wst"]
                   + [f"{a}{c}" for c in range(4) for a in ("norm", "v")] + ["y0", "y1"])
        own = lambda dve, name: dve.wait_ge(st.sem, st.place[name])
        with nc.Block() as block:

            @block.sync
            def _(sp):
                sp.dma_start(WS[:, :, :], A["gmlp_ws_2"][0].rearrange("g t s -> t g s")).then_inc(ws_in, 16)
                sp.dma_start(BS[:, :], A["gmlp_bs_2"].rearrange("l g t -> l (g t)")).then_inc(bs_in, 16)
                sp.dma_start(LG[:, :], A["gmlp_ln_g_2"][0].partition_broadcast(P)).then_inc(ln_in, 16)
                sp.dma_start(LNB[:, :], A["gmlp_ln_b_2"][0].partition_broadcast(P)).then_inc(ln_in, 16)

            @block.vector
            def _(dve):
                dve.wait_ge(ws_in, 16)
                st.done(dve.tensor_tensor(WS[:, :, :], WS[:, :, :], heads(C[:, INCL + 1, :], 4), ALU.mult), "mask")
                st.done(dve.tensor_reduce(ST[:, 0, :], GV[:, :, :], AX, ALU.add), "sum")
                own(dve, "sum")
                st.done(dve.tensor_scalar(ST[:, 0, :], ST[:, 0, :], 1.0 / UNIT, None, ALU.mult), "mean")
                own(dve, "mean")
                for c in range(4):
                    st.done(dve.tensor_scalar(GV[:, c, :], GV[:, c, :], ST[:, 0, c:c + 1], None, ALU.subtract), f"cent{c}")
                dve.wait_ge(sq_s, 1)
                st.done(dve.tensor_reduce(ST[:, 1, :], SQ[:, :, :], AX, ALU.add), "var")
                own(dve, "var")
                st.done(dve.tensor_scalar(ST[:, 1, :], ST[:, 1, :], 1.0 / UNIT, 1e-5, ALU.mult, ALU.add), "eps")
                own(dve, "eps")
                st.done(dve.reciprocal(ST[:, 1, :], ST[:, 1, :]), "inv")
                dve.wait_ge(turn_s, 1)
                st.done(dve.tensor_copy(WST[:, :, :], per_head(PS[:, 0, :])), "wst")
                dve.wait_ge(root_s, 1)
                dve.wait_ge(ln_in, 32)
                for c in range(4):
                    st.done(dve.scalar_tensor_tensor(GV[:, c, :], GV[:, c, :], ST[:, 2, c:c + 1], LG[:, :], ALU.mult, ALU.mult), f"norm{c}")
                    own(dve, f"norm{c}")
                    st.done(dve.tensor_tensor(GV[:, c, :], GV[:, c, :], LNB[:, :], ALU.add), f"v{c}")
                for m in range(2):
                    dve.wait_ge(mix_s, m + 1)
                    st.done(dve.tensor_tensor(Y[:, m, :], b["GU"][:, m, :], PS[:, 1 + m, :], ALU.mult), f"y{m}")

            @block.scalar
            def _(act):
                own(act, "cent3")
                act.activation(SQ[:, :, :], GV[:, :, :], ACT.Square).then_inc(sq_s, 1)
                own(act, "inv")
                act.activation(ST[:, 2, :], ST[:, 1, :], ACT.Sqrt).then_inc(root_s, 1)

            @block.tensor
            def _(pe):
                own(pe, "mask")
                for g in range(4):
                    last = pe.transpose(PS[:, 0, g * P:(g + 1) * P], WS[:, g, :], C[:, IDENT, :])
                last.then_inc(turn_s, 1)
                pe.wait_ge(bs_in, 16)
                own(pe, "v3")
                for m in range(2):
                    for half in range(2):
                        g = 2 * m + half
                        rows = slice(64 * half, 64 * half + 64)
                        for n in range(4):
                            last = contract(pe, PS[rows, 1 + m, n * P:(n + 1) * P],
                                            [(GV[:, n, g * 64:(g + 1) * 64], WST[:, g, :]),
                                             (C[0:1, ONES, 0:64], BS[0:1, g * P:(g + 1) * P])])
                    last.then_inc(mix_s, 1)


def conv_branches_stage(nc, PS, C, PAR, b, Y, RS):
    taps = 31
    ZP, SP = b["ZP"], b["SP"]
    par, conv = PAR[:, 0, :], PAR[:, 1, :]
    names = [f"z{t}_{m}" for t in range(taps) for m in range(2)] + [f"s{t}_{m}" for t in range(3) for m in range(2)]
    names += ["d0", "d1", "zc0", "zc1", "mean", "cent0", "cent1", "eps", "inv", "norm0", "norm1"]
    with stage(nc, "vector_steps", "sum_done", "squares", "sum_sq", "root", "out") as (dve_s, sum_s, sq_s, sumsq_s, root_s, out_s):
        st = Steps(dve_s, names)
        own = lambda e, name: e.wait_ge(st.sem, st.place[name])
        with nc.Block() as block:

            @block.vector
            def _(dve):
                acc = lambda m: PS[:, m, :]
                for t in range(taps):
                    for m in range(2):
                        src, w = ZP[:, m, t:t + 512], conv[:, t * 2 + m:t * 2 + m + 1]
                        if t == 0:
                            ins = dve.tensor_scalar(acc(m), src, w, par[:, CONFB + m:CONFB + m + 1], ALU.mult, ALU.add)
                        else:
                            own(dve, f"z{t - 1}_{m}")
                            ins = dve.scalar_tensor_tensor(acc(m), src, w, acc(m), ALU.mult, ALU.add)
                        st.done(ins, f"z{t}_{m}")
                for t in range(3):
                    for m in range(2):
                        src, w, a = SP[:, m, t:t + 512], par[:, SCONV + t * 2 + m:SCONV + t * 2 + m + 1], PS[:, 2 + m, :]
                        if t == 0:
                            ins = dve.tensor_scalar(a, src, w, None, ALU.mult)
                        else:
                            own(dve, f"s{t - 1}_{m}")
                            ins = dve.scalar_tensor_tensor(a, src, w, a, ALU.mult, ALU.add)
                        st.done(ins, f"s{t}_{m}")
                for m in range(2):
                    own(dve, f"s2_{m}")
                    st.done(dve.tensor_tensor(Y[:, 6 + m, :], b["SBB"][:, m, :], PS[:, 2 + m, :], ALU.mult), f"d{m}")
                for m in range(2):
                    own(dve, f"z{taps - 1}_{m}")
                    st.done(dve.tensor_copy(Y[:, 4 + m, :], acc(m)), f"zc{m}")
                dve.wait_ge(sum_s, 1)
                st.done(dve.tensor_scalar(RS[:, 0, :], PS[:, 4, :], 1.0 / UNIT, None, ALU.mult), "mean")
                own(dve, "mean")
                for m in range(2):
                    st.done(dve.tensor_tensor(Y[:, 4 + m, :], Y[:, 4 + m, :], RS[:, 0, :], ALU.subtract), f"cent{m}")
                dve.wait_ge(sumsq_s, 1)
                st.done(dve.tensor_scalar(RS[:, 1, :], PS[:, 5, :], 1.0 / UNIT, 1e-5, ALU.mult, ALU.add), "eps")
                own(dve, "eps")
                st.done(dve.reciprocal(RS[:, 1, :], RS[:, 1, :]), "inv")
                dve.wait_ge(root_s, 1)
                for m in range(2):
                    st.done(dve.scalar_tensor_tensor(Y[:, 4 + m, :], Y[:, 4 + m, :], par[:, CLNG + m:CLNG + m + 1], RS[:, 1, :], ALU.mult, ALU.mult), f"norm{m}")

            @block.scalar
            def _(act):
                for m in range(2):
                    own(act, f"cent{m}")
                    act.activation(ZP[:, m, 0:512], Y[:, 4 + m, :], ACT.Square).then_inc(sq_s, 1)
                own(act, "inv")
                act.activation(RS[:, 1, :], RS[:, 1, :], ACT.Sqrt).then_inc(root_s, 1)
                for m in range(2):
                    own(act, f"norm{m}")
                    act.activation(Y[:, 4 + m, :], Y[:, 4 + m, :], ACT.Silu, bias=par[:, CLNB + m:CLNB + m + 1]).then_inc(out_s, 1)

            @block.tensor
            def _(pe):
                own(pe, "zc1")
                contract(pe, PS[:, 4, :], [(C[:, ONES, :], Y[:, 4 + m, :]) for m in range(2)]).then_inc(sum_s, 1)
                pe.wait_ge(sq_s, 2)
                contract(pe, PS[:, 5, :], [(C[:, ONES, :], ZP[:, m, 0:512]) for m in range(2)]).then_inc(sumsq_s, 1)


def nsa_prep_stage(nc, PS, C, A, PAR, b, new):
    W1, W2 = new("W1", [P, 2, 16, P]), new("W2", [P, 2, D_HEAD])
    CW, HC = new("CW", [P, 2, 16, 2 * N_CMP]), new("HC", [P, 2, 2 * N_CMP])
    SQ, RI = new("NSQ", [P, 4, 512]), new("NRI", [P, 4, 512])
    KCM, KSQ, KRI = new("KCM0", [P, N_CMP]), new("KSQ", [P, N_CMP]), new("KRI", [P, N_CMP])
    par = PAR[:, 0, :]
    tiles = [(b["Q"][:, 0, :], QG), (b["Q"][:, 1, :], QG), (b["K"][:, 0, :], KG + 1), (b["K"][:, 1, :], KG + 2)]
    vnames = ([f"cw{t}_{j}" for t in range(2) for j in range(16)]
              + [f"{a}{n}" for n in range(4) for a in ("mean", "inv")] + [f"norm{n}" for n in range(4)]
              + ["kc", "vc", "kmean", "kinv", "knorm"])
    with stage(nc, "w1k_in", "w1v_in", "w2_in", "vector_steps", "scalar_steps", "tensor_steps") as (w1k, w1v, w2_in, dve_s, act_s, pe_s):
        dve_st = Steps(dve_s, vnames)
        act_st = Steps(act_s, [f"sq{n}" for n in range(4)] + ["gelu0", "gelu1"] + [f"root{n}" for n in range(4)] + ["ksq", "kroot"])
        pe_st = Steps(pe_s, [f"sum{n}" for n in range(4)] + ["hid0", "hid1", "kc", "vc", "ksum"])
        own = lambda e, st, name: e.wait_ge(st.sem, st.place[name])
        with nc.Block() as block:

            @block.sync
            def _(sp):
                for t, s in enumerate((w1k, w1v)):
                    sp.dma_start(W1[:, t], k_tiles(A["nsa_cmp_w1_2"][0][t])).then_inc(s, 16)
                sp.dma_start(W2[:, :, :], A["nsa_cmp_w2_2"][0].rearrange("t e d -> e t d")).then_inc(w2_in, 16)

            @block.scalar
            def _(act):
                for n, (x, _) in enumerate(tiles):
                    act_st.done(act.activation(SQ[:, n, :], x, ACT.Square), f"sq{n}")
                for t in range(2):
                    own(act, pe_st, f"hid{t}")
                    act_st.done(act.activation(HC[:, t, :], PS[:, 4 + t, 0:2 * N_CMP], ACT.Gelu_apprx_tanh), f"gelu{t}")
                for n in range(4):
                    own(act, dve_st, f"inv{n}")
                    act_st.done(act.activation(RI[:, n, :], RI[:, n, :], ACT.Sqrt), f"root{n}")
                own(act, dve_st, "kc")
                act_st.done(act.activation(KSQ[:, :], KCM[:, :], ACT.Square), "ksq")
                own(act, dve_st, "kinv")
                act_st.done(act.activation(KRI[:, :], KRI[:, :], ACT.Sqrt), "kroot")

            @block.tensor
            def _(pe):
                for n in range(4):
                    own(pe, act_st, f"sq{n}")
                    pe_st.done(pe.matmul(PS[:, n, :], C[:, BLOCK64, :], SQ[:, n, :], start=True, stop=True), f"sum{n}")
                for t, s in enumerate((w1k, w1v)):
                    pe.wait_ge(s, 16)
                    own(pe, dve_st, f"cw{t}_15")
                    pe_st.done(contract(pe, PS[:, 4 + t, 0:2 * N_CMP], [(W1[:, t, j, :], CW[:, t, j, :]) for j in range(16)]), f"hid{t}")
                pe.wait_ge(w2_in, 16)
                own(pe, act_st, "gelu0")
                for h in range(KV):
                    last = pe.matmul(PS[64 * h:64 * h + 64, 6, 0:N_CMP], W2[:, 0, :], HC[:, 0, h * N_CMP:(h + 1) * N_CMP], start=True, stop=True)
                pe_st.done(last, "kc")
                own(pe, act_st, "gelu1")
                for h in range(KV):
                    last = pe.matmul(PS[0:N_CMP, 7, h * D_HEAD:(h + 1) * D_HEAD], HC[:, 1, h * N_CMP:(h + 1) * N_CMP], W2[:, 1, :], start=True, stop=True)
                pe_st.done(last, "vc")
                own(pe, act_st, "ksq")
                pe_st.done(pe.matmul(PS[:, 4, 0:N_CMP], C[:, BLOCK64, :], KSQ[:, :], start=True, stop=True), "ksum")

            @block.vector
            def _(dve):
                for t in range(2):
                    for j in range(16):
                        src = b["KC"][:, 2 * t:2 * t + 2, 2 * j:2 * j + 16 * (N_CMP - 1) + 1:16]
                        dst = CW[:, t, j, :].rearrange("p (h n) -> p h n", h=KV)
                        dve_st.done(dve.tensor_scalar(dst, src, par[:, PE_ + 16 * t + j:PE_ + 16 * t + j + 1], None, ALU.add), f"cw{t}_{j}")
                for n in range(4):
                    own(dve, pe_st, f"sum{n}")
                    dve_st.done(dve.tensor_scalar(RI[:, n, :], PS[:, n, :], 1.0 / D_HEAD, 1e-6, ALU.mult, ALU.add), f"mean{n}")
                    own(dve, dve_st, f"mean{n}")
                    dve_st.done(dve.reciprocal(RI[:, n, :], RI[:, n, :]), f"inv{n}")
                for n, (x, g) in enumerate(tiles):
                    own(dve, act_st, f"root{n}")
                    dve_st.done(dve.scalar_tensor_tensor(x, x, par[:, g:g + 1], RI[:, n, :], ALU.mult, ALU.mult), f"norm{n}")
                own(dve, pe_st, "kc")
                dve_st.done(dve.tensor_copy(KCM[:, :], PS[:, 6, 0:N_CMP]), "kc")
                own(dve, pe_st, "vc")
                dve_st.done(dve.tensor_copy(b["VCM"][0:N_CMP, :], PS[0:N_CMP, 7, 0:P]), "vc")
                own(dve, pe_st, "ksum")
                dve_st.done(dve.tensor_scalar(KRI[:, :], PS[:, 4, 0:N_CMP], 1.0 / D_HEAD, 1e-6, ALU.mult, ALU.add), "kmean")
                own(dve, dve_st, "kmean")
                dve_st.done(dve.reciprocal(KRI[:, :], KRI[:, :]), "kinv")
                own(dve, act_st, "kroot")
                dve_st.done(dve.scalar_tensor_tensor(b["KCM"][:, :], KCM[:, :], par[:, KG:KG + 1], KRI[:, :], ALU.mult, ALU.mult), "knorm")


def attention_stage(nc, PS, C, b, Y, new):
    H4 = 4
    scale = D_HEAD ** -0.5
    PR, PT = [new(f"PR{n}", [P, H4, 512]) for n in range(2)], [new(f"PT{n}", [P, 512]) for n in range(2)]
    MX, SU, CO = new("MX", [P, 2, H4]), new("SU", [P, 2, H4]), new("CO", [P, 2, H4])
    OA = new("OA", [P, 2, H4 * D_HEAD])
    items = [(c, br) for c in range(4) for br in range(3)]
    keys = lambda c, br: N_CMP if br == 0 else P * (c + 1)
    blocks = lambda c, br: 1 if br == 0 else c + 1
    pnames, anames, vnames = [], [], []
    for i, (c, br) in enumerate(items):
        anames += [f"exp{i}_{h}" for h in range(H4)]
        vnames += [f"mask{i}", f"max{i}", f"neg{i}"] + ([f"valid{i}"] if br == 0 else []) + [f"pt{i}_{h}" for h in range(H4)]
        vnames += [f"inv{i}", f"coef{i}"] + [f"out{i}_{h}" for h in range(H4)]
    order = ["s0"]
    for i, (c, br) in enumerate(items):
        for h in range(H4):
            order.append(f"t{i}_{h}")
            if h:
                order.append(f"o{i}_{h - 1}")
            if h == H4 - 1 and i + 1 < len(items):
                order.append(f"s{i + 1}")
        order.append(f"o{i}_{H4 - 1}")
        if br == 2 :
            order.append(f"y{c}")
    with stage(nc, "tensor_steps", "scalar_steps", "vector_steps", "y_kept") as (pe_s, act_s, dve_s, y_s):
        pe_st, act_st, dve_st = Steps(pe_s, order), Steps(act_s, anames), Steps(dve_s, vnames)
        own = lambda e, st, name: e.wait_ge(st.sem, st.place[name])

        def scores_of(i):
            c, br = items[i]
            return PS[:, 0:H4, 0:keys(c, br)]

        with nc.Block() as block:

            @block.tensor
            def _(pe):
                def scores(i):
                    c, br = items[i]
                    if i:
                        own(pe, act_st, f"exp{i - 1}_{H4 - 1}")
                    for hh in range(H4):
                        h, g = divmod(hh, 2)
                        rows = slice(64 * h, 64 * h + 64)
                        q = b["Q"][rows, g, c * P:(c + 1) * P]
                        k = b["KCM"][rows, :] if br == 0 else b["K"][rows, br - 1, 0:keys(c, br)]
                        last = pe.matmul(scores_of(i)[:, hh, :], q, k, start=True, stop=True)
                    pe_st.done(last, f"s{i}")

                def turn(i, hh):
                    c, br = items[i]
                    own(pe, dve_st, f"valid{i}") if br == 0 else own(pe, act_st, f"exp{i}_{hh}")
                    n = i * H4 + hh
                    if n >= 2:
                        j, k = divmod(n - 2, H4)
                        own(pe, dve_st, f"pt{j}_{k}")
                    for j in range(blocks(c, br)):
                        w = min(P, keys(c, br))
                        last = pe.transpose(PS[0:w, 4 + hh % 2, j * P:(j + 1) * P], PR[i % 2][:, hh, j * P:j * P + w], C[:, IDENT, :])
                    pe_st.done(last, f"t{i}_{hh}")

                def output(i, hh):
                    c, br = items[i]
                    h = hh // 2
                    own(pe, dve_st, f"pt{i}_{hh}")
                    w = min(P, keys(c, br))
                    v = lambda j: b["VCM"][0:w, h * 64:(h + 1) * 64] if br == 0 else b["V"][:, br - 1, j * P + h * 64:j * P + (h + 1) * 64]
                    pe_st.done(contract(pe, PS[:, 6, hh * 64:(hh + 1) * 64],
                                        [(PT[hh % 2][0:w, j * P:(j + 1) * P], v(j)) for j in range(blocks(c, br))]), f"o{i}_{hh}")

                scores(0)
                for i, (c, br) in enumerate(items):
                    for hh in range(H4):
                        turn(i, hh)
                        if hh == 1 and i:
                            own(pe, dve_st, f"out{i - 1}_{H4 - 1}")
                        if hh:
                            output(i, hh - 1)
                        if hh == H4 - 1 and i + 1 < len(items):
                            scores(i + 1)
                    output(i, H4 - 1)
                    if br == 2:
                        own(pe, dve_st, f"out{i}_{H4 - 1}")
                        if c:
                            pe.wait_ge(y_s, c)
                        for m in range(2):
                            last = pe.transpose(PS[:, 7, m * P:(m + 1) * P], OA[:, c % 2, m * P:(m + 1) * P], C[:, IDENT, :])
                        pe_st.done(last, f"y{c}")

            @block.scalar
            def _(act):
                for i, (c, br) in enumerate(items):
                    own(act, dve_st, f"neg{i}")
                    if i >= 2:
                        own(act, pe_st, f"t{i - 2}_{H4 - 1}")
                    for hh in range(H4):
                        act_st.done(act.activation(PR[i % 2][:, hh, 0:keys(c, br)], scores_of(i)[:, hh, :], ACT.Exp, scale=scale,
                                                   bias=MX[:, i % 2, hh:hh + 1], accum_out=SU[:, i % 2, hh:hh + 1]), f"exp{i}_{hh}")
                    if br == 2:
                        act.wait_ge(pe_st.sem, pe_st.place[f"y{c}"])
                        act.copy(Y[:, 2:4, c * P:(c + 1) * P], PS[:, 7, 0:2 * P].rearrange("p (m n) -> p m n", m=2)).then_inc(y_s, 1)

            @block.vector
            def _(dve):
                for i, (c, br) in enumerate(items):
                    own(dve, pe_st, f"s{i}")
                    s = scores_of(i)
                    if br == 0:
                        part, mask = s, C[:, CMP_ADD, c * 32:c * 32 + N_CMP]
                    else:
                        part, mask = s[:, :, c * P:(c + 1) * P], C[:, CAUSAL, :]
                    dve_st.done(dve.tensor_tensor(part, part, heads(mask, H4), ALU.add), f"mask{i}")
                    own(dve, dve_st, f"mask{i}")
                    dve_st.done(dve.tensor_reduce(MX[:, i % 2, :], s, AX, ALU.max), f"max{i}")
                    own(dve, dve_st, f"max{i}")
                    dve_st.done(dve.tensor_scalar(MX[:, i % 2, :], MX[:, i % 2, :], -scale, None, ALU.mult), f"neg{i}")
                    if br == 0:
                        own(dve, act_st, f"exp{i}_{H4 - 1}")
                        pr = PR[i % 2][:, :, 0:N_CMP]
                        dve_st.done(dve.tensor_tensor(pr, pr, heads(C[:, CMP_OK, c * 32:c * 32 + N_CMP], H4), ALU.mult), f"valid{i}")
                    for hh in range(H4):
                        own(dve, pe_st, f"t{i}_{hh}")
                        w = min(P, keys(c, br))
                        n = blocks(c, br) * P
                        dve_st.done(dve.tensor_copy(PT[hh % 2][0:w, 0:n], PS[0:w, 4 + hh % 2, 0:n]), f"pt{i}_{hh}")
                    dve_st.done(dve.reciprocal(CO[:, i % 2, :], SU[:, i % 2, :]), f"inv{i}")
                    own(dve, dve_st, f"inv{i}")
                    gate = b["NG"][:, c, :].rearrange("p (h r) -> p h r", r=3)[:, :, br]
                    dve_st.done(dve.tensor_tensor(CO[:, i % 2, :], CO[:, i % 2, :], gate, ALU.mult), f"coef{i}")
                    own(dve, dve_st, f"coef{i}")
                    own(dve, pe_st, f"o{i}_{H4 - 1}")
                    for hh in range(H4):
                        o, ps, co = OA[:, c % 2, hh * 64:(hh + 1) * 64], PS[:, 6, hh * 64:(hh + 1) * 64], CO[:, i % 2, hh:hh + 1]
                        if br == 0:
                            ins = dve.tensor_scalar(o, ps, co, None, ALU.mult)
                        else:
                            ins = dve.scalar_tensor_tensor(o, ps, co, o, ALU.mult, ALU.add)
                        dve_st.done(ins, f"out{i}_{hh}")


def gate_stage(nc, PS, A, H, PAR, Y, M, WG, WB, SG, TMP):
    D = M.shape[1] * P
    js = [(n, m) for n in range(4) for m in range(2)]
    with stage(nc, "wg0_in", "wg1_in", "wb0_in", "wb1_in", "projected", "sigmoid_done", "vector_steps") as (
            g0, g1, b0, b1, proj_s, sig_s, dve_s):
        gate_in, branch_in = (g0, g1), (b0, b1)
        proj = Steps(proj_s, [f"{a}{n}_{m}" for n, m in js for a in "gb"])
        sig = Steps(sig_s, [f"{n}_{m}" for n, m in js])
        dve_st = Steps(dve_s, [x for n, m in js for x in ([f"m{n}_{m}"] if n == 0 else [f"m{n}_{m}", f"s{n}_{m}"])])
        gl = k_tiles(A["w_gate_2"][0])
        with nc.Block() as block:

            @block.sync
            def _(sp):
                with sp.Fori(0, D // UNIT) as g:
                    for n in range(4):
                        r = n % 2
                        if n >= 2:
                            proj.wait(sp, g, f"b{n - 2}_1")
                        else:
                            proj.wait_before(sp, g, f"b{n + 2}_1")
                        sp.dma_start(WG[:, r], gl[:, :, ds(g * UNIT + n * D, UNIT)]).then_inc(gate_in[r], 16)
                        sp.dma_start(WB[:, r, 0:2], k_tiles(A["w_branch_2"][0][n])[:, :, ds(g * UNIT, UNIT)]).then_inc(branch_in[r], 16)

            @block.tensor
            def _(pe):
                proj.open(pe)
                with pe.Fori(0, D // UNIT) as g:
                    for n, m in js:
                        r = n % 2
                        j = 2 * r + m
                        if m == 0:
                            pe.wait_ge(gate_in[r], 16 * (g * 2 + (n // 2 + 1)))
                        if n >= 2:
                            sig.wait(pe, g, f"{n - 2}_{m}")
                        else:
                            sig.wait_before(pe, g, f"{n + 2}_{m}")
                        last = contract(pe, PS[:, j, :], [(WG[:, r, k, m * P:(m + 1) * P], H[:, k, :]) for k in range(8)])
                        proj.done(last, f"g{n}_{m}")
                        if m == 0:
                            pe.wait_ge(branch_in[r], 16 * (g * 2 + (n // 2 + 1)))
                        if n >= 2:
                            dve_st.wait(pe, g, f"m{n - 2}_{m}")
                        else:
                            dve_st.wait_before(pe, g, f"m{n + 2}_{m}")
                        last = contract(pe, PS[:, 4 + j, :], [(WB[:, r, k, m * P:(m + 1) * P], Y[:, 2 * n + k, :]) for k in range(2)])
                        proj.done(last, f"b{n}_{m}")

            @block.scalar
            def _(act):
                sig.open(act)
                with act.Fori(0, D // UNIT) as g:
                    for n, m in js:
                        j = 2 * (n % 2) + m
                        proj.wait(act, g, f"g{n}_{m}")
                        if n >= 2:
                            dve_st.wait(act, g, f"m{n - 2}_{m}")
                        else:
                            dve_st.wait_before(act, g, f"m{n + 2}_{m}")
                        bias = PAR[:, 0, ds(g * 2 + (BGATE + n * 8 + m), 1)]
                        sig.done(act.activation(SG[:, j, :], PS[:, j, :], ACT.Sigmoid, bias=bias), f"{n}_{m}")

            @block.vector
            def _(dve):
                dve_st.open(dve)
                with dve.Fori(0, D // UNIT) as g:
                    for n, m in js:
                        j = 2 * (n % 2) + m
                        sig.wait(dve, g, f"{n}_{m}")
                        proj.wait(dve, g, f"b{n}_{m}")
                        dst = tile(M, g * 2 + m)
                        if n == 0:
                            dve_st.done(dve.tensor_tensor(dst, SG[:, j, :], PS[:, 4 + j, :], ALU.mult), f"m{n}_{m}")
                        else:
                            dve_st.done(dve.tensor_tensor(TMP[:, m, :], SG[:, j, :], PS[:, 4 + j, :], ALU.mult), f"m{n}_{m}")
                            dve_st.wait(dve, g, f"m{n}_{m}")
                            dve_st.done(dve.tensor_tensor(dst, dst, TMP[:, m, :], ALU.add), f"s{n}_{m}")


def mlp_up_stage(nc, PS, A, H, HID, W):
    T = HID.shape[1]
    with stage(nc, "w0_in", "w1_in", "projected", "relu_done", "squared") as (w0, w1, proj_s, relu_s, sq_s):
        w_loaded = (w0, w1)
        names = [f"tile{j}" for j in range(4)]
        proj, relu, sq = Steps(proj_s, names), Steps(relu_s, names), Steps(sq_s, names)
        wl = k_tiles(A["w_mlp1_2"][0])
        with nc.Block() as block:

            @block.sync
            def _(sp):
                with sp.Fori(0, T // 4) as g:
                    for s in range(2):
                        proj.wait_before(sp, g, f"tile{2 * s + 1}")
                        sp.dma_start(W[:, s], wl[:, :, ds(g * 2 * UNIT + s * UNIT, UNIT)]).then_inc(w_loaded[s], 16)

            @block.tensor
            def _(pe):
                proj.open(pe)
                with pe.Fori(0, T // 4) as g:
                    for j in range(4):
                        s, m = divmod(j, 2)
                        if m == 0:
                            pe.wait_ge(w_loaded[s], 16 * (g + 1))
                        relu.wait_before(pe, g, f"tile{j}")
                        last = contract(pe, PS[:, j, :], [(W[:, s, k, m * P:(m + 1) * P], H[:, k, :]) for k in range(8)])
                        proj.done(last, f"tile{j}")

            @block.vector
            def _(dve):
                relu.open(dve)
                with dve.Fori(0, T // 4) as g:
                    for j in range(4):
                        proj.wait(dve, g, f"tile{j}")
                        relu.done(dve.tensor_scalar(tile(HID, g * 4 + j), PS[:, j, :], 0.0, None, ALU.max), f"tile{j}")

            @block.scalar
            def _(act):
                with act.Fori(0, T // 4) as g:
                    for j in range(4):
                        relu.wait(act, g, f"tile{j}")
                        t = tile(HID, g * 4 + j)
                        sq.done(act.activation(t, t, ACT.Square), f"tile{j}")


def store_stage(nc, PS, C, X, H, out):
    S = X.shape[2]
    D = out.shape[1]
    T, K = S // P, D // P
    with stage(nc, "turned", "kept", "written") as (turned, kept, written):
        rows = H[:, :, :].rearrange("p k n -> p (k n)").rearrange("p (c f) -> p c f", c=T)
        with nc.Block() as block:

            @block.tensor
            def _(pe):
                for c in range(T):
                    for half in range(2):
                        for k in range(4):
                            last = pe.transpose(PS[:, 2 * c + half, k * P:(k + 1) * P], X[:, 4 * half + k, c * P:(c + 1) * P], C[:, IDENT, :])
                        last.then_inc(turned, 1)

            @block.vector
            def _(dve):
                for c in range(T):
                    for half in range(2):
                        dve.wait_ge(turned, 2 * c + half + 1)
                        dve.tensor_copy(rows[:, c, half * 512:(half + 1) * 512], PS[:, 2 * c + half, :]).then_inc(kept, 1)

            @block.sync
            def _(sp):
                for c in range(T):
                    sp.wait_ge(kept, 2 * c + 2)
                    sp.dma_start(out[c * P:(c + 1) * P, :], rows[:, c, :]).then_inc(written, 16)
                sp.wait_ge(written, 16 * T)


def second_block(nc, PS, C, A, X, H, PAR, ROWS, RS, new_in, dump, out):
    flat = lambda t: t[:, :, :].rearrange("p a n -> p (a n)")
    vec = lambda n: A[n].rearrange("l (m p) -> (l m) p", p=P)
    loads = [(FINAL, A["final_norm"].rearrange("(m p) -> m p", p=P)), (NORM1, vec("norm1_g_2")), (NORM2, vec("norm2_g_2")),
             (BGATE, vec("b_gate_2")), (SCONV, A["sconv_w_2"][0].rearrange("t (m p) -> (t m) p", p=P)),
             (CONFB, vec("conf_conv_b_2")), (CLNG, vec("conf_ln_g_2")), (CLNB, vec("conf_ln_b_2")),
             (PE_, A["nsa_cmp_pe_2"][0].rearrange("t (j a) d -> (t j) (a d)", a=2)),
             (P, A["conf_conv_w_2"][0].rearrange("t (m p) -> (t m) p", p=P))]
    extra = []
    for half in range(2):
        cols = slice(64 * half, 64 * half + 64)
        extra += [(ROWS[QG:QG + 1, 0, cols], A["nsa_q_norm_g_2"]), (ROWS[KG:KG + 3, 0, cols], A["nsa_k_norm_g_2"][0])]
    params_stage(nc, PS, C, ROWS, PAR, loads, 2, extra)
    par = PAR[:, 0, :]
    rms_stage(nc, PS, C, X, X, par[:, FINAL:FINAL + 8], H, RS[:, 0, :], 1e-6)
    rms_stage(nc, PS, C, X, H, par[:, NORM1:NORM1 + 8], H, RS[:, 0, :], 1e-6)
    dump("xn", flat(H))
    with ExitStack() as mid:
        new = new_in(mid)
        Y = new("Y", [P, 8, 512])
        with ExitStack() as br:
            new = new_in(br)
            b = {n: new(n, s) for n, s in dict(
                GU=[P, 2, 512], GV=[P, 4, UNIT], Q=[P, 2, 512], KC=[P, 4, 512], K=[P, 2, 512], V=[P, 2, 512], CB=[P, 2, 512],
                ZP=[P, 2, 542], SC=[P, 2, 512], SP=[P, 2, 514], SBB=[P, 2, 512], NG=[P, 4, 12], KCM=[P, N_CMP], VCM=[P, P]).items()}
            with ExitStack() as w:
                new = new_in(w)
                second_proj_stage(nc, PS, A, H, new("W", [P, 2, 8, UNIT]), new("WNG", [P, 8, 12]), b)
            with ExitStack() as w:
                gmlp_stage(nc, PS, C, A, b, Y, new_in(w))
            conv_branches_stage(nc, PS, C, PAR, b, Y, RS)
            with ExitStack() as w:
                nsa_prep_stage(nc, PS, C, A, PAR, b, new_in(w))
            with ExitStack() as w:
                attention_stage(nc, PS, C, b, Y, new_in(w))
        dump("y", flat(Y))
        M = new_in(mid)("M", [P, 8, 512])
        with ExitStack() as w:
            new = new_in(w)
            gate_stage(nc, PS, A, H, PAR, Y, M, new("WG", [P, 2, 8, UNIT]), new("WB", [P, 2, 4, UNIT]), new("SG", [P, 4, 512]), new("TMP", [P, 2, 512]))
        dump("mixed", flat(M))
        with ExitStack() as w:
            slab_stage(nc, PS, A["w_out_2"][0], M, X, new_in(w)("SLAB", [P, 4, 1024]))
    dump("x1", flat(X))
    rms_stage(nc, PS, C, X, H, par[:, NORM2:NORM2 + 8], H, RS[:, 0, :], 1e-6)
    with ExitStack() as ffn:
        new = new_in(ffn)
        HID = new("HID", [P, 32, 512])
        with ExitStack() as w:
            mlp_up_stage(nc, PS, A, H, HID, new_in(w)("W", [P, 2, 8, UNIT]))
        with ExitStack() as w:
            slab_stage(nc, PS, A["w_mlp2_2"][0], HID, X, new_in(w)("SLAB", [P, 4, 1024]))
    store_stage(nc, PS, C, X, H, out)


def params_stage(nc, PS, C, ROWS, PAR, loads, n_tiles, extra=()):
    with stage(nc, "cleared", "rows_in", "turned", "kept") as (cleared, rows_in, turned, kept):
        with nc.Block() as block:

            @block.sync
            def _(sp):
                sp.wait_ge(cleared, 1)
                for at, src in loads:
                    n = src.shape[0]
                    sp.dma_start(ROWS[at % P:at % P + n, at // P, :], src).then_inc(rows_in, 16)
                for dst, src in extra:
                    sp.dma_start(dst, src).then_inc(rows_in, 16)
                sp.wait_ge(rows_in, 16 * (len(loads) + len(extra)))

            @block.tensor
            def _(pe):
                pe.wait_ge(rows_in, 16 * (len(loads) + len(extra)))
                for n in range(n_tiles):
                    pe.transpose(PS[:, n, 0:P], ROWS[:, n, :], C[:, IDENT, :]).then_inc(turned, 1)

            @block.vector
            def _(dve):
                dve.memset(ROWS[:, :, :], 0.0).then_inc(cleared, 1)
                dve.wait_ge(turned, n_tiles)
                dve.tensor_copy(PAR[:, :, :], PS[:, 0:n_tiles, 0:P]).then_inc(kept, 1)


def at_layer(ap, l):
    axes = " ".join(f"d{n}" for n in range(1, len(ap.shape)))
    first, rest = axes.split(" ", 1) if " " in axes else (axes, "")
    return ap[ds(l, 1)].rearrange(f"l {axes} -> (l {first}) {rest}")


def build(nc, A, out, dumps=None):
    S, D = A["x"].shape[1:]
    K = D // P
    with ExitStack() as top:
        named = {}

        def new_in(ctx):
            def new(name, shape, dt=F32):
                named[name] = named.get(name, 0) + 1
                return ctx.enter_context(nc.sbuf_tensor(f"{name}_{named[name]}", shape, dt))
            return new

        new = new_in(top)
        PS = top.enter_context(nc.psum_tensor("PS", [P, 8, 512], F32))
        C = new("C", [P, N_CONST, P])
        X = new("X", [P, K, S])
        H = new("H", [P, K, S])
        PAR = new("PAR", [P, 2, P])
        ROWS = new("ROWS", [P, 2, P])
        SMALL = new("SMALL", [P, 32])
        RS = new("RS", [P, 2, S])

        def dump(name, ap, l=None):
            if name in (dumps or {}):
                with stage(nc, "dump") as (s,):
                    with nc.Block() as block:
                        @block.sync
                        def _(sp):
                            dst = dumps[name] if l is None else dumps[name][ds(l, 1)].rearrange("l p n -> (l p) n")
                            sp.dma_start(dst, ap).then_inc(s, 16)
                            sp.wait_ge(s, 16)

        with stage(nc, "consts_in") as (consts_in,):
            with nc.Block() as block:

                @block.sync
                def _(sp):
                    sp.dma_start(C[:, :, :], A["consts"]).then_inc(consts_in, 16)
                    sp.wait_ge(consts_in, 16)

        load_norm_stage(nc, PS, C, A["x"].rearrange("b s d -> (b s) d"), X, H)
        mixer_layers(nc, PS, C, A, X, H, PAR, ROWS, SMALL, RS, new_in, dump)
        second_block(nc, PS, C, A, X, H, PAR, ROWS, RS, new_in, dump, out.rearrange("b s d -> (b s) d"))


MIX, FFN, DNN, HGN, BIAS = 60, 68, 76, 77, 66


def mixer_layers(nc, PS, C, A, X, H, PAR, ROWS, SMALL, RS, new_in, dump):
    flat = lambda t: t[:, :, :].rearrange("p a n -> p (a n)")
    with nc.Fori(0, A["w_in"].shape[0]) as l:
        conv = at_layer(A["dn_conv"], l).rearrange("j (m p) -> (j m) p", p=P)
        fconv = at_layer(A["ffn_conv"], l).rearrange("j (m p) -> (j m) p", p=P)
        row = lambda n: A[n][ds(l, 1)].rearrange("l (m p) -> (l m) p", p=P)
        bc = lambda n: A[n][ds(l, 1)].rearrange("l a b -> l (a b)").rearrange("l n -> (l n)").partition_broadcast(P)
        params_stage(nc, PS, C, ROWS, PAR,
                     [(0, conv), (MIX, row("mix_norm")), (FFN, row("ffn_norm")), (DNN, row("dn_norm")), (HGN, row("hg_norm")),
                      (P, fconv), (P + BIAS, row("ffn_conv_bias"))], 2,
                     [(SMALL[:, 0:8], bc("dn_a_log")), (SMALL[:, 8:16], bc("dn_dt_bias")),
                      (SMALL[:, 16:17], A["layer"][ds(l, 1)].partition_broadcast(P))])
        with ExitStack() as mix:
            new = new_in(mix)
            ODN = new("ODN", [P, 4, 512])
            with ExitStack() as dn:
                new = new_in(dn)
                O2 = new("O2", [P, 8, 512])
                QKV = new("QKV", [P, 12, 516])
                Z = new("Z", [P, 4, 512])
                BA = new("BA", [P, 4, 16])
                rms_stage(nc, PS, C, X, H, PAR[:, 0, MIX:MIX + 8], H, RS[:, 0, :], 1e-6)
                dump("h", flat(H), l)
                with ExitStack() as w:
                    new = new_in(w)
                    W = new("W", [P, 2, 8, UNIT])
                    CONV = new("CONV", [P, 2, 512])
                    WBA = new("WBA", [P, 8, 16])
                    qkv_stage(nc, PS, C, A, l, A["w_in"], H, QKV, CONV, Z, WBA, BA, W, PAR[:, 0, :])
                dump("qkv", flat(QKV), l)
                dump("z", flat(Z), l)
                with ExitStack() as w:
                    new = new_in(w)
                    KTOK = new("KTOK", [P, 4, 512])
                    VTOK = new("VTOK", [P, 4, 512])
                    BETA = new("BETA", [P, 4, 8])
                    G = new("G", [P, 4, 8])
                    with ExitStack() as w2:
                        new2 = new_in(w2)
                        delta_prep_stage(nc, PS, C, l, QKV, BA, SMALL, KTOK, VTOK, new2("SQ", [P, 2, 512]), RS,
                                         new2("KS", [P, 512]), new2("VS", [P, 512]), BETA, G, new2("TMP", [P, 3, 32]))
                    dump("qkv2", flat(QKV), l)
                    dump("beta", flat(BETA), l)
                    dump("g", flat(G), l)
                    delta_stage(nc, PS, C, QKV, KTOK, VTOK, BETA, G, O2, new)
                dump("o2", flat(O2), l)
                with ExitStack() as w:
                    head_norm_stage(nc, PS, C, O2, Z, PAR[:, 0, DNN:DNN + 1], ODN, new_in(w)("SQ", [P, 1, 512]), RS)
                dump("odn", flat(ODN), l)
            OHG = new_in(mix)("OHG", [P, 4, 512])
            with ExitStack() as hg:
                new = new_in(hg)
                O2 = new("O2", [P, 8, 512])
                LF = new("LF", [P, 8, 512])
                KK = new("KK", [P, 8, 512])
                HI = new("HI", [P, 4, 512])
                HQ = new("HQ", [P, 4, 512])
                HG = new("HG", [P, 4, 512])
                with ExitStack() as w:
                    new = new_in(w)
                    LB, OM, PAIRB = new("LB", [P, 1024]), new("OM", [P, 1024]), new("PAIRB", [P, 2, 1024])
                    W = new("W", [P, 2, 8, UNIT])
                    lower_bound_stage(nc, A, SMALL, LB, OM, PAIRB)
                    hgrn_proj_stage(nc, PS, l, A["w_in"], H, W, LB, OM, LF, KK, HI, HQ, HG, PAIRB[:, 0, :].rearrange("p (a n) -> p a n", a=2),
                                    PAIRB[:, 1, :].rearrange("p (a n) -> p a n", a=2))
                dump("lf", flat(LF), l)
                dump("kk", flat(KK), l)
                with ExitStack() as w:
                    hgrn_stage(nc, PS, C, LF, KK, HI, HQ, O2, new_in(w))
                dump("ho2", flat(O2), l)
                with ExitStack() as w:
                    head_norm_stage(nc, PS, C, O2, HG, PAR[:, 0, HGN:HGN + 1], OHG, new_in(w)("SQ", [P, 1, 512]), RS)
                dump("ohg", flat(OHG), l)
            with ExitStack() as br:
                new = new_in(br)
                M = new("M", [P, 8, 512])
                with ExitStack() as w:
                    new = new_in(w)
                    branch_stage(nc, PS, l, A, H, ODN, OHG, M, new("WG", [P, 2, 8, UNIT]), new("WB", [P, 2, 4, UNIT]),
                                 new("SG", [P, 4, 512]), new("TMP", [P, 2, 512]))
                dump("m", flat(M), l)
                with ExitStack() as w:
                    slab_stage(nc, PS, at_layer(A["w_out"], l), M, X, new_in(w)("SLAB", [P, 4, 1024]))
        dump("xm", flat(X), l)
        rms_stage(nc, PS, C, X, H, PAR[:, 0, FFN:FFN + 8], H, RS[:, 0, :], 1e-6)
        with ExitStack() as ffn:
            new = new_in(ffn)
            HID = new("HID", [P, 22, 512])
            with ExitStack() as w:
                new = new_in(w)
                ffn_up_stage(nc, PS, l, A, H, PAR[:, 1, :], HID, new("W", [P, 2, 8, UNIT]), new("GP", [P, 2, 514]), new("ACC", [P, 2, 512]))
            with ExitStack() as w:
                slab_stage(nc, PS, at_layer(A["w_down"], l), HID, X, new_in(w)("SLAB", [P, 4, 1024]))
        dump("x", flat(X), l)


INPUTS = ['x', 'mix_norm', 'w_in', 'dn_conv', 'dn_a_log', 'dn_dt_bias', 'dn_norm', 'hg_lb_logits', 'hg_norm',
          'w_branch_dn', 'w_branch_hg', 'w_out', 'ffn_norm', 'w_up', 'ffn_conv', 'ffn_conv_bias', 'w_down',
          'final_norm', 'norm1_g_2', 'w_in_2', 'gmlp_ln_g_2', 'gmlp_ln_b_2', 'gmlp_ws_2', 'gmlp_bs_2',
          'nsa_q_norm_g_2', 'nsa_k_norm_g_2', 'nsa_cmp_pe_2', 'nsa_cmp_w1_2', 'nsa_cmp_w2_2', 'conf_conv_w_2',
          'conf_conv_b_2', 'conf_ln_g_2', 'conf_ln_b_2', 'sconv_w_2', 'w_branch_2', 'w_gate_2', 'b_gate_2', 'w_out_2',
          'norm2_g_2', 'w_mlp1_2', 'w_mlp2_2']


def kernel(**inputs):
    import concourse.bacc as bacc
    from concourse.bass_utils import run_bass_kernel_spmd as run

    nc = bacc.Bacc("TRN2", target_bir_lowering=False, num_devices=1)
    arrays = {n: np.ascontiguousarray(inputs[n]) for n in INPUTS}
    depth = arrays["w_in"].shape[0]
    arrays["consts"] = constant_table(31, 32, 16)
    arrays["layer"] = np.arange(depth, dtype=np.float32).reshape(depth, 1)
    A = {n: nc.dram_tensor(f"in_{n}", a.shape, mybir.dt.from_np(a.dtype), kind="ExternalInput").ap() for n, a in arrays.items()}
    out = nc.dram_tensor("out", (1, 512, 1024), F32, kind="ExternalOutput").ap()
    build(nc, A, out)
    r = run(nc, [{f"in_{n}": a for n, a in arrays.items()}], core_ids=[0])
    return r.results[0]["out"]
```

```python
from contextlib import ExitStack, contextmanager

import numpy as np
import concourse.bass as bass
from concourse import mybir

P = 128
F32 = mybir.dt.float32
F32R = mybir.dt.float32r
I32 = mybir.dt.int32
ALU = mybir.AluOpType
ACT = mybir.ActivationFunctionType
AX = mybir.AxisListType.X
ds = bass.ds
LEVELS = 7
UNIT = 256

IDENT, ONES, INCL, AFTER, REACH, PAIR = 0, 1, 2, 4, 6, 6 + 2 * LEVELS
BLOCK64, CAUSAL, CMP_ADD, CMP_OK, N_CONST = 6 + 4 * LEVELS, 7 + 4 * LEVELS, 8 + 4 * LEVELS, 9 + 4 * LEVELS, 10 + 4 * LEVELS


def constant_table(n_cmp, cmp_len, cmp_stride):
    r = np.arange(P)
    s, t = r[:, None], r[None, :]
    c = np.zeros((P, N_CONST, P), np.float32)
    c[:, IDENT] = s == t
    c[:, ONES] = 1
    for lane in (0, 1):
        a, b = (s, t) if lane == 0 else (P - 1 - s, P - 1 - t)
        c[:, INCL + lane] = a <= b
        c[:, AFTER + lane] = a > b
        for n in range(LEVELS):
            half = 1 << n
            same = a // (2 * half) == b // (2 * half)
            second_a, second_b = a // half % 2 == 1, b // half % 2 == 1
            c[:, REACH + lane * LEVELS + n] = same & np.where(second_b, second_a & (a <= b), ~second_a & (a > b))
            c[:, PAIR + lane * LEVELS + n] = same & ~second_a & second_b
    c[:, BLOCK64] = s // 64 == t // 64
    c[:, CAUSAL] = np.where(t <= s, 0.0, -1e30)
    for chunk in range(4):
        for n in range(n_cmp):
            ok = n * cmp_stride + cmp_len - 1 <= chunk * P + r
            c[:, CMP_OK, chunk * 32 + n] = ok
            c[:, CMP_ADD, chunk * 32 + n] = np.where(ok, 0.0, -1e30)
    return c


class Steps:

    def __init__(self, sem, names):
        self.sem, self.per = sem, len(names)
        self.place = {n: k + 1 for k, n in enumerate(names)}
        self.names, self.given = list(names), 0

    def open(self, e):
        e.sem_inc(self.sem, self.per)

    def done(self, instruction, name):
        assert self.names[self.given % self.per] == name, (name, self.names[self.given % self.per])
        self.given += 1
        return instruction.then_inc(self.sem, 1)

    def wait(self, e, turn, name):
        e.wait_ge(self.sem, turn * self.per + self.per + self.place[name])

    def wait_before(self, e, turn, name):
        e.wait_ge(self.sem, turn * self.per + self.place[name])


@contextmanager
def stage(nc, *names, also=()):
    with ExitStack() as ctx:
        sems = [ctx.enter_context(nc.semaphore(n)) for n in names]
        yield sems
        for s in (*sems, *also):
            nc.gpsimd.sem_clear(s)
        nc.all_engine_barrier()


def pass_waits(e, passed):
    e.sem_inc(passed, 1)


def wide(ap, n):
    return ap.unsqueeze(2).broadcast_to((ap.shape[0], ap.shape[1], n))


def heads(ap, n):
    return ap.unsqueeze(1).broadcast_to((ap.shape[0], n, ap.shape[1]))


def contract(e, out, pairs):
    for n, (lhsT, rhs) in enumerate(pairs):
        last = e.matmul(out, lhsT, rhs, start=n == 0, stop=n == len(pairs) - 1)
    return last


def product(e, out, quads, first=True, final=True):
    for n, (wh, wl, xh, xl) in enumerate(quads):
        e.matmul(out, wh, xh, start=first and n == 0, stop=False)
        e.matmul(out, wh, xl, start=False, stop=False)
        last = e.matmul(out, wl, xh, start=False, stop=final and n == len(quads) - 1)
    return last


class Early:

    def __init__(self, nc, ctx, new, K, cols, pieces):
        self.raw, self.pieces = new("RAW", [P, 2, K, cols]), pieces
        self.loaded = tuple(ctx.enter_context(nc.semaphore(f"{self.raw.name}_{s}_in")) for s in range(2))
        self.issued = False

    def load_first(self, sp):
        if not self.issued:
            self.load(sp)

    def load(self, sp):
        self.issued = True
        for s in range(2):
            for dst, src in self.pieces(self.raw, s):
                sp.dma_start(dst, src).then_inc(self.loaded[s], 16)


class Feed:

    def __init__(self, new, early, hi_sem, lo_sem, free, landed=lambda g, s: (g + 1) * 16):
        self.raw, self.loaded = early.raw, early.loaded
        self.hi, self.lo = new("WHI", self.raw.shape, F32R), new("WLO", self.raw.shape, F32R)
        self.free, self.landed = free, landed
        self.hi_st, self.lo_st = Steps(hi_sem, ["unit0", "unit1"]), Steps(lo_sem, ["unit0", "unit1"])

    def load(self, sp, g, s, pieces):
        self.lo_st.wait_before(sp, g, f"unit{s}")
        for dst, src in pieces:
            sp.dma_start(dst, src).then_inc(self.loaded[s], 16)

    def split_hi(self, act, g, s):
        act.wait_ge(self.loaded[s], self.landed(g, s))
        self.free(act, g, s)
        self.hi_st.done(act.copy(self.hi[:, s], self.raw[:, s]), f"unit{s}")

    def split_lo(self, dve, g, s):
        self.hi_st.wait(dve, g, f"unit{s}")
        self.lo_st.done(dve.tensor_tensor(self.lo[:, s], self.raw[:, s], self.hi[:, s], ALU.subtract), f"unit{s}")

    def ready(self, pe, g, s):
        self.lo_st.wait(pe, g, f"unit{s}")

    def quads(self, s, m, H, k0=0, k1=8):
        c = slice(m * P, (m + 1) * P)
        return [(self.hi[:, s, k, c], self.lo[:, s, k, c], H[0][:, k - k0, :], H[1][:, k - k0, :]) for k in range(k0, k1)]

    def token_quads(self, s, c, H):
        t = slice(c * P, (c + 1) * P)
        return [(H[0][:, k, t], H[1][:, k, t], self.hi[:, s, k, :], self.lo[:, s, k, :]) for k in range(8)]


def after_step(used, names):
    return lambda e, g, s: used.wait_before(e, g, names[s])


def split_tiles_hi(act, sources, his, done):
    for x, hi in zip(sources, his):
        act.copy(hi, x).then_inc(done, 1)


def split_tiles_lo(dve, sources, his, los, hi_done, done):
    for k, (x, hi, lo) in enumerate(zip(sources, his, los)):
        dve.wait_ge(hi_done, k + 1)
        dve.tensor_tensor(lo, x, hi, ALU.subtract).then_inc(done, 1)


def tiles_of(buf, n):
    return [buf[:, k, :] for k in range(n)]


def split_pair(new, K=8):
    return new("HHI", [P, K, 512], F32R), new("HLO", [P, K, 512], F32R)


def turns(e, n, body):
    if n > 1:
        with e.Fori(0, n - 1) as g:
            body(g, True)
    body(n - 1, False)


def load_norm_stage(nc, PS, C, x, X, H):
    S = X.shape[2]
    D = x.shape[1]
    T, K = S // P, D // P
    with stage(nc, "x_in", "turned", "x_kept") as (x_in, turned_s, kept_s):
        turned = Steps(turned_s, [f"tile{k}" for k in range(K)])
        kept = Steps(kept_s, [f"tile{k}" for k in range(K)])
        rows = H[:, :, :].rearrange("p k n -> p (k n)").rearrange("p (c f) -> p c f", c=T)
        with nc.Block() as block:

            @block.sync
            def _(sp):
                sp.dma_start(rows, x.rearrange("(c p) f -> p c f", p=P)).then_inc(x_in, 16)

            @block.tensor
            def _(pe):
                pe.wait_ge(x_in, 16)
                for k in range(K):
                    for c in range(T):
                        last = pe.transpose(PS[:, k, c * P:(c + 1) * P], rows[:, c, k * P:(k + 1) * P], C[:, IDENT, :])
                    turned.done(last, f"tile{k}")

            @block.vector
            def _(dve):
                for k in range(K):
                    dve.wait_ge(turned.sem, k + 1)
                    kept.done(dve.tensor_copy(X[:, k, :], PS[:, k, :]), f"tile{k}")


def rms_stage(nc, PS, C, X, out, weight, RS, eps, new, split=True, early=None):
    K = X.shape[1]
    SQ, T = new("SQ", [P, 4, 512]), new("NT", [P, 4, 512])
    with stage(nc, "squares", "sums", "vector_steps", "root", "hi_done", "lo_done") as (sq_s, sum_s, dve_s, root_s, hi_s, lo_s):
        sums = Steps(sum_s, [f"sum{k}" for k in range(K)])
        with nc.Block() as block:

            @block.sync
            def _(sp):
                if early:
                    early.load(sp)

            @block.scalar
            def _(act):
                for k in range(K):
                    if k >= 4:
                        act.wait_ge(sum_s, k - 3)
                    act.activation(SQ[:, k % 4, :], X[:, k, :], ACT.Square).then_inc(sq_s, 1)
                act.wait_ge(dve_s, 1)
                act.activation(RS[:, :], RS[:, :], ACT.Ln).then_inc(root_s, 1)
                act.wait_ge(root_s, 1)
                act.activation(RS[:, :], RS[:, :], ACT.Exp, scale=-0.5).then_inc(root_s, 1)
                if split:
                    for k in range(K):
                        act.wait_ge(dve_s, 2 + k)
                        act.copy(out[0][:, k, :], T[:, k % 4, :]).then_inc(hi_s, 1)

            @block.tensor
            def _(pe):
                for k in range(K):
                    pe.wait_ge(sq_s, k + 1)
                    last = pe.matmul(PS[:, 0, :], C[:, ONES, :], SQ[:, k % 4, :], start=k == 0, stop=k == K - 1)
                    sums.done(last, f"sum{k}")

            @block.vector
            def _(dve):
                dve.wait_ge(sum_s, K)
                dve.tensor_scalar(RS[:, :], PS[:, 0, :], 1.0 / (K * P), eps, ALU.mult, ALU.add).then_inc(dve_s, 1)
                dve.wait_ge(root_s, 2)
                for k in range(K):
                    if split and k >= 4:
                        dve.wait_ge(lo_s, k - 3)
                    dst = T[:, k % 4, :] if split else out[:, k, :]
                    dve.scalar_tensor_tensor(dst, X[:, k, :], weight[:, k:k + 1], RS[:, :], ALU.mult, ALU.mult).then_inc(dve_s, 1)

            @block.gpsimd
            def _(pool):
                if split:
                    for k in range(K):
                        pool.wait_ge(hi_s, k + 1)
                        pool.tensor_tensor(out[1][:, k, :], T[:, k % 4, :], out[0][:, k, :], ALU.subtract).then_inc(lo_s, 1)


def k_tiles(w):
    return w.rearrange("(k p) n -> p k n", p=P)


def slab_piece(w, raw, s, k):
    rows = w.rearrange("(k p) n -> k p n", p=P)
    src = rows[k] if isinstance(k, int) else rows[ds(k, 1)].rearrange("k p n -> (k p) n")
    return raw[:, s].rearrange("p m n -> p (m n)"), src


def early_slabs(nc, ctx, new, w):
    return Early(nc, ctx, new, 8, P, lambda raw, s: [slab_piece(w, raw, s, s)])


def slab_stage(nc, PS, w, source, X, new, early):
    K, M = source.shape[1], X.shape[1]
    SH, SL = new("SH", [P, 2, 512], F32R), new("SL", [P, 2, 512], F32R)
    with stage(nc, "slab_hi", "slab_lo", "source_hi", "source_lo", "slabs_used", "tiles_done", "added", also=early.loaded) as (
            hi_s, lo_s, shi_s, slo_s, used_s, tiles, added):
        used = Steps(used_s, ["slab0", "slab1"])
        feed = Feed(new, early, hi_s, lo_s, after_step(used, ["slab0", "slab1"]))
        shi, slo = Steps(shi_s, ["slab0", "slab1"]), Steps(slo_s, ["slab0", "slab1"])
        with nc.Block() as block:

            @block.sync
            def _(sp):
                early.load_first(sp)
                with sp.Fori(1, K // 2) as g:
                    for s in range(2):
                        feed.load(sp, g, s, [slab_piece(w, feed.raw, s, g * 2 + s)])

            @block.scalar
            def _(act):
                feed.hi_st.open(act)
                shi.open(act)

                def split(g, s):
                    feed.split_hi(act, g, s)
                    shi.done(act.copy(SH[:, s, :], tile(source, g * 2 + s)), f"slab{s}")

                for s in range(2):
                    split(0, s)
                with act.Fori(1, K // 2) as g:
                    for s in range(2):
                        split(g, s)

            @block.vector
            def _(dve):
                feed.lo_st.open(dve)
                slo.open(dve)

                def split(g, s):
                    feed.split_lo(dve, g, s)
                    shi.wait(dve, g, f"slab{s}")
                    slo.done(dve.tensor_tensor(SL[:, s, :], tile(source, g * 2 + s), SH[:, s, :], ALU.subtract), f"slab{s}")

                for s in range(2):
                    split(0, s)
                with dve.Fori(1, K // 2) as g:
                    for s in range(2):
                        split(g, s)
                for m in range(M):
                    dve.wait_ge(tiles, m + 1)
                    dve.tensor_tensor(X[:, m, :], X[:, m, :], PS[:, m, :], ALU.add).then_inc(added, 1)

            @block.tensor
            def _(pe):
                used.open(pe)

                def use(g, s, first, final):
                    slo.wait(pe, g, f"slab{s}")
                    for m in range(M):
                        last = product(pe, PS[:, m, :], [(feed.hi[:, s, m, :], feed.lo[:, s, m, :], SH[:, s, :], SL[:, s, :])], first, final)
                        if final:
                            last.then_inc(tiles, 1)
                    if not final:
                        used.done(last, f"slab{s}")

                use(0, 0, True, False)
                use(0, 1, False, False)
                with pe.Fori(1, K // 2 - 1) as g:
                    for s in range(2):
                        use(g, s, False, False)
                use(K // 2 - 1, 0, False, False)
                use(K // 2 - 1, 1, False, True)


def tile(buf, k):
    return buf[:, k, :] if isinstance(k, int) else buf[:, ds(k, 1), :].rearrange("p a n -> p (a n)")


def qkv_stage(nc, PS, C, A, l, w_in, H, QKV, CONV, Z, WBA, BA, PAR, new, early):
    T = 4
    names = [f"tile{j}" for j in range(4)]
    pair = split_pair(new)
    with stage(nc, "wba_in", "weights_hi", "weights_lo", "h_hi", "h_lo", "projected", "vector_steps",
               "silu_done", "ba_done", "ba_kept", also=early.loaded) as (
            wba_in, hi_s, lo_s, h_hi, h_lo, proj_s, dve_s, silu_s, ba_done, ba_kept):
        proj = Steps(proj_s, names)
        feed = Feed(new, early, hi_s, lo_s, after_step(proj, ["tile1", "tile3"]))
        dve_st = Steps(dve_s, [f"{a}{j}" for j in range(4) for a in ("kept", "tap0_", "tap1_", "tap2_", "tap3_", "tap4_")])
        silu = Steps(silu_s, names)
        wl = w_in[ds(l, 1)].rearrange("l (k p) n -> p (l k) n", p=P)
        with nc.Block() as block:

            @block.sync
            def _(sp):
                early.load_first(sp)
                with sp.Fori(1, 4) as g:
                    for s in range(2):
                        feed.load(sp, g, s, [(feed.raw[:, s], wl[:, :, ds(g * 2 * UNIT + s * UNIT, UNIT)])])
                sp.dma_start(WBA[:, :, :], wl[:, :, ds(4 * 512, 16)]).then_inc(wba_in, 16)

            @block.tensor
            def _(pe):
                proj.open(pe)

                def group(g, free):
                    for j in range(4):
                        s, m = divmod(j, 2)
                        if m == 0:
                            feed.ready(pe, g, s)
                        free(g, j)
                        proj.done(product(pe, PS[:, j, :], feed.quads(s, m, pair)), f"tile{j}")

                pe.wait_ge(h_lo, 8)
                with pe.Fori(0, 3) as g:
                    group(g, lambda g, j: dve_st.wait_before(pe, g, f"kept{j}"))
                group(3, lambda g, j: dve_st.wait_before(pe, g, f"kept{j}"))
                pe.wait_ge(wba_in, 16)
                for c in range(T):
                    last = contract(pe, PS[:, 4, c * 16:(c + 1) * 16],
                                    [(H[:, k, c * P:(c + 1) * P], WBA[:, k, :]) for k in range(8)])
                last.then_inc(ba_done, 1)

            @block.vector
            def _(dve):
                dve_st.open(dve)
                dve.memset(QKV[:, :, 0:2], 0.0)
                dve.memset(QKV[:, :, 514:516], 0.0)
                feed.lo_st.open(dve)
                split_tiles_lo(dve, tiles_of(H, 8), tiles_of(pair[0], 8), tiles_of(pair[1], 8), h_hi, h_lo)
                feed.split_lo(dve, 0, 0)
                feed.split_lo(dve, 0, 1)
                with dve.Fori(0, 3) as g:
                    for j in range(4):
                        t = g * 4 + j
                        proj.wait(dve, g, f"tile{j}")
                        dve_st.done(dve.tensor_copy(QKV[:, ds(t, 1), 2:514].rearrange("p a n -> p (a n)"), PS[:, j, :]), f"kept{j}")
                        dve_st.wait(dve, g, f"kept{j}")
                        if j >= 2:
                            silu.wait(dve, g, f"tile{j - 2}")
                        else:
                            silu.wait_before(dve, g, f"tile{j + 2}")
                        acc = CONV[:, j % 2, :]
                        for tap in range(5):
                            x_tap = QKV[:, ds(t, 1), tap:tap + 512].rearrange("p a n -> p (a n)")
                            w_tap = PAR[:, ds(t + tap * 12, 1)]
                            if tap == 0:
                                ins = dve.tensor_scalar(acc, x_tap, w_tap, None, ALU.mult)
                            else:
                                dve_st.wait(dve, g, f"tap{tap - 1}_{j}")
                                ins = dve.scalar_tensor_tensor(acc, x_tap, w_tap, acc, ALU.mult, ALU.add)
                            dve_st.done(ins, f"tap{tap}_{j}")
                        if j % 2:
                            feed.split_lo(dve, g + 1, j // 2)
                dve.wait_ge(ba_done, 1)
                dve.tensor_copy(BA[:, :, :].rearrange("p c n -> p (c n)"), PS[:, 4, 0:64]).then_inc(ba_kept, 1)

            @block.scalar
            def _(act):
                silu.open(act)
                feed.hi_st.open(act)
                split_tiles_hi(act, tiles_of(H, 8), tiles_of(pair[0], 8), h_hi)
                feed.split_hi(act, 0, 0)
                feed.split_hi(act, 0, 1)
                with act.Fori(0, 3) as g:
                    for j in range(4):
                        dve_st.wait(act, g, f"tap4_{j}")
                        silu.done(act.activation(QKV[:, ds(g * 4 + j, 1), 2:514].rearrange("p a n -> p (a n)"), CONV[:, j % 2, :], ACT.Silu), f"tile{j}")
                        if j % 2 == 0:
                            feed.split_hi(act, g + 1, j // 2)
                for j in range(4):
                    proj.wait(act, 3, f"tile{j}")
                    silu.done(act.activation(Z[:, j, :], PS[:, j, :], ACT.Silu), f"tile{j}")


def delta_prep_stage(nc, PS, C, l, QKV, BA, SMALL, KTOK, VTOK, BETA, G, new):
    T8 = range(8)
    SQ, R, TMP = new("SQ", [P, 8, 512]), new("R", [P, 8, 512]), new("TMP", [P, 3, 32])
    with stage(nc, "vector_steps", "scalar_steps", "sums", "turned", "gate_steps") as (dve_s, act_s, sum_s, turn_s, gate_s):
        dve_st = Steps(dve_s, [f"mean{t}" for t in T8] + [f"x{t}" for t in (4, 5, 6, 7, 0, 1, 2, 3)] + [f"v_tok{h}" for h in range(4)])
        act_st = Steps(act_s, [f"sq{t}" for t in T8] + [f"ln{t}" for t in T8] + [f"exp{t}" for t in (4, 5, 6, 7, 0, 1, 2, 3)]
                       + [f"k_tok{h}" for h in range(4)])
        gate = Steps(gate_s, ["eb", "ea", "eb1", "beta", "a", "nabs", "exp", "relu", "ln", "sum", "g"])
        after = lambda e, st, name: e.wait_ge(st.sem, st.place[name])
        x = lambda t: QKV[:, t, 2:514]
        tok = lambda buf, h: buf[:, :, h * P:(h + 1) * P]

        with nc.Block() as block:

            @block.scalar
            def _(act):
                for t in T8:
                    act_st.done(act.activation(SQ[:, t, :], x(t), ACT.Square), f"sq{t}")
                for t in T8:
                    after(act, dve_st, f"mean{t}")
                    act_st.done(act.activation(R[:, t, :], R[:, t, :], ACT.Ln), f"ln{t}")
                for t in (4, 5, 6, 7, 0, 1, 2, 3):
                    after(act, act_st, f"ln{t}")
                    act_st.done(act.activation(R[:, t, :], R[:, t, :], ACT.Exp, scale=-0.5), f"exp{t}")
                for h in range(4):
                    act.wait_ge(turn_s, h + 1)
                    act_st.done(act.copy(tok(KTOK, h), PS[:, h, :].rearrange("p (c d) -> p c d", d=P)), f"k_tok{h}")
                a_log = SMALL[:, 0:8]
                gate.done(act.activation(BETA[:, :, :], BA[:, :, 0:8], ACT.Exp, scale=-1.0), "eb")
                gate.done(act.activation(TMP[:, 0, 0:8], a_log, ACT.Exp), "ea")
                act.wait_ge(gate.sem, gate.place["nabs"])
                act.activation(G[:, :, :], TMP[:, 2, :].rearrange("p (c n) -> p c n", n=8), ACT.Exp).then_inc(gate.sem, 1)
                act.wait_ge(gate.sem, gate.place["relu"])
                act.activation(G[:, :, :], G[:, :, :], ACT.Ln, bias=1.0).then_inc(gate.sem, 1)

            @block.tensor
            def _(pe):
                for t in T8:
                    after(pe, act_st, f"sq{t}")
                    pe.matmul(PS[:, t, :], C[:, ONES, :], SQ[:, t, :], start=True, stop=True).then_inc(sum_s, 1)
                after(pe, dve_st, "mean7")
                for n in range(8):
                    h = n % 4
                    if n < 4:
                        after(pe, dve_st, f"x{4 + h}")
                    for c in range(4):
                        last = pe.transpose(PS[:, n, c * P:(c + 1) * P], x(4 + n)[:, c * P:(c + 1) * P], C[:, IDENT, :])
                    last.then_inc(turn_s, 1)

            @block.vector
            def _(dve):
                for t in T8:
                    dve.wait_ge(sum_s, t + 1)
                    dve_st.done(dve.tensor_scalar(R[:, t, :], PS[:, t, :], 1e-6, None, ALU.add), f"mean{t}")
                for t in (4, 5, 6, 7, 0, 1, 2, 3):
                    after(dve, act_st, f"exp{t}")
                    if t >= 4:
                        ins = dve.tensor_tensor(x(t), x(t), R[:, t, :], ALU.mult)
                    else:
                        ins = dve.scalar_tensor_tensor(x(t), x(t), P ** -0.5, R[:, t, :], ALU.mult, ALU.mult)
                    dve_st.done(ins, f"x{t}")
                for h in range(4):
                    dve.wait_ge(turn_s, 5 + h)
                    dve_st.done(dve.tensor_copy(tok(VTOK, h), PS[:, 4 + h, :].rearrange("p (c d) -> p c d", d=P)), f"v_tok{h}")
                a = TMP[:, 1, :]
                dve.wait_ge(gate.sem, gate.place["ea"])
                dve.tensor_scalar(BETA[:, :, :], BETA[:, :, :], 1.0, None, ALU.add).then_inc(gate.sem, 1)
                dve.wait_ge(gate.sem, gate.place["eb1"])
                dve.reciprocal(BETA[:, :, :], BETA[:, :, :]).then_inc(gate.sem, 1)
                dve.tensor_tensor(a.rearrange("p (c n) -> p c n", n=8), BA[:, :, 8:16], heads(SMALL[:, 8:16], 4), ALU.add).then_inc(gate.sem, 1)
                dve.wait_ge(gate.sem, gate.place["a"])
                dve.scalar_tensor_tensor(TMP[:, 2, :], a, -1.0, a, ALU.mult, ALU.min).then_inc(gate.sem, 1)
                dve.wait_ge(gate.sem, gate.place["exp"])
                dve.tensor_scalar(a, a, 0.0, None, ALU.max).then_inc(gate.sem, 1)
                dve.wait_ge(gate.sem, gate.place["ln"])
                dve.tensor_tensor(a.rearrange("p (c n) -> p c n", n=8), a.rearrange("p (c n) -> p c n", n=8), G[:, :, :], ALU.add).then_inc(gate.sem, 1)
                dve.wait_ge(gate.sem, gate.place["sum"])
                dve.scalar_tensor_tensor(G[:, :, :], a.rearrange("p (c n) -> p c n", n=8), -1.0, heads(TMP[:, 0, 0:8], 4), ALU.mult, ALU.mult).then_inc(gate.sem, 1)


def per_head(bank):
    return bank.rearrange("p (h n) -> p h n", h=4)


def delta_stage(nc, PS, C, QKV, KTOK, VTOK, BETA, G, O2, new):
    lanes = (0, 1)
    B = [{n: new(f"{n}{d}", [P, 4, P]) for n in
          ("GB", "BB", "KT", "EG", "DM", "AT", "LB", "T", "TT", "PP", "QK", "VB", "KBG", "KD", "WT", "VN", "QG", "ST")} for d in lanes]
    for d in lanes:
        B[d].update({n: new(f"{n}{d}", [P, 4]) for n in ("GCS", "EGS", "LD", "BE")})
    last_col = (P - 1, 0)
    pool_names = ["gb", "bb", "kt", "vb", "kd", "kbg"]
    pe_names = ["gc", "bg", "qk"] + ["p0"] + [f"{a}{n}" for n in range(1, LEVELS) for a in "pd"] + ["wt", "vn", "o", "st"]
    act_names = ["eg", "dm", "egs", "ld"] + [f"p{n}" for n in range(1, LEVELS)] + ["wt", "o"]
    dve_names = (["gcs"] + [f"dif{h}" for h in range(4)] + ["be", "ldif", "mask", "at", "atb", "qk", "t", "tt", "qg"]
                 + [f"{a}{n}" for n in range(LEVELS) for a in ("lb", "t", "tt")][:-3] + [f"lb{LEVELS - 1}", f"tt{LEVELS - 1}", "vn"]
                 + [f"st{h}" for h in range(4)])
    with stage(nc, *[f"{e}{d}" for d in lanes for e in ("delta_pe", "delta_act", "delta_dve", "delta_pool")], "waits_passed") as sems:
        pe_st = [Steps(sems[4 * d], pe_names) for d in lanes]
        act_st = [Steps(sems[4 * d + 1], act_names) for d in lanes]
        dve_st = [Steps(sems[4 * d + 2], dve_names) for d in lanes]
        pool_st = [Steps(sems[4 * d + 3], pool_names) for d in lanes]

        def chunk(i, d):
            return i if d == 0 else i * -1 + 3

        def bank(d, n):
            return PS[:, 4 * d + n, :]

        with nc.Block() as block:

            @block.gpsimd
            def _(pool):
                for d in lanes:
                    pool_st[d].open(pool)
                with pool.Fori(0, 4) as i:
                    for d in lanes:
                        b, c, st = B[d], chunk(i, d), pool_st[d]
                        pe_st[d].wait_before(pool, i, "bg")
                        g_c = G[:, ds(c, 1), 4 * d:4 * d + 4].rearrange("p a n -> p (a n)")
                        b_c = BETA[:, ds(c, 1), 4 * d:4 * d + 4].rearrange("p a n -> p (a n)")
                        st.done(pool.tensor_copy(b["GB"][:, :, :], wide(g_c, P)), "gb")
                        st.done(pool.tensor_copy(b["BB"][:, :, :], wide(b_c, P)), "bb")
                        pe_st[d].wait_before(pool, i, "qk")
                        st.done(pool.tensor_copy(b["KT"][:, :, :], QKV[:, 4:8, ds(c * P + 2, P)]), "kt")
                    for d in lanes:
                        b, c, st = B[d], chunk(i, d), pool_st[d]
                        pe_st[d].wait_before(pool, i, "st")
                        b_c = BETA[:, ds(c, 1), 4 * d:4 * d + 4].rearrange("p a n -> p (a n)")
                        k_c, v_c = (x[:, ds(c, 1), :].rearrange("p a (h n) -> p (a h) n", h=4) for x in (KTOK, VTOK))
                        st.done(pool.tensor_tensor(b["VB"][:, :, :], v_c, wide(b_c, P), ALU.mult), "vb")
                        act_st[d].wait(pool, i, "ld")
                        pass_waits(pool, sems[8])
                        st.done(pool.tensor_tensor(b["KD"][:, :, :], k_c, wide(b["LD"][:, :], P), ALU.mult), "kd")
                        dve_st[d].wait(pool, i, "be")
                        pass_waits(pool, sems[8])
                        st.done(pool.tensor_tensor(b["KBG"][:, :, :], k_c, wide(b["BE"][:, :], P), ALU.mult), "kbg")

            @block.tensor
            def _(pe):
                for d in lanes:
                    pe_st[d].open(pe)

                def each_head(d, n, lhsT, rhs):
                    for h in range(4):
                        last = pe.matmul(bank(d, n)[:, h * P:(h + 1) * P], lhsT(h), rhs(h), start=True, stop=True)
                    return last

                with pe.Fori(0, 4) as i:
                    for d in lanes:
                        b, c, st = B[d], chunk(i, d), pe_st[d]
                        pool_st[d].wait(pe, i, "bb")
                        act_st[d].wait_before(pe, i, "wt")
                        dve_st[d].wait_before(pe, i, "vn")
                        pe.matmul(bank(d, 3)[:, 0:4], C[:, INCL + d, :], G[:, ds(c, 1), 4 * d:4 * d + 4].rearrange("p a n -> p (a n)"), start=True, stop=True)
                        st.done(each_head(d, 0, lambda h: b["GB"][:, h, :], lambda h: C[:, INCL + d, :]), "gc")
                        act_st[d].wait_before(pe, i, "o")
                        dve_st[d].wait_before(pe, i, "st3")
                        pool_st[d].wait(pe, i, "kt")
                        each_head(d, 1, lambda h: b["BB"][:, h, :], lambda h: C[:, IDENT, :])
                        st.done(each_head(d, 2, lambda h: b["KT"][:, h, :], lambda h: QKV[:, 4 + h, ds(c * P + 2, P)]), "bg")
                        dve_st[d].wait(pe, i, "gcs")
                        st.done(each_head(d, 3, lambda h: b["KT"][:, h, :], lambda h: QKV[:, h, ds(c * P + 2, P)]), "qk")
                    for n in range(LEVELS):
                        for d in lanes:
                            b, st = B[d], pe_st[d]
                            dve_st[d].wait(pe, i, f"lb{n}")
                            if n == 0:
                                act_st[d].wait(pe, i, "eg")
                            elif n > 1:
                                act_st[d].wait(pe, i, f"p{n - 1}")
                            st.done(each_head(d, 0, lambda h: b["LB"][:, h, :], lambda h: b["T"][:, h, :]), f"p{n}")
                        for d in lanes if n else ():
                            b, st = B[d], pe_st[d]
                            act_st[d].wait(pe, i, f"p{n}")
                            dve_st[d].wait(pe, i, f"tt{n - 1}")
                            if n < LEVELS - 1:
                                each_head(d, 1, lambda h: b["TT"][:, h, :], lambda h: b["PP"][:, h, :])
                            st.done(each_head(d, 2, lambda h: b["PP"][:, h, :], lambda h: b["TT"][:, h, :]), f"d{n}")
                    for d in lanes:
                        b, st = B[d], pe_st[d]
                        dve_st[d].wait(pe, i, f"tt{LEVELS - 1}")
                        pool_st[d].wait(pe, i, "kbg")
                        st.done(each_head(d, 3, lambda h: b["KBG"][:, h, :], lambda h: b["TT"][:, h, :]), "wt")
                    for d in lanes:
                        b, st = B[d], pe_st[d]
                        act_st[d].wait(pe, i, "wt")
                        dve_st[d].wait_before(pe, i, "st3")
                        for h in range(4):
                            last = contract(pe, bank(d, 0)[:, h * P:(h + 1) * P],
                                            [(b["TT"][:, h, :], b["VB"][:, h, :]), (b["WT"][:, h, :], b["ST"][:, h, :])])
                        st.done(last, "vn")
                    for d in lanes:
                        b, st = B[d], pe_st[d]
                        dve_st[d].wait(pe, i, "vn")
                        for h in range(4):
                            last = contract(pe, bank(d, 1)[:, h * P:(h + 1) * P],
                                            [(b["ST"][:, h, :], b["QG"][:, h, :]), (b["VN"][:, h, :], b["QK"][:, h, :])])
                        st.done(last, "o")
                        st.done(each_head(d, 2, lambda h: b["KD"][:, h, :], lambda h: b["VN"][:, h, :]), "st")

            @block.scalar
            def _(act):
                for d in lanes:
                    act_st[d].open(act)
                with act.Fori(0, 4) as i:
                    for d in lanes:
                        b, st = B[d], act_st[d]
                        pe_st[d].wait(act, i, "gc")
                        dve_st[d].wait_before(act, i, "st3")
                        st.done(act.activation(b["EG"][:, :, :], per_head(bank(d, 0)), ACT.Exp), "eg")
                        dve_st[d].wait(act, i, "dif3")
                        st.done(act.activation(b["DM"][:, :, :], b["DM"][:, :, :], ACT.Exp), "dm")
                        st.done(act.activation(b["EGS"][:, :], b["GCS"][:, :], ACT.Exp), "egs")
                        dve_st[d].wait(act, i, "ldif")
                        st.done(act.activation(b["LD"][:, :], b["LD"][:, :], ACT.Exp), "ld")
                    for n in range(1, LEVELS):
                        for d in lanes:
                            pe_st[d].wait(act, i, f"p{n}")
                            act_st[d].done(act.copy(B[d]["PP"][:, :, :], per_head(bank(d, 0))), f"p{n}")
                    for d in lanes:
                        pe_st[d].wait(act, i, "wt")
                        act_st[d].done(act.mul(B[d]["WT"][:, :, :], per_head(bank(d, 3)), -1.0), "wt")
                    for d in lanes:
                        pe_st[d].wait(act, i, "o")
                        act_st[d].done(act.copy(O2[:, 4 * d:4 * d + 4, ds(chunk(i, d) * P, P)], per_head(bank(d, 1))), "o")

            @block.vector
            def _(dve):
                for d in lanes:
                    dve_st[d].open(dve)
                    dve.memset(B[d]["ST"][:, :, :], 0.0)
                with dve.Fori(0, 4) as i:
                    for d in lanes:
                        b, c, st = B[d], chunk(i, d), dve_st[d]
                        gcb = per_head(bank(d, 0))
                        pe_st[d].wait(dve, i, "gc")
                        act_st[d].wait_before(dve, i, "egs")
                        st.done(dve.tensor_copy(b["GCS"][:, :], bank(d, 3)[:, 0:4]), "gcs")
                        st.wait(dve, i, "gcs")
                        act_st[d].wait(dve, i, "eg")
                        for h in range(4):
                            st.done(dve.tensor_scalar(b["DM"][:, h, :], gcb[:, h, :], b["GCS"][:, h:h + 1], 0.0, ALU.subtract, ALU.min), f"dif{h}")
                        act_st[d].wait(dve, i, "egs")
                        pool_st[d].wait_before(dve, i, "kbg")
                        b_c = BETA[:, ds(c, 1), 4 * d:4 * d + 4].rearrange("p a n -> p (a n)")
                        st.done(dve.tensor_tensor(b["BE"][:, :], b_c, b["EGS"][:, :], ALU.mult), "be")
                        pool_st[d].wait_before(dve, i, "kd")
                        st.done(dve.tensor_tensor(b["LD"][:, :], gcb[:, :, last_col[d]], b["GCS"][:, :], ALU.subtract), "ldif")
                        act_st[d].wait(dve, i, "dm")
                        st.done(dve.tensor_tensor(b["DM"][:, :, :], b["DM"][:, :, :], heads(C[:, INCL + d, :], 4), ALU.mult), "mask")
                        pe_st[d].wait(dve, i, "bg")
                        st.wait(dve, i, "mask")
                        st.done(dve.tensor_tensor(b["AT"][:, :, :], per_head(bank(d, 2)), b["DM"][:, :, :], ALU.mult), "at")
                        st.wait(dve, i, "at")
                        st.done(dve.tensor_tensor(b["AT"][:, :, :], per_head(bank(d, 1)), b["AT"][:, :, :], ALU.mult), "atb")
                        pe_st[d].wait(dve, i, "qk")
                        st.done(dve.tensor_tensor(b["QK"][:, :, :], per_head(bank(d, 3)), b["DM"][:, :, :], ALU.mult), "qk")
                        st.done(dve.tensor_copy(b["T"][:, :, :], heads(C[:, IDENT, :], 4)), "t")
                        st.done(dve.tensor_copy(b["TT"][:, :, :], heads(C[:, IDENT, :], 4)), "tt")
                        act_st[d].wait(dve, i, "eg")
                        st.done(dve.tensor_tensor(b["QG"][:, :, :], QKV[:, 0:4, ds(c * P + 2, P)], b["EG"][:, :, :], ALU.mult), "qg")
                    for d in lanes:
                        b, st = B[d], dve_st[d]
                        st.wait(dve, i, "atb")
                        st.done(dve.tensor_tensor(b["LB"][:, :, :], b["AT"][:, :, :], heads(C[:, PAIR + d * LEVELS, :], 4), ALU.mult), "lb0")
                    for d in lanes:
                        b, st = B[d], dve_st[d]
                        st.wait(dve, i, "lb0")
                        pe_st[d].wait(dve, i, "p0")
                        st.done(dve.tensor_tensor(b["T"][:, :, :], b["T"][:, :, :], per_head(bank(d, 0)), ALU.subtract), "t0")
                        st.done(dve.tensor_tensor(b["TT"][:, :, :], b["TT"][:, :, :], b["LB"][:, :, :], ALU.subtract), "tt0")
                        st.wait(dve, i, "tt0")
                        st.done(dve.tensor_tensor(b["LB"][:, :, :], b["AT"][:, :, :], heads(C[:, PAIR + d * LEVELS + 1, :], 4), ALU.mult), "lb1")
                    for n in range(1, LEVELS):
                        for d in lanes:
                            b, st = B[d], dve_st[d]
                            pe_st[d].wait(dve, i, f"d{n}")
                            if n < LEVELS - 1:
                                st.done(dve.tensor_tensor(b["T"][:, :, :], b["T"][:, :, :], per_head(bank(d, 1)), ALU.subtract), f"t{n}")
                            st.done(dve.tensor_tensor(b["TT"][:, :, :], b["TT"][:, :, :], per_head(bank(d, 2)), ALU.subtract), f"tt{n}")
                            if n < LEVELS - 1:
                                st.done(dve.tensor_tensor(b["LB"][:, :, :], b["AT"][:, :, :], heads(C[:, PAIR + d * LEVELS + n + 1, :], 4), ALU.mult), f"lb{n + 1}")
                    for d in lanes:
                        pe_st[d].wait(dve, i, "vn")
                        dve_st[d].done(dve.tensor_copy(B[d]["VN"][:, :, :], per_head(bank(d, 0))), "vn")
                    for d in lanes:
                        b, st = B[d], dve_st[d]
                        pe_st[d].wait(dve, i, "st")
                        for h in range(4):
                            st.done(dve.scalar_tensor_tensor(b["ST"][:, h, :], b["ST"][:, h, :], b["EG"][:, h, last_col[d]:last_col[d] + 1],
                                                             bank(d, 2)[:, h * P:(h + 1) * P], ALU.mult, ALU.add), f"st{h}")


def head_norm_stage(nc, PS, C, O2, Z, weight, out, new, early=None):
    heads_4 = range(4)
    SQ, R = new("HSQ", [P, 4, 512]), new("HR", [P, 4, 512])
    with stage(nc, "vector_steps", "scalar_steps", "sums") as (dve_s, act_s, sum_s):
        dve_st = Steps(dve_s, [f"{a}{h}" for a in ("add", "mean", "norm", "out") for h in heads_4])
        act_st = Steps(act_s, [f"{a}{h}" for a in ("sq", "ln", "exp") for h in heads_4])
        after = lambda e, st, name: e.wait_ge(st.sem, st.place[name])
        with nc.Block() as block:

            @block.sync
            def _(sp):
                if early:
                    early.load(sp)

            @block.vector
            def _(dve):
                for h in heads_4:
                    dve_st.done(dve.tensor_tensor(O2[:, h, :], O2[:, h, :], O2[:, h + 4, :], ALU.add), f"add{h}")
                for h in heads_4:
                    dve.wait_ge(sum_s, h + 1)
                    dve_st.done(dve.tensor_scalar(R[:, h, :], PS[:, h, :], 1.0 / P, 1e-6, ALU.mult, ALU.add), f"mean{h}")
                for h in heads_4:
                    after(dve, act_st, f"exp{h}")
                    dve_st.done(dve.scalar_tensor_tensor(O2[:, h, :], O2[:, h, :], weight, R[:, h, :], ALU.mult, ALU.mult), f"norm{h}")
                for h in heads_4:
                    after(dve, dve_st, f"norm{h}")
                    dve_st.done(dve.tensor_tensor(out[:, h, :], O2[:, h, :], Z[:, h, :], ALU.mult), f"out{h}")

            @block.scalar
            def _(act):
                for h in heads_4:
                    after(act, dve_st, f"add{h}")
                    act_st.done(act.activation(SQ[:, h, :], O2[:, h, :], ACT.Square), f"sq{h}")
                for h in heads_4:
                    after(act, dve_st, f"mean{h}")
                    act_st.done(act.activation(R[:, h, :], R[:, h, :], ACT.Ln), f"ln{h}")
                for h in heads_4:
                    after(act, act_st, f"ln{h}")
                    act_st.done(act.activation(R[:, h, :], R[:, h, :], ACT.Exp, scale=-0.5), f"exp{h}")

            @block.tensor
            def _(pe):
                for h in heads_4:
                    after(pe, act_st, f"sq{h}")
                    pe.matmul(PS[:, h, :], C[:, ONES, :], SQ[:, h, :], start=True, stop=True).then_inc(sum_s, 1)


def lower_bound_stage(nc, A, SMALL, LB, OM, PAIRB, early):
    lg = A["hg_lb_logits"]
    with stage(nc, "logits_in", "steps") as (logits_in, steps):
        with nc.Block() as block:

            @block.sync
            def _(sp):
                for n in range(2):
                    sp.dma_start(PAIRB[:, n, :], lg[n].rearrange("d n -> (d n)").partition_broadcast(P)).then_inc(logits_in, 16)
                early.load(sp)

            @block.vector
            def _(dve):
                dve.wait_ge(logits_in, 32)
                dve.tensor_tensor(LB[:, :], PAIRB[:, 0, :], PAIRB[:, 1, :], ALU.subtract).then_inc(steps, 1)
                dve.wait_ge(steps, 2)
                dve.tensor_scalar(LB[:, :], LB[:, :], 1.0, None, ALU.add).then_inc(steps, 1)
                dve.wait_ge(steps, 3)
                dve.reciprocal(LB[:, :], LB[:, :]).then_inc(steps, 1)
                dve.wait_ge(steps, 4)
                dve.tensor_scalar(LB[:, :], LB[:, :], SMALL[:, 16:17], None, ALU.mult).then_inc(steps, 1)
                dve.wait_ge(steps, 5)
                dve.tensor_scalar(OM[:, :], LB[:, :], -1.0, 1.0, ALU.mult, ALU.add).then_inc(steps, 1)

            @block.scalar
            def _(act):
                act.wait_ge(steps, 1)
                act.activation(LB[:, :], LB[:, :], ACT.Exp).then_inc(steps, 1)


HGRN_COL, HGRN_ORDER = 4 * 512 + 16, (1, 2, 3, 0, 4)


def hgrn_proj_stage(nc, PS, l, w_in, H, LB, OM, LF, KK, HI, HQ, HG, new, early):
    pair = split_pair(new)
    E0, E1 = HQ[:, 0:2, :], HQ[:, 2:4, :]
    col0 = HGRN_COL
    order = HGRN_ORDER
    with stage(nc, "weights_hi", "weights_lo", "h_hi", "h_lo", "projected", "vector_steps", "scalar_steps", also=early.loaded) as (
            hi_s, lo_s, h_hi, h_lo, proj_s, dve_s, act_s):
        pnames = []
        for g in range(5):
            pnames += [f"unit{g}_0", f"unit{g}_1"] if g < 3 else [f"unit{g}_{m}" for m in range(4)]
        proj = Steps(proj_s, pnames)
        act_st = Steps(act_s, [f"{a}{g}_{c}" for g in range(2) for c in range(4) for a in ("e", "ln1", "lnb")]
                       + [f"hi{c}" for c in range(4)] + [f"silu{g}_{m}" for g in (3, 4) for m in range(4)])
        dve_st = Steps(dve_s, [f"{a}{g}_{c}" for g in range(2) for c in range(4) for a in ("lbe", "e1", "inv", "er", "kk", "lf")]
                       + [f"q{m}" for m in range(4)])

        def bank(g, c):
            return PS[:, 4 * (g % 2) + c, :]

        def free(e, g, s):
            if g:
                e.wait_ge(proj.sem, proj.place[f"unit{g - 1}_{s}" if g <= 3 else f"unit{g - 1}_{2 * s + 1}"])

        feed = Feed(new, early, hi_s, lo_s, free)
        wl = w_in[ds(l, 1)].rearrange("l (k p) n -> p (l k) n", p=P)
        with nc.Block() as block:

            @block.sync
            def _(sp):
                early.load_first(sp)
                for g in range(1, 5):
                    for s in range(2):
                        feed.load(sp, g, s, [(feed.raw[:, s], wl[:, :, ds(col0 + order[g] * 512 + s * UNIT, UNIT)])])

            @block.tensor
            def _(pe):
                def bank_free(g, c):
                    if g >= 2:
                        pe.wait_ge(act_st.sem, act_st.place[f"hi{c}" if g == 4 else f"e{g - 2}_{c}"])

                pe.wait_ge(h_lo, 8)
                for g in range(3):
                    for s in range(2):
                        feed.ready(pe, g, s)
                        for c in range(4):
                            if s == 0:
                                bank_free(g, c)
                            last = product(pe, bank(g, c)[:, s * UNIT:(s + 1) * UNIT], feed.token_quads(s, c, pair))
                        proj.done(last, f"unit{g}_{s}")
                for g in (3, 4):
                    for m in range(4):
                        s, half = divmod(m, 2)
                        if half == 0:
                            feed.ready(pe, g, s)
                        bank_free(g, m)
                        proj.done(product(pe, bank(g, m), feed.quads(s, half, pair)), f"unit{g}_{m}")

            @block.scalar
            def _(act):
                feed.hi_st.open(act)
                split_tiles_hi(act, tiles_of(H, 8), tiles_of(pair[0], 8), h_hi)
                feed.split_hi(act, 0, 0)
                feed.split_hi(act, 0, 1)
                feed.split_hi(act, 1, 0)
                feed.split_hi(act, 1, 1)
                for g in range(2):
                    act.wait_ge(proj.sem, proj.place[f"unit{g}_1"])
                    for c in range(4):
                        if g or c >= 2:
                            gg, cc = (g, c - 2) if c >= 2 else (g - 1, c + 2)
                            act.wait_ge(dve_st.sem, dve_st.place[f"lf{gg}_{cc}"])
                        act_st.done(act.activation(E0[:, c % 2, :], bank(g, c), ACT.Exp, scale=-1.0), f"e{g}_{c}")
                        act.wait_ge(act_st.sem, act_st.place[f"e{g}_{c}"])
                        act_st.done(act.activation(E1[:, c % 2, :], E0[:, c % 2, :], ACT.Ln, bias=1.0), f"ln1{g}_{c}")
                        act.wait_ge(dve_st.sem, dve_st.place[f"lbe{g}_{c}"])
                        act_st.done(act.activation(LF[:, g * 4 + c, :], LF[:, g * 4 + c, :], ACT.Ln, bias=1.0), f"lnb{g}_{c}")
                        if c % 2:
                            feed.split_hi(act, g + 2, c // 2)
                act.wait_ge(proj.sem, proj.place["unit2_1"])
                for c in range(4):
                    act_st.done(act.copy(HI[:, c, :], bank(2, c)), f"hi{c}")
                act.wait_ge(dve_st.sem, dve_st.place["lf1_3"])
                for g, dst in ((3, HQ), (4, HG)):
                    for m in range(4):
                        act.wait_ge(proj.sem, proj.place[f"unit{g}_{m}"])
                        act_st.done(act.activation(dst[:, m, :], bank(g, m), ACT.Silu), f"silu{g}_{m}")
                        if g == 3 and m % 2:
                            feed.split_hi(act, 4, m // 2)

            @block.vector
            def _(dve):
                feed.lo_st.open(dve)
                split_tiles_lo(dve, tiles_of(H, 8), tiles_of(pair[0], 8), tiles_of(pair[1], 8), h_hi, h_lo)
                feed.split_lo(dve, 0, 0)
                feed.split_lo(dve, 0, 1)
                feed.split_lo(dve, 1, 0)
                feed.split_lo(dve, 1, 1)
                for g in range(2):
                    cols = slice(g * 512, (g + 1) * 512)
                    for c in range(4):
                        lf, kk = LF[:, g * 4 + c, :], KK[:, g * 4 + c, :]
                        own = lambda name: dve.wait_ge(dve_st.sem, dve_st.place[f"{name}{g}_{c}"])
                        dve.wait_ge(act_st.sem, act_st.place[f"e{g}_{c}"])
                        dve_st.done(dve.tensor_tensor(lf, E0[:, c % 2, :], LB[:, cols], ALU.mult), f"lbe{g}_{c}")
                        dve_st.done(dve.tensor_scalar(kk, E0[:, c % 2, :], 1.0, None, ALU.add), f"e1{g}_{c}")
                        own("e1")
                        dve_st.done(dve.reciprocal(kk, kk), f"inv{g}_{c}")
                        own("inv")
                        dve_st.done(dve.tensor_tensor(kk, kk, E0[:, c % 2, :], ALU.mult), f"er{g}_{c}")
                        own("er")
                        dve_st.done(dve.tensor_tensor(kk, kk, OM[:, cols], ALU.mult), f"kk{g}_{c}")
                        dve.wait_ge(act_st.sem, act_st.place[f"lnb{g}_{c}"])
                        dve_st.done(dve.tensor_tensor(lf, lf, E1[:, c % 2, :], ALU.subtract), f"lf{g}_{c}")
                        if c % 2:
                            feed.split_lo(dve, g + 2, c // 2)
                for m in range(4):
                    if m % 2:
                        feed.split_lo(dve, 4, m // 2)
                    dve.wait_ge(act_st.sem, act_st.place[f"silu3_{m}"])
                    dve_st.done(dve.tensor_scalar(HQ[:, m, :], HQ[:, m, :], P ** -0.5, None, ALU.mult), f"q{m}")


def hgrn_stage(nc, PS, C, LF, KK, HI, HQ, O2, new):
    lanes = (0, 1)
    B = [{n: new(f"h{n}{d}", [P, 4, P]) for n in ("LFS", "KS", "IS", "KT", "EC", "ES", "QE", "KD", "AT", "ST", "X0", "X1", "E0", "E1")} for d in lanes]
    last_col = (P - 1, 0)
    pool_names = ["lf", "k", "i", "kd"]
    pe_names = ["kt", "cum", "suf", "dia", "e0"]
    for n in range(LEVELS):
        if n + 1 < LEVELS:
            pe_names.append(f"e{n + 1}")
        pe_names.append(f"a{n}")
    pe_names += ["o", "st"]
    act_names = ["kt", "cum", "suf"] + [f"e{n}" for n in range(LEVELS)] + ["o"]
    dve_names = ["zero", "dia", "qe"]
    for n in range(LEVELS):
        dve_names += [f"xq{n}", f"xk{n}"]
        if n:
            dve_names.append(f"a{n - 1}")
    dve_names += [f"a{LEVELS - 1}"] + [f"st{h}" for h in range(4)]
    with stage(nc, *[f"{e}{d}" for d in lanes for e in ("hgrn_pe", "hgrn_act", "hgrn_dve", "hgrn_pool")], "waits_passed") as sems:
        pe_st = [Steps(sems[4 * d], pe_names) for d in lanes]
        act_st = [Steps(sems[4 * d + 1], act_names) for d in lanes]
        dve_st = [Steps(sems[4 * d + 2], dve_names) for d in lanes]
        pool_st = [Steps(sems[4 * d + 3], pool_names) for d in lanes]

        def chunk(i, d):
            return i if d == 0 else i * -1 + 3

        def bank(d, n):
            return PS[:, 4 * d + n, :]

        def halves(ap, n, second):
            v = ap.rearrange("p h (b two a) -> p (h b) two a", two=2, a=1 << n)
            return v[:, :, 1 if second else 0, :]

        with nc.Block() as block:

            @block.gpsimd
            def _(pool):
                for d in lanes:
                    pool_st[d].open(pool)
                with pool.Fori(0, 4) as i:
                    for d in lanes:
                        b, st = B[d], pool_st[d]
                        row = ds(chunk(i, d) + 4 * d, 1)
                        f = lambda t: t[:, :, :].rearrange("p h n -> p (h n)")
                        pe_st[d].wait_before(pool, i, f"e{LEVELS - 1}")
                        st.done(pool.tensor_copy(f(b["LFS"]), LF[:, row, :].rearrange("p a n -> p (a n)")), "lf")
                        st.wait_before(pool, i, "kd")
                        st.done(pool.tensor_copy(f(b["KS"]), KK[:, row, :].rearrange("p a n -> p (a n)")), "k")
                        pe_st[d].wait_before(pool, i, "st")
                        st.done(pool.tensor_copy(f(b["IS"]), HI[:, ds(chunk(i, d), 1), :].rearrange("p a n -> p (a n)")), "i")
                    for d in lanes:
                        b, st = B[d], pool_st[d]
                        act_st[d].wait(pool, i, "suf")
                        st.done(pool.tensor_tensor(b["KD"][:, :, :], b["KS"][:, :, :], b["ES"][:, :, :], ALU.mult), "kd")

            @block.tensor
            def _(pe):
                for d in lanes:
                    pe_st[d].open(pe)

                def each_head(d, n, lhsT, rhs):
                    for h in range(4):
                        last = pe.matmul(bank(d, n)[:, h * P:(h + 1) * P], lhsT(h), rhs(h), start=True, stop=True)
                    return last

                def exponents(i, d, n):
                    b, st = B[d], pe_st[d]
                    if n >= 2:
                        act_st[d].wait(pe, i, f"e{n - 2}")
                    else:
                        act_st[d].wait(pe, i, ("cum", "suf")[n])
                    st.done(each_head(d, n % 2, lambda h: b["LFS"][:, h, :], lambda h: C[:, REACH + d * LEVELS + n, :]), f"e{n}")

                with pe.Fori(0, 4) as i:
                    for d in lanes:
                        b, c, st = B[d], chunk(i, d), pe_st[d]
                        pool_st[d].wait(pe, i, "k")
                        dve_st[d].wait_before(pe, i, "st3")
                        for h in range(4):
                            last = pe.transpose(bank(d, 2)[:, h * P:(h + 1) * P], b["KS"][:, h, :], C[:, IDENT, :])
                        st.done(last, "kt")
                        act_st[d].wait_before(pe, i, f"e{LEVELS - 1}")
                        st.done(each_head(d, 0, lambda h: b["LFS"][:, h, :], lambda h: C[:, INCL + d, :]), "cum")
                        st.done(pe.matmul(bank(d, 1), C[:, AFTER + d, :], b["LFS"][:, :, :].rearrange("p h n -> p (h n)"), start=True, stop=True), "suf")
                        act_st[d].wait(pe, i, "kt")
                        st.done(each_head(d, 3, lambda h: b["KT"][:, h, :], lambda h: HQ[:, h, ds(c * P, P)]), "dia")
                    for d in lanes:
                        exponents(i, d, 0)
                    for n in range(LEVELS):
                        for d in lanes:
                            b, st = B[d], pe_st[d]
                            if n + 1 < LEVELS:
                                exponents(i, d, n + 1)
                            if n == 0:
                                act_st[d].wait(pe, i, "kt")
                            dve_st[d].wait(pe, i, f"xk{n}")
                            x = b[f"X{n % 2}"]
                            st.done(each_head(d, 2 + n % 2, lambda h: x[:, h, :], lambda h: x[:, h, :]), f"a{n}")
                    for d in lanes:
                        b, st = B[d], pe_st[d]
                        dve_st[d].wait(pe, i, f"a{LEVELS - 1}")
                        pool_st[d].wait(pe, i, "kd")
                        for h in range(4):
                            last = contract(pe, bank(d, 3)[:, h * P:(h + 1) * P],
                                            [(b["ST"][:, h, :], b["QE"][:, h, :]), (b["IS"][:, h, :], b["AT"][:, h, :])])
                        st.done(last, "o")
                        st.done(each_head(d, 2, lambda h: b["KD"][:, h, :], lambda h: b["IS"][:, h, :]), "st")

            @block.scalar
            def _(act):
                for d in lanes:
                    act_st[d].open(act)
                with act.Fori(0, 4) as i:
                    for d in lanes:
                        b, st = B[d], act_st[d]
                        pe_st[d].wait(act, i, "kt")
                        dve_st[d].wait_before(act, i, f"xk{LEVELS - 1}")
                        st.done(act.copy(b["KT"][:, :, :], per_head(bank(d, 2))), "kt")
                        pe_st[d].wait(act, i, "cum")
                        dve_st[d].wait_before(act, i, "st3")
                        st.done(act.activation(b["EC"][:, :, :], per_head(bank(d, 0)), ACT.Exp), "cum")
                        pe_st[d].wait(act, i, "suf")
                        pool_st[d].wait_before(act, i, "kd")
                        st.done(act.activation(b["ES"][:, :, :], per_head(bank(d, 1)), ACT.Exp), "suf")
                    for n in range(LEVELS):
                        for d in lanes:
                            b, st = B[d], act_st[d]
                            pe_st[d].wait(act, i, f"e{n}")
                            if n >= 2:
                                dve_st[d].wait(act, i, f"xk{n - 2}")
                            else:
                                dve_st[d].wait_before(act, i, f"xk{LEVELS - 1}")
                            st.done(act.activation(b[f"E{n % 2}"][:, :, :], per_head(bank(d, n % 2)), ACT.Exp), f"e{n}")
                    for d in lanes:
                        pe_st[d].wait(act, i, "o")
                        act_st[d].done(act.copy(O2[:, 4 * d:4 * d + 4, ds(chunk(i, d) * P, P)], per_head(bank(d, 3))), "o")

            @block.vector
            def _(dve):
                for d in lanes:
                    dve_st[d].open(dve)
                    dve.memset(B[d]["ST"][:, :, :], 0.0)
                mask = lambda n: heads(C[:, n, :], 4).bitcast(I32)
                with dve.Fori(0, 4) as i:
                    for d in lanes:
                        b, c, st = B[d], chunk(i, d), dve_st[d]
                        pe_st[d].wait_before(dve, i, "o")
                        st.done(dve.memset(b["AT"][:, :, :], 0.0), "zero")
                        pe_st[d].wait(dve, i, "dia")
                        st.wait(dve, i, "zero")
                        pass_waits(dve, sems[8])
                        st.done(dve.copy_predicated(b["AT"][:, :, :], mask(IDENT), per_head(bank(d, 3))), "dia")
                        act_st[d].wait(dve, i, "cum")
                        st.done(dve.tensor_tensor(b["QE"][:, :, :], HQ[:, :, ds(c * P, P)], b["EC"][:, :, :], ALU.mult), "qe")
                    for n in range(LEVELS):
                        for d in lanes:
                            b, c, st = B[d], chunk(i, d), dve_st[d]
                            act_st[d].wait(dve, i, f"e{n}")
                            if n >= 2:
                                pe_st[d].wait(dve, i, f"a{n - 2}")
                            x, e = b[f"X{n % 2}"][:, :, :], b[f"E{n % 2}"][:, :, :]
                            later = d == 0
                            q = HQ[:, :, ds(c * P, P)]
                            qv = q.rearrange("p h (b two a) -> p h b two a", two=2, a=1 << n)[:, :, :, int(later), :]
                            xv = x.rearrange("p h (b two a) -> p h b two a", two=2, a=1 << n)[:, :, :, int(later), :]
                            ev = e.rearrange("p h (b two a) -> p h b two a", two=2, a=1 << n)[:, :, :, int(later), :]
                            st.done(dve.tensor_tensor(xv, qv, ev, ALU.mult), f"xq{n}")
                            st.done(dve.tensor_tensor(halves(x, n, not later), halves(b["KT"][:, :, :], n, not later), halves(e, n, not later), ALU.mult), f"xk{n}")
                            if n:
                                pe_st[d].wait(dve, i, f"a{n - 1}")
                                st.wait(dve, i, f"a{n - 2}" if n > 1 else "dia")
                                pass_waits(dve, sems[8])
                                st.done(dve.copy_predicated(b["AT"][:, :, :], mask(PAIR + d * LEVELS + n - 1), per_head(bank(d, 2 + (n - 1) % 2))), f"a{n - 1}")
                    for d in lanes:
                        b, st, n = B[d], dve_st[d], LEVELS - 1
                        pe_st[d].wait(dve, i, f"a{n}")
                        st.wait(dve, i, f"a{n - 1}")
                        pass_waits(dve, sems[8])
                        st.done(dve.copy_predicated(b["AT"][:, :, :], mask(PAIR + d * LEVELS + n), per_head(bank(d, 2 + n % 2))), f"a{n}")
                    for d in lanes:
                        b, st = B[d], dve_st[d]
                        pe_st[d].wait(dve, i, "st")
                        for h in range(4):
                            st.done(dve.scalar_tensor_tensor(b["ST"][:, h, :], b["ST"][:, h, :], b["EC"][:, h, last_col[d]:last_col[d] + 1],
                                                             bank(d, 2)[:, h * P:(h + 1) * P], ALU.mult, ALU.add), f"st{h}")


def branch_pieces(A, l, raw, r, t):
    gates, branch = (A[n][ds(l, 1)].rearrange("l (k p) n -> p (l k) n", p=P) for n in ("w_in", ("w_branch_dn", "w_branch_hg")[r]))
    D = branch.shape[2]
    return [(raw[:, r, 0:8, :], gates[:, :, ds(t * P + (gates.shape[2] - (2 - r) * D), P)]), (raw[:, r, 8:12, :], branch[:, :, ds(t * P, P)])]


def branch_stage(nc, PS, l, A, H, ODN, OHG, M, new, early):
    pair, o_pair = split_pair(new), split_pair(new)
    SG, TMP = new("SG", [P, 4, 512]), new("TMP", [P, 2, 512])
    sources = tiles_of(H, 8) + tiles_of(ODN, 4) + tiles_of(OHG, 4)
    his, los = (tiles_of(h, 8) + tiles_of(o, 8) for h, o in zip(pair, o_pair))
    order = [(m, r, 2 * r + m) for m in range(2) for r in range(2)]
    D = M.shape[1] * P
    with stage(nc, "weights_hi", "weights_lo", "inputs_hi", "inputs_lo", "projected", "sigmoid_done", "vector_steps", also=early.loaded) as (
            hi_s, lo_s, in_hi, in_lo, proj_s, sig_s, dve_s):
        proj = Steps(proj_s, [f"{a}{j}" for _, _, j in order for a in "gb"])
        feed = Feed(new, early, hi_s, lo_s, lambda e, g, s: None, lambda g, s: (g + 1) * 32)
        sig = Steps(sig_s, [f"tile{j}" for _, _, j in order])
        dve_st = Steps(dve_s, ["dn0", "hg0", "sum0", "dn1", "hg1", "sum1"])
        with nc.Block() as block:

            @block.sync
            def _(sp):
                early.load_first(sp)
                with sp.Fori(1, D // P) as t:
                    for r in range(2):
                        feed.load(sp, t, r, branch_pieces(A, l, feed.raw, r, t))

            @block.tensor
            def _(pe):
                proj.open(pe)
                pe.wait_ge(in_lo, 16)
                with pe.Fori(0, D // UNIT) as g:
                    for m, r, j in order:
                        feed.ready(pe, g * 2 + m, r)
                        sig.wait_before(pe, g, f"tile{j}")
                        proj.done(product(pe, PS[:, j, :], feed.quads(r, 0, pair)), f"g{j}")
                        dve_st.wait_before(pe, g, ("dn0", "dn1", "hg0", "hg1")[j])
                        o = [part[:, 4 * r:4 * r + 4, :] for part in o_pair]
                        proj.done(product(pe, PS[:, 4 + j, :], feed.quads(r, 0, o, 8, 12)), f"b{j}")

            @block.scalar
            def _(act):
                sig.open(act)
                feed.hi_st.open(act)
                split_tiles_hi(act, sources, his, in_hi)
                feed.split_hi(act, 0, 0)
                feed.split_hi(act, 0, 1)

                def body(g, more):
                    for m, r, j in order:
                        proj.wait(act, g, f"g{j}")
                        dve_st.wait_before(act, g, ("dn0", "dn1", "hg0", "hg1")[j])
                        sig.done(act.activation(SG[:, j, :], PS[:, j, :], ACT.Sigmoid), f"tile{j}")
                        if more or m == 0:
                            proj.wait(act, g, f"b{j}")
                            feed.split_hi(act, g * 2 + (m + 1), r)

                turns(act, D // UNIT, body)

            @block.vector
            def _(dve):
                dve_st.open(dve)
                feed.lo_st.open(dve)
                split_tiles_lo(dve, sources, his, los, in_hi, in_lo)
                feed.split_lo(dve, 0, 0)
                feed.split_lo(dve, 0, 1)

                def body(g, more):
                    for m in range(2):
                        sig.wait(dve, g, f"tile{m}")
                        proj.wait(dve, g, f"b{m}")
                        dve_st.done(dve.tensor_tensor(tile(M, g * 2 + m), SG[:, m, :], PS[:, 4 + m, :], ALU.mult), f"dn{m}")
                        if more or m == 0:
                            feed.split_lo(dve, g * 2 + (m + 1), 0)
                        sig.wait(dve, g, f"tile{2 + m}")
                        proj.wait(dve, g, f"b{2 + m}")
                        dve_st.done(dve.tensor_tensor(TMP[:, m, :], SG[:, 2 + m, :], PS[:, 6 + m, :], ALU.mult), f"hg{m}")
                        dve_st.wait(dve, g, f"hg{m}")
                        dve_st.done(dve.tensor_tensor(tile(M, g * 2 + m), tile(M, g * 2 + m), TMP[:, m, :], ALU.add), f"sum{m}")
                        if more or m == 0:
                            feed.split_lo(dve, g * 2 + (m + 1), 1)

                turns(dve, D // UNIT, body)


def ffn_piece(A, l, raw, s, g):
    wl = A["w_up"][ds(l, 1)].rearrange("l (k p) n -> p (l k) n", p=P)
    return raw[:, s], wl[:, :, ds(g * UNIT + s * (wl.shape[2] // 2), UNIT)]


def ffn_up_stage(nc, PS, l, A, H, PAR, HID, new, early, next_early):
    F = A["w_down"].shape[1]
    T = F // UNIT
    GP, ACC = new("GP", [P, 2, 514]), new("ACC", [P, 2, 512])
    with stage(nc, "weights_hi", "weights_lo", "projected", "vector_steps", "silu_done", also=early.loaded) as (
            hi_s, lo_s, proj_s, dve_s, silu_s):
        proj = Steps(proj_s, [f"tile{j}" for j in range(4)])
        feed = Feed(new, early, hi_s, lo_s, after_step(proj, ["tile1", "tile3"]))
        dve_st = Steps(dve_s, [f"{a}{m}" for m in range(2) for a in ("kept", "tap0_", "tap1_", "tap2_")] + ["hid0", "hid1"])
        silu = Steps(silu_s, ["tile0", "tile1"])
        with nc.Block() as block:

            @block.sync
            def _(sp):
                early.load_first(sp)
                with sp.Fori(1, T) as g:
                    for s in range(2):
                        feed.load(sp, g, s, [ffn_piece(A, l, feed.raw, s, g)])
                next_early.load(sp)

            @block.tensor
            def _(pe):
                proj.open(pe)
                with pe.Fori(0, T) as g:
                    for j in range(4):
                        s, m = divmod(j, 2)
                        if m == 0:
                            feed.ready(pe, g, s)
                        dve_st.wait_before(pe, g, f"kept{m}" if s == 0 else f"hid{m}")
                        proj.done(product(pe, PS[:, j, :], feed.quads(s, m, H)), f"tile{j}")

            @block.vector
            def _(dve):
                dve_st.open(dve)
                feed.lo_st.open(dve)
                dve.memset(GP[:, :, 0:1], 0.0)
                dve.memset(GP[:, :, 513:514], 0.0)
                feed.split_lo(dve, 0, 0)
                feed.split_lo(dve, 0, 1)

                def body(g, more):
                    for m in range(2):
                        proj.wait(dve, g, f"tile{m}")
                        dve_st.done(dve.tensor_copy(GP[:, m, 1:513], PS[:, m, :]), f"kept{m}")
                        dve_st.wait(dve, g, f"kept{m}")
                        w = lambda tap: PAR[:, ds(g * 2 + (m + tap * 22), 1)]
                        silu.wait_before(dve, g, f"tile{m}")
                        dve_st.done(dve.tensor_scalar(ACC[:, m, :], GP[:, m, 0:512], w(0), w(3), ALU.mult, ALU.add), f"tap0_{m}")
                        for tap in (1, 2):
                            dve_st.wait(dve, g, f"tap{tap - 1}_{m}")
                            dve_st.done(dve.scalar_tensor_tensor(ACC[:, m, :], GP[:, m, tap:tap + 512], w(tap), ACC[:, m, :], ALU.mult, ALU.add), f"tap{tap}_{m}")
                    if more:
                        feed.split_lo(dve, g + 1, 0)
                    for m in range(2):
                        silu.wait(dve, g, f"tile{m}")
                        proj.wait(dve, g, f"tile{2 + m}")
                        t = tile(HID, g * 2 + m)
                        dve_st.done(dve.tensor_tensor(t, t, PS[:, 2 + m, :], ALU.mult), f"hid{m}")
                    if more:
                        feed.split_lo(dve, g + 1, 1)

                turns(dve, T, body)

            @block.scalar
            def _(act):
                silu.open(act)
                feed.hi_st.open(act)
                feed.split_hi(act, 0, 0)
                feed.split_hi(act, 0, 1)

                def body(g, more):
                    for m in range(2):
                        dve_st.wait(act, g, f"tap2_{m}")
                        silu.done(act.activation(tile(HID, g * 2 + m), ACC[:, m, :], ACT.Silu), f"tile{m}")
                        if more:
                            feed.split_hi(act, g + 1, m)

                turns(act, T, body)


GU, GV_, Q_, KC_, VC_, KS_, VS_, KW_, VW_, NG_, CA_, CB_, SB_, SC_, SH_ = (
    0, 256, 512, 768, 896, 1024, 1152, 1280, 1408, 1536, 1548, 1804, 2060, 2316, 2572)
KV, D_HEAD, N_CMP = 2, 64, 31
FINAL, NORM1, NORM2, BGATE, SCONV, CONFB, CLNG, CLNB, QG, KG, PE_ = 0, 8, 16, 24, 56, 62, 64, 66, 68, 69, 72


def second_proj_stage(nc, PS, A, H, b, new, early):
    whole = lambda col: [(0, col, UNIT)]
    twice = lambda col: [(0, col, 64), (64, col, 64), (P, col + 64, 64), (P + 64, col + 64, 64)]
    units = [whole(GU), whole(GV_), [(0, Q_, 64), (64, Q_ + P, 64), (P, Q_ + 64, 64), (P + 64, Q_ + P + 64, 64)],
             twice(KC_), twice(VC_),
             [(0, KS_, P), (P, KW_, P)], [(0, VS_, P), (P, VW_, P)], whole(CB_), whole(CA_), whole(SC_), whole(SH_), whole(SB_)]
    landed = [16 * sum(len(units[v]) for v in range(u % 2, u + 1, 2)) for u in range(len(units))]
    pair = split_pair(new)
    WNG = new("WNG", [P, 8, 12])

    products = ([(0, "act", f"gu{m}") for m in range(2)] + [(1, "act", f"gv{c}") for c in range(4)]
                + [(2, "dve", f"q{g}") for g in range(2)]
                + [(3, "dve", f"kc{h}") for h in range(2)] + [(4, "dve", f"vc{h}") for h in range(2)]
                + [(5, "dve", f"ks{m}") for m in range(2)] + [(6, "dve", f"vs{m}") for m in range(2)]
                + [(7, "act", f"cb{m}") for m in range(2)] + [(8, "dve", f"ca{m}") for m in range(2)]
                + [(9, "dve", f"sc{m}") for m in range(2)] + [(10, "dve", f"sh{m}") for m in range(2)]
                + [(11, "dve", f"sb{m}") for m in range(2)] + [(12, "act", "ng")])
    engine_of = {name: e for _, e, name in products}
    unit_of = {name: u for u, _, name in products}
    with stage(nc, "wng_in", "weights_hi", "weights_lo", "xn_hi", "xn_lo", "projected", "emptied_act", "emptied_dve", also=early.loaded) as (
            wng_in, hi_s, lo_s, x_hi, x_lo, proj_s, act_s, dve_s):
        proj = Steps(proj_s, [name for _, _, name in products])
        out_st = {"act": Steps(act_s, [n for _, e, n in products if e == "act"]),
                  "dve": Steps(dve_s, [n for _, e, n in products if e == "dve"])}
        wl = k_tiles(A["w_in_2"][0])
        bank_of = {name: n % 8 for n, (_, _, name) in enumerate(products)}
        last_of_unit = {u: name for u, _, name in products}

        def free(e, g, s):
            if g:
                e.wait_ge(proj.sem, proj.place[last_of_unit[2 * g - 2 + s]])

        feed = Feed(new, early, hi_s, lo_s, free, lambda g, s: landed[2 * g + s])

        def in_order(names, split, work):
            split(0, 0)
            split(0, 1)
            ahead = 2
            for name in names:
                while ahead < len(units) and ahead - 2 < unit_of[name]:
                    split(ahead // 2, ahead % 2)
                    ahead += 1
                work(name)

        with nc.Block() as block:

            @block.sync
            def _(sp):
                early.load_first(sp)
                for u, pieces in enumerate(units[2:], 2):
                    feed.load(sp, u // 2, u % 2, [(feed.raw[:, u % 2, :, at:at + n], wl[:, :, col:col + n]) for at, col, n in pieces])
                sp.dma_start(WNG[:, :, :], wl[:, :, NG_:NG_ + 12]).then_inc(wng_in, 16)

            @block.tensor
            def _(pe):
                pe.wait_ge(x_lo, 8)
                for n, (u, _, name) in enumerate(products):
                    s = u % 2
                    if n == 0 or products[n - 1][0] != u:
                        if u == len(units):
                            pe.wait_ge(wng_in, 16)
                        else:
                            feed.ready(pe, u // 2, s)
                    if n >= 8:
                        before = products[n - 8][2]
                        st = out_st[engine_of[before]]
                        pe.wait_ge(st.sem, st.place[before])
                    bank = PS[:, bank_of[name], :]
                    tokens = lambda k, c: H[:, k, c * P:(c + 1) * P]
                    if name[:2] == "gv":
                        c = int(name[2])
                        last = product(pe, bank[:, 0:UNIT], feed.token_quads(s, c, pair))
                    elif name[:2] == "vs":
                        for c in range(2):
                            last = product(pe, bank[:, c * UNIT:(c + 1) * UNIT], feed.token_quads(s, 2 * int(name[2]) + c, pair))
                    elif name == "ng":
                        for c in range(4):
                            last = contract(pe, bank[:, c * 12:(c + 1) * 12], [(tokens(k, c), WNG[:, k, :]) for k in range(8)])
                    else:
                        last = product(pe, bank, feed.quads(s, int(name[-1]), pair))
                    proj.done(last, name)

            def source(e, name):
                e.wait_ge(proj.sem, proj.place[name])
                return PS[:, bank_of[name], :]

            @block.scalar
            def _(act):
                feed.hi_st.open(act)
                split_tiles_hi(act, tiles_of(H, 8), tiles_of(pair[0], 8), x_hi)

                def work(name):
                    ps = source(act, name)
                    n = int(name[2]) if len(name) == 3 else 0
                    if name[:2] == "gu":
                        ins = act.activation(b["GU"][:, n, :], ps, ACT.Gelu_apprx_tanh)
                    elif name[:2] == "gv":
                        ins = act.activation(b["GV"][:, n, :], ps[:, 0:UNIT], ACT.Gelu_apprx_tanh)
                    elif name[:2] == "cb":
                        ins = act.activation(b["CB"][:, n, :], ps, ACT.Sigmoid)
                    else:
                        ins = act.activation(b["NG"][:, :, :].rearrange("p c n -> p (c n)"), ps[:, 0:48], ACT.Sigmoid)
                    out_st["act"].done(ins, name)

                in_order(out_st["act"].names, lambda g, s: feed.split_hi(act, g, s), work)

            @block.vector
            def _(dve):
                st = out_st["dve"]
                dve.memset(b["ZP"][:, :, 0:30], 0.0)
                dve.memset(b["SP"][:, :, 0:2], 0.0)
                feed.lo_st.open(dve)
                split_tiles_lo(dve, tiles_of(H, 8), tiles_of(pair[0], 8), tiles_of(pair[1], 8), x_hi, x_lo)

                def work(name):
                    ps = source(dve, name)
                    n = int(name[-1]) if name[-1].isdigit() else 0
                    if name[0] == "q":
                        ins = dve.tensor_copy(b["Q"][:, n, :], ps)
                    elif name[:2] in ("kc", "vc"):
                        dst = b["KC"][:, 2 * (name[0] == "v") + n, :]
                        dve.tensor_copy(dst[0:64, :], ps[0:64, :])
                        ins = dve.tensor_copy(dst[64:P, 0:511], ps[64:P, 1:512])
                    elif name[:2] == "ks":
                        ins = dve.tensor_copy(b["K"][:, n, :], ps)
                    elif name[:2] == "vs":
                        dst = b["V"][:, :, n * UNIT:(n + 1) * UNIT].rearrange("p v (c d) -> p c v d", d=P)
                        ins = dve.tensor_copy(dst, ps.rearrange("p (c v d) -> p c v d", c=2, d=P))
                    elif name[:2] == "ca":
                        dve.wait_ge(out_st["act"].sem, out_st["act"].place[f"cb{n}"])
                        ins = dve.tensor_tensor(b["ZP"][:, n, 30:542], b["CB"][:, n, :], ps, ALU.mult)
                    elif name[:2] == "sc":
                        ins = dve.tensor_copy(b["SC"][:, n, :], ps)
                    elif name[:2] == "sh":
                        if n == 0:
                            dve.wait_ge(st.sem, st.place["sc1"])
                        ins = dve.tensor_tensor(b["SP"][:, n, 2:514], b["SC"][:, n, :], ps, ALU.mult)
                    else:
                        ins = dve.tensor_copy(b["SBB"][:, n, :], ps)
                    st.done(ins, name)

                in_order(st.names, lambda g, s: feed.split_lo(dve, g, s), work)


def gmlp_stage(nc, PS, C, A, b, Y, new):
    WS, WST, BS, LG, LNB = new("WS", [P, 4, P]), new("WST", [P, 4, P]), new("BS", [1, 512]), new("LG", [P, UNIT]), new("LNB", [P, UNIT])
    ST, SQ = new("STAT", [P, 4, 4]), new("GSQ", [P, 4, UNIT])
    GV = b["GV"]
    with stage(nc, "ws_in", "bs_in", "ln_in", "vector_steps", "squares", "root", "turned", "mixed") as (
            ws_in, bs_in, ln_in, dve_s, sq_s, root_s, turn_s, mix_s):
        st = Steps(dve_s, ["mask", "sum", "mean"] + [f"cent{c}" for c in range(4)] + ["var", "eps", "inv", "wst"]
                   + [f"{a}{c}" for c in range(4) for a in ("norm", "v")] + ["y0", "y1"])
        own = lambda dve, name: dve.wait_ge(st.sem, st.place[name])
        with nc.Block() as block:

            @block.sync
            def _(sp):
                sp.dma_start(WS[:, :, :], A["gmlp_ws_2"][0].rearrange("g t s -> t g s")).then_inc(ws_in, 16)
                sp.dma_start(BS[:, :], A["gmlp_bs_2"].rearrange("l g t -> l (g t)")).then_inc(bs_in, 16)
                sp.dma_start(LG[:, :], A["gmlp_ln_g_2"][0].partition_broadcast(P)).then_inc(ln_in, 16)
                sp.dma_start(LNB[:, :], A["gmlp_ln_b_2"][0].partition_broadcast(P)).then_inc(ln_in, 16)

            @block.vector
            def _(dve):
                dve.wait_ge(ws_in, 16)
                st.done(dve.tensor_tensor(WS[:, :, :], WS[:, :, :], heads(C[:, INCL + 1, :], 4), ALU.mult), "mask")
                st.done(dve.tensor_reduce(ST[:, 0, :], GV[:, :, :], AX, ALU.add), "sum")
                own(dve, "sum")
                st.done(dve.tensor_scalar(ST[:, 0, :], ST[:, 0, :], 1.0 / UNIT, None, ALU.mult), "mean")
                own(dve, "mean")
                for c in range(4):
                    st.done(dve.tensor_scalar(GV[:, c, :], GV[:, c, :], ST[:, 0, c:c + 1], None, ALU.subtract), f"cent{c}")
                dve.wait_ge(sq_s, 1)
                st.done(dve.tensor_reduce(ST[:, 1, :], SQ[:, :, :], AX, ALU.add), "var")
                own(dve, "var")
                st.done(dve.tensor_scalar(ST[:, 1, :], ST[:, 1, :], 1.0 / UNIT, 1e-5, ALU.mult, ALU.add), "eps")
                own(dve, "eps")
                st.done(dve.reciprocal(ST[:, 1, :], ST[:, 1, :]), "inv")
                dve.wait_ge(turn_s, 1)
                st.done(dve.tensor_copy(WST[:, :, :], per_head(PS[:, 0, :])), "wst")
                dve.wait_ge(root_s, 1)
                dve.wait_ge(ln_in, 32)
                for c in range(4):
                    st.done(dve.scalar_tensor_tensor(GV[:, c, :], GV[:, c, :], ST[:, 2, c:c + 1], LG[:, :], ALU.mult, ALU.mult), f"norm{c}")
                    own(dve, f"norm{c}")
                    st.done(dve.tensor_tensor(GV[:, c, :], GV[:, c, :], LNB[:, :], ALU.add), f"v{c}")
                for m in range(2):
                    dve.wait_ge(mix_s, m + 1)
                    st.done(dve.tensor_tensor(Y[:, m, :], b["GU"][:, m, :], PS[:, 1 + m, :], ALU.mult), f"y{m}")

            @block.scalar
            def _(act):
                own(act, "cent3")
                act.activation(SQ[:, :, :], GV[:, :, :], ACT.Square).then_inc(sq_s, 1)
                own(act, "inv")
                act.activation(ST[:, 2, :], ST[:, 1, :], ACT.Sqrt).then_inc(root_s, 1)

            @block.tensor
            def _(pe):
                own(pe, "mask")
                for g in range(4):
                    last = pe.transpose(PS[:, 0, g * P:(g + 1) * P], WS[:, g, :], C[:, IDENT, :])
                last.then_inc(turn_s, 1)
                pe.wait_ge(bs_in, 16)
                own(pe, "v3")
                for m in range(2):
                    for half in range(2):
                        g = 2 * m + half
                        rows = slice(64 * half, 64 * half + 64)
                        for n in range(4):
                            last = contract(pe, PS[rows, 1 + m, n * P:(n + 1) * P],
                                            [(GV[:, n, g * 64:(g + 1) * 64], WST[:, g, :]),
                                             (C[0:1, ONES, 0:64], BS[0:1, g * P:(g + 1) * P])])
                    last.then_inc(mix_s, 1)


def conv_branches_stage(nc, PS, C, PAR, b, Y, RS):
    taps = 31
    ZP, SP = b["ZP"], b["SP"]
    par, conv = PAR[:, 0, :], PAR[:, 1, :]
    names = [f"z{t}_{m}" for t in range(taps) for m in range(2)] + [f"s{t}_{m}" for t in range(3) for m in range(2)]
    names += ["d0", "d1", "zc0", "zc1", "mean", "cent0", "cent1", "eps", "inv", "norm0", "norm1"]
    with stage(nc, "vector_steps", "sum_done", "squares", "sum_sq", "root", "out") as (dve_s, sum_s, sq_s, sumsq_s, root_s, out_s):
        st = Steps(dve_s, names)
        own = lambda e, name: e.wait_ge(st.sem, st.place[name])
        with nc.Block() as block:

            @block.vector
            def _(dve):
                acc = lambda m: PS[:, m, :]
                for t in range(taps):
                    for m in range(2):
                        src, w = ZP[:, m, t:t + 512], conv[:, t * 2 + m:t * 2 + m + 1]
                        if t == 0:
                            ins = dve.tensor_scalar(acc(m), src, w, par[:, CONFB + m:CONFB + m + 1], ALU.mult, ALU.add)
                        else:
                            own(dve, f"z{t - 1}_{m}")
                            ins = dve.scalar_tensor_tensor(acc(m), src, w, acc(m), ALU.mult, ALU.add)
                        st.done(ins, f"z{t}_{m}")
                for t in range(3):
                    for m in range(2):
                        src, w, a = SP[:, m, t:t + 512], par[:, SCONV + t * 2 + m:SCONV + t * 2 + m + 1], PS[:, 2 + m, :]
                        if t == 0:
                            ins = dve.tensor_scalar(a, src, w, None, ALU.mult)
                        else:
                            own(dve, f"s{t - 1}_{m}")
                            ins = dve.scalar_tensor_tensor(a, src, w, a, ALU.mult, ALU.add)
                        st.done(ins, f"s{t}_{m}")
                for m in range(2):
                    own(dve, f"s2_{m}")
                    st.done(dve.tensor_tensor(Y[:, 6 + m, :], b["SBB"][:, m, :], PS[:, 2 + m, :], ALU.mult), f"d{m}")
                for m in range(2):
                    own(dve, f"z{taps - 1}_{m}")
                    st.done(dve.tensor_copy(Y[:, 4 + m, :], acc(m)), f"zc{m}")
                dve.wait_ge(sum_s, 1)
                st.done(dve.tensor_scalar(RS[:, 0, :], PS[:, 4, :], 1.0 / UNIT, None, ALU.mult), "mean")
                own(dve, "mean")
                for m in range(2):
                    st.done(dve.tensor_tensor(Y[:, 4 + m, :], Y[:, 4 + m, :], RS[:, 0, :], ALU.subtract), f"cent{m}")
                dve.wait_ge(sumsq_s, 1)
                st.done(dve.tensor_scalar(RS[:, 1, :], PS[:, 5, :], 1.0 / UNIT, 1e-5, ALU.mult, ALU.add), "eps")
                own(dve, "eps")
                st.done(dve.reciprocal(RS[:, 1, :], RS[:, 1, :]), "inv")
                dve.wait_ge(root_s, 1)
                for m in range(2):
                    st.done(dve.scalar_tensor_tensor(Y[:, 4 + m, :], Y[:, 4 + m, :], par[:, CLNG + m:CLNG + m + 1], RS[:, 1, :], ALU.mult, ALU.mult), f"norm{m}")

            @block.scalar
            def _(act):
                for m in range(2):
                    own(act, f"cent{m}")
                    act.activation(ZP[:, m, 0:512], Y[:, 4 + m, :], ACT.Square).then_inc(sq_s, 1)
                own(act, "inv")
                act.activation(RS[:, 1, :], RS[:, 1, :], ACT.Sqrt).then_inc(root_s, 1)
                for m in range(2):
                    own(act, f"norm{m}")
                    act.activation(Y[:, 4 + m, :], Y[:, 4 + m, :], ACT.Silu, bias=par[:, CLNB + m:CLNB + m + 1]).then_inc(out_s, 1)

            @block.tensor
            def _(pe):
                own(pe, "zc1")
                contract(pe, PS[:, 4, :], [(C[:, ONES, :], Y[:, 4 + m, :]) for m in range(2)]).then_inc(sum_s, 1)
                pe.wait_ge(sq_s, 2)
                contract(pe, PS[:, 5, :], [(C[:, ONES, :], ZP[:, m, 0:512]) for m in range(2)]).then_inc(sumsq_s, 1)


def nsa_prep_stage(nc, PS, C, A, PAR, b, new):
    W1, W2 = new("W1", [P, 2, 16, P]), new("W2", [P, 2, D_HEAD])
    CW, HC = new("CW", [P, 2, 16, 2 * N_CMP]), new("HC", [P, 2, 2 * N_CMP])
    SQ, RI = new("NSQ", [P, 4, 512]), new("NRI", [P, 4, 512])
    KCM, KSQ, KRI = new("KCM0", [P, N_CMP]), new("KSQ", [P, N_CMP]), new("KRI", [P, N_CMP])
    par = PAR[:, 0, :]
    tiles = [(b["Q"][:, 0, :], QG), (b["Q"][:, 1, :], QG), (b["K"][:, 0, :], KG + 1), (b["K"][:, 1, :], KG + 2)]
    vnames = ([f"cw{t}_{j}" for t in range(2) for j in range(16)]
              + [f"mean{n}" for n in range(4)] + [f"norm{n}" for n in range(4)]
              + ["kc", "vc", "kmean", "kinv", "knorm"])
    with stage(nc, "w1k_in", "w1v_in", "w2_in", "vector_steps", "scalar_steps", "tensor_steps") as (w1k, w1v, w2_in, dve_s, act_s, pe_s):
        dve_st = Steps(dve_s, vnames)
        act_st = Steps(act_s, [f"sq{n}" for n in range(4)] + ["gelu0", "gelu1"] + [f"{a}{n}" for a in ("ln", "root") for n in range(4)] + ["ksq", "kroot"])
        pe_st = Steps(pe_s, [f"sum{n}" for n in range(4)] + ["hid0", "hid1", "kc", "vc", "ksum"])
        own = lambda e, st, name: e.wait_ge(st.sem, st.place[name])
        with nc.Block() as block:

            @block.sync
            def _(sp):
                for t, s in enumerate((w1k, w1v)):
                    sp.dma_start(W1[:, t], k_tiles(A["nsa_cmp_w1_2"][0][t])).then_inc(s, 16)
                sp.dma_start(W2[:, :, :], A["nsa_cmp_w2_2"][0].rearrange("t e d -> e t d")).then_inc(w2_in, 16)

            @block.scalar
            def _(act):
                for n, (x, _) in enumerate(tiles):
                    act_st.done(act.activation(SQ[:, n, :], x, ACT.Square), f"sq{n}")
                for t in range(2):
                    own(act, pe_st, f"hid{t}")
                    act_st.done(act.activation(HC[:, t, :], PS[:, 4 + t, 0:2 * N_CMP], ACT.Gelu_apprx_tanh), f"gelu{t}")
                for n in range(4):
                    own(act, dve_st, f"mean{n}")
                    act_st.done(act.activation(RI[:, n, :], RI[:, n, :], ACT.Ln), f"ln{n}")
                for n in range(4):
                    own(act, act_st, f"ln{n}")
                    act_st.done(act.activation(RI[:, n, :], RI[:, n, :], ACT.Exp, scale=-0.5), f"root{n}")
                own(act, dve_st, "kc")
                act_st.done(act.activation(KSQ[:, :], KCM[:, :], ACT.Square), "ksq")
                own(act, dve_st, "kinv")
                act_st.done(act.activation(KRI[:, :], KRI[:, :], ACT.Sqrt), "kroot")

            @block.tensor
            def _(pe):
                for n in range(4):
                    own(pe, act_st, f"sq{n}")
                    pe_st.done(pe.matmul(PS[:, n, :], C[:, BLOCK64, :], SQ[:, n, :], start=True, stop=True), f"sum{n}")
                for t, s in enumerate((w1k, w1v)):
                    pe.wait_ge(s, 16)
                    own(pe, dve_st, f"cw{t}_15")
                    pe_st.done(contract(pe, PS[:, 4 + t, 0:2 * N_CMP], [(W1[:, t, j, :], CW[:, t, j, :]) for j in range(16)]), f"hid{t}")
                pe.wait_ge(w2_in, 16)
                own(pe, act_st, "gelu0")
                for h in range(KV):
                    last = pe.matmul(PS[64 * h:64 * h + 64, 6, 0:N_CMP], W2[:, 0, :], HC[:, 0, h * N_CMP:(h + 1) * N_CMP], start=True, stop=True)
                pe_st.done(last, "kc")
                own(pe, act_st, "gelu1")
                for h in range(KV):
                    last = pe.matmul(PS[0:N_CMP, 7, h * D_HEAD:(h + 1) * D_HEAD], HC[:, 1, h * N_CMP:(h + 1) * N_CMP], W2[:, 1, :], start=True, stop=True)
                pe_st.done(last, "vc")
                own(pe, act_st, "ksq")
                pe_st.done(pe.matmul(PS[:, 4, 0:N_CMP], C[:, BLOCK64, :], KSQ[:, :], start=True, stop=True), "ksum")

            @block.vector
            def _(dve):
                for t in range(2):
                    for j in range(16):
                        src = b["KC"][:, 2 * t:2 * t + 2, 2 * j:2 * j + 16 * (N_CMP - 1) + 1:16]
                        dst = CW[:, t, j, :].rearrange("p (h n) -> p h n", h=KV)
                        dve_st.done(dve.tensor_scalar(dst, src, par[:, PE_ + 16 * t + j:PE_ + 16 * t + j + 1], None, ALU.add), f"cw{t}_{j}")
                for n in range(4):
                    own(dve, pe_st, f"sum{n}")
                    dve_st.done(dve.tensor_scalar(RI[:, n, :], PS[:, n, :], 1.0 / D_HEAD, 1e-6, ALU.mult, ALU.add), f"mean{n}")
                for n, (x, g) in enumerate(tiles):
                    own(dve, act_st, f"root{n}")
                    dve_st.done(dve.scalar_tensor_tensor(x, x, par[:, g:g + 1], RI[:, n, :], ALU.mult, ALU.mult), f"norm{n}")
                own(dve, pe_st, "kc")
                dve_st.done(dve.tensor_copy(KCM[:, :], PS[:, 6, 0:N_CMP]), "kc")
                own(dve, pe_st, "vc")
                dve_st.done(dve.tensor_copy(b["VCM"][0:N_CMP, :], PS[0:N_CMP, 7, 0:P]), "vc")
                own(dve, pe_st, "ksum")
                dve_st.done(dve.tensor_scalar(KRI[:, :], PS[:, 4, 0:N_CMP], 1.0 / D_HEAD, 1e-6, ALU.mult, ALU.add), "kmean")
                own(dve, dve_st, "kmean")
                dve_st.done(dve.reciprocal(KRI[:, :], KRI[:, :]), "kinv")
                own(dve, act_st, "kroot")
                dve_st.done(dve.scalar_tensor_tensor(b["KCM"][:, :], KCM[:, :], par[:, KG:KG + 1], KRI[:, :], ALU.mult, ALU.mult), "knorm")


def attention_stage(nc, PS, C, b, Y, new):
    H4 = 4
    scale = D_HEAD ** -0.5
    PR, PT = [new(f"PR{n}", [P, H4, 512]) for n in range(2)], [new(f"PT{n}", [P, 512]) for n in range(2)]
    MX, SU, CO = new("MX", [P, 2, H4]), new("SU", [P, 2, H4]), new("CO", [P, 2, H4])
    OA = new("OA", [P, 2, H4 * D_HEAD])
    items = [(c, br) for c in range(4) for br in range(3)]
    keys = lambda c, br: N_CMP if br == 0 else P * (c + 1)
    blocks = lambda c, br: 1 if br == 0 else c + 1
    anames, vnames = [], []
    for i, (c, br) in enumerate(items):
        anames += [f"exp{i}_{h}" for h in range(H4)]
        vnames += [f"mask{i}", f"max{i}", f"neg{i}"] + ([f"valid{i}"] if br == 0 else []) + [f"pt{i}_{h}" for h in range(H4)]
        vnames += [f"inv{i}", f"coef{i}"] + [f"out{i}_{h}" for h in range(H4)]
    order = ["s0"]
    for i, (c, br) in enumerate(items):
        for h in range(H4):
            order.append(f"t{i}_{h}")
            if h:
                order.append(f"o{i}_{h - 1}")
            if h == H4 - 1 and i + 1 < len(items):
                order.append(f"s{i + 1}")
        order.append(f"o{i}_{H4 - 1}")
        if br == 2 :
            order.append(f"y{c}")
    with stage(nc, "tensor_steps", "scalar_steps", "vector_steps", "y_kept") as (pe_s, act_s, dve_s, y_s):
        pe_st, act_st, dve_st = Steps(pe_s, order), Steps(act_s, anames), Steps(dve_s, vnames)
        own = lambda e, st, name: e.wait_ge(st.sem, st.place[name])

        def scores_of(i):
            c, br = items[i]
            return PS[:, 0:H4, 0:keys(c, br)]

        with nc.Block() as block:

            @block.tensor
            def _(pe):
                def scores(i):
                    c, br = items[i]
                    if i:
                        own(pe, act_st, f"exp{i - 1}_{H4 - 1}")
                    for hh in range(H4):
                        h, g = divmod(hh, 2)
                        rows = slice(64 * h, 64 * h + 64)
                        q = b["Q"][rows, g, c * P:(c + 1) * P]
                        k = b["KCM"][rows, :] if br == 0 else b["K"][rows, br - 1, 0:keys(c, br)]
                        last = pe.matmul(scores_of(i)[:, hh, :], q, k, start=True, stop=True)
                    pe_st.done(last, f"s{i}")

                def turn(i, hh):
                    c, br = items[i]
                    own(pe, dve_st, f"valid{i}") if br == 0 else own(pe, act_st, f"exp{i}_{hh}")
                    n = i * H4 + hh
                    if n >= 2:
                        j, k = divmod(n - 2, H4)
                        own(pe, dve_st, f"pt{j}_{k}")
                    for j in range(blocks(c, br)):
                        w = min(P, keys(c, br))
                        last = pe.transpose(PS[0:w, 4 + hh % 2, j * P:(j + 1) * P], PR[i % 2][:, hh, j * P:j * P + w], C[:, IDENT, :])
                    pe_st.done(last, f"t{i}_{hh}")

                def output(i, hh):
                    c, br = items[i]
                    h = hh // 2
                    own(pe, dve_st, f"pt{i}_{hh}")
                    w = min(P, keys(c, br))
                    v = lambda j: b["VCM"][0:w, h * 64:(h + 1) * 64] if br == 0 else b["V"][:, br - 1, j * P + h * 64:j * P + (h + 1) * 64]
                    pe_st.done(contract(pe, PS[:, 6, hh * 64:(hh + 1) * 64],
                                        [(PT[hh % 2][0:w, j * P:(j + 1) * P], v(j)) for j in range(blocks(c, br))]), f"o{i}_{hh}")

                scores(0)
                for i, (c, br) in enumerate(items):
                    for hh in range(H4):
                        turn(i, hh)
                        if hh == 1 and i:
                            own(pe, dve_st, f"out{i - 1}_{H4 - 1}")
                        if hh:
                            output(i, hh - 1)
                        if hh == H4 - 1 and i + 1 < len(items):
                            scores(i + 1)
                    output(i, H4 - 1)
                    if br == 2:
                        own(pe, dve_st, f"out{i}_{H4 - 1}")
                        if c:
                            pe.wait_ge(y_s, c)
                        for m in range(2):
                            last = pe.transpose(PS[:, 7, m * P:(m + 1) * P], OA[:, c % 2, m * P:(m + 1) * P], C[:, IDENT, :])
                        pe_st.done(last, f"y{c}")

            @block.scalar
            def _(act):
                for i, (c, br) in enumerate(items):
                    own(act, dve_st, f"neg{i}")
                    if i >= 2:
                        own(act, pe_st, f"t{i - 2}_{H4 - 1}")
                    for hh in range(H4):
                        act_st.done(act.activation(PR[i % 2][:, hh, 0:keys(c, br)], scores_of(i)[:, hh, :], ACT.Exp, scale=scale,
                                                   bias=MX[:, i % 2, hh:hh + 1], accum_out=SU[:, i % 2, hh:hh + 1]), f"exp{i}_{hh}")
                    if br == 2:
                        act.wait_ge(pe_st.sem, pe_st.place[f"y{c}"])
                        act.copy(Y[:, 2:4, c * P:(c + 1) * P], PS[:, 7, 0:2 * P].rearrange("p (m n) -> p m n", m=2)).then_inc(y_s, 1)

            @block.vector
            def _(dve):
                for i, (c, br) in enumerate(items):
                    own(dve, pe_st, f"s{i}")
                    s = scores_of(i)
                    if br == 0:
                        part, mask = s, C[:, CMP_ADD, c * 32:c * 32 + N_CMP]
                    else:
                        part, mask = s[:, :, c * P:(c + 1) * P], C[:, CAUSAL, :]
                    dve_st.done(dve.tensor_tensor(part, part, heads(mask, H4), ALU.add), f"mask{i}")
                    own(dve, dve_st, f"mask{i}")
                    dve_st.done(dve.tensor_reduce(MX[:, i % 2, :], s, AX, ALU.max), f"max{i}")
                    own(dve, dve_st, f"max{i}")
                    dve_st.done(dve.tensor_scalar(MX[:, i % 2, :], MX[:, i % 2, :], -scale, None, ALU.mult), f"neg{i}")
                    if br == 0:
                        own(dve, act_st, f"exp{i}_{H4 - 1}")
                        pr = PR[i % 2][:, :, 0:N_CMP]
                        dve_st.done(dve.tensor_tensor(pr, pr, heads(C[:, CMP_OK, c * 32:c * 32 + N_CMP], H4), ALU.mult), f"valid{i}")
                    for hh in range(H4):
                        own(dve, pe_st, f"t{i}_{hh}")
                        w = min(P, keys(c, br))
                        n = blocks(c, br) * P
                        dve_st.done(dve.tensor_copy(PT[hh % 2][0:w, 0:n], PS[0:w, 4 + hh % 2, 0:n]), f"pt{i}_{hh}")
                    dve_st.done(dve.reciprocal(CO[:, i % 2, :], SU[:, i % 2, :]), f"inv{i}")
                    own(dve, dve_st, f"inv{i}")
                    gate = b["NG"][:, c, :].rearrange("p (h r) -> p h r", r=3)[:, :, br]
                    dve_st.done(dve.tensor_tensor(CO[:, i % 2, :], CO[:, i % 2, :], gate, ALU.mult), f"coef{i}")
                    own(dve, dve_st, f"coef{i}")
                    own(dve, pe_st, f"o{i}_{H4 - 1}")
                    for hh in range(H4):
                        o, ps, co = OA[:, c % 2, hh * 64:(hh + 1) * 64], PS[:, 6, hh * 64:(hh + 1) * 64], CO[:, i % 2, hh:hh + 1]
                        if br == 0:
                            ins = dve.tensor_scalar(o, ps, co, None, ALU.mult)
                        else:
                            ins = dve.scalar_tensor_tensor(o, ps, co, o, ALU.mult, ALU.add)
                        dve_st.done(ins, f"out{i}_{hh}")


def gate_pieces(A, raw, n, t):
    gates, branch = k_tiles(A["w_gate_2"][0]), k_tiles(A["w_branch_2"][0][n])
    return [(raw[:, n % 2, 0:8, :], gates[:, :, ds(t * P + n * branch.shape[2], P)]), (raw[:, n % 2, 8:10, :], branch[:, :, ds(t * P, P)])]


def gate_stage(nc, PS, A, H, PAR, Y, M, new, early, next_early):
    pair, y_pair = split_pair(new), split_pair(new)
    SG, TMP = new("SG", [P, 4, 512]), new("TMP", [P, 3, 512])
    sources = tiles_of(H, 8) + tiles_of(Y, 8)
    his, los = (tiles_of(h, 8) + tiles_of(y, 8) for h, y in zip(pair, y_pair))
    D = M.shape[1] * P
    js = [(n, m) for m in range(2) for n in range(4)]
    with stage(nc, "weights_hi", "weights_lo", "inputs_hi", "inputs_lo", "projected", "sigmoid_done", "vector_steps", also=early.loaded) as (
            hi_s, lo_s, in_hi, in_lo, proj_s, sig_s, dve_s):
        proj = Steps(proj_s, [f"{a}{n}_{m}" for n, m in js for a in "gb"])
        sig = Steps(sig_s, [f"{n}_{m}" for n, m in js])
        dve_st = Steps(dve_s, [x for n, m in js for x in ([f"m{n}_{m}"] if n == 0 else [f"m{n}_{m}", f"s{n}_{m}"])])
        feed = Feed(new, early, hi_s, lo_s, lambda e, g, s: None, lambda g, s: (g + 1) * 32)
        turn = lambda g, n, m: g * 4 + (2 * m + n // 2)
        with nc.Block() as block:

            @block.sync
            def _(sp):
                early.load_first(sp)
                for n in (2, 3):
                    feed.load(sp, 1, n % 2, gate_pieces(A, feed.raw, n, 0))
                with sp.Fori(1, D // P) as t:
                    for n in range(4):
                        feed.load(sp, t * 2 + n // 2, n % 2, gate_pieces(A, feed.raw, n, t))
                next_early.load(sp)

            @block.tensor
            def _(pe):
                proj.open(pe)
                pe.wait_ge(in_lo, 16)
                with pe.Fori(0, D // UNIT) as g:
                    for n, m in js:
                        r = n % 2
                        j = 2 * r + m
                        feed.ready(pe, turn(g, n, m), r)
                        if n >= 2:
                            sig.wait(pe, g, f"{n - 2}_{m}")
                        else:
                            sig.wait_before(pe, g, f"{n + 2}_{m}")
                        proj.done(product(pe, PS[:, j, :], feed.quads(r, 0, pair)), f"g{n}_{m}")
                        if n >= 2:
                            dve_st.wait(pe, g, f"m{n - 2}_{m}")
                        else:
                            dve_st.wait_before(pe, g, f"m{n + 2}_{m}")
                        proj.done(product(pe, PS[:, 4 + j, :], feed.quads(r, 0, [part[:, 2 * n:2 * n + 2, :] for part in y_pair], 8, 10)), f"b{n}_{m}")

            @block.scalar
            def _(act):
                sig.open(act)
                feed.hi_st.open(act)
                split_tiles_hi(act, sources, his, in_hi)
                feed.split_hi(act, 0, 0)
                feed.split_hi(act, 0, 1)

                def body(g, more):
                    for n, m in js:
                        j = 2 * (n % 2) + m
                        proj.wait(act, g, f"g{n}_{m}")
                        if n >= 2:
                            dve_st.wait(act, g, f"m{n - 2}_{m}")
                        else:
                            dve_st.wait_before(act, g, f"m{n + 2}_{m}")
                        bias = PAR[:, 0, ds(g * 2 + (BGATE + n * 8 + m), 1)]
                        sig.done(act.activation(SG[:, j, :], PS[:, j, :], ACT.Sigmoid, bias=bias), f"{n}_{m}")
                        if more or m == 0 or n < 2:
                            proj.wait(act, g, f"b{n}_{m}")
                            feed.split_hi(act, turn(g, n + 2, m), n % 2)

                turns(act, D // UNIT, body)

            @block.vector
            def _(dve):
                dve_st.open(dve)
                feed.lo_st.open(dve)
                split_tiles_lo(dve, sources, his, los, in_hi, in_lo)
                feed.split_lo(dve, 0, 0)
                feed.split_lo(dve, 0, 1)

                def body(g, more):
                    for n, m in js:
                        j = 2 * (n % 2) + m
                        sig.wait(dve, g, f"{n}_{m}")
                        proj.wait(dve, g, f"b{n}_{m}")
                        dst = tile(M, g * 2 + m)
                        if n == 0:
                            dve_st.done(dve.tensor_tensor(dst, SG[:, j, :], PS[:, 4 + j, :], ALU.mult), f"m{n}_{m}")
                        else:
                            dve_st.done(dve.tensor_tensor(TMP[:, n - 1, :], SG[:, j, :], PS[:, 4 + j, :], ALU.mult), f"m{n}_{m}")
                            dve_st.wait(dve, g, f"m{n}_{m}")
                            dve_st.done(dve.tensor_tensor(dst, dst, TMP[:, n - 1, :], ALU.add), f"s{n}_{m}")
                        if more or m == 0 or n < 2:
                            feed.split_lo(dve, turn(g, n + 2, m), n % 2)

                turns(dve, D // UNIT, body)


def mlp_up_stage(nc, PS, A, H, HID, new, early):
    T = HID.shape[1] // 4
    with stage(nc, "weights_hi", "weights_lo", "projected", "relu_done", "squared", also=early.loaded) as (
            hi_s, lo_s, proj_s, relu_s, sq_s):
        names = [f"tile{j}" for j in range(4)]
        proj, relu, sq = Steps(proj_s, names), Steps(relu_s, names), Steps(sq_s, names)
        feed = Feed(new, early, hi_s, lo_s, after_step(proj, ["tile1", "tile3"]))
        wl = k_tiles(A["w_mlp1_2"][0])
        with nc.Block() as block:

            @block.sync
            def _(sp):
                early.load_first(sp)
                with sp.Fori(1, T) as g:
                    for s in range(2):
                        feed.load(sp, g, s, [(feed.raw[:, s], wl[:, :, ds(g * 2 * UNIT + s * UNIT, UNIT)])])

            @block.tensor
            def _(pe):
                proj.open(pe)
                with pe.Fori(0, T) as g:
                    for j in range(4):
                        s, m = divmod(j, 2)
                        if m == 0:
                            feed.ready(pe, g, s)
                        relu.wait_before(pe, g, f"tile{j}")
                        proj.done(product(pe, PS[:, j, :], feed.quads(s, m, H)), f"tile{j}")

            @block.vector
            def _(dve):
                relu.open(dve)
                feed.lo_st.open(dve)
                feed.split_lo(dve, 0, 0)
                feed.split_lo(dve, 0, 1)

                def body(g, more):
                    for s in range(2):
                        for j in (2 * s, 2 * s + 1):
                            proj.wait(dve, g, f"tile{j}")
                            relu.done(dve.tensor_scalar(tile(HID, g * 4 + j), PS[:, j, :], 0.0, None, ALU.max), f"tile{j}")
                        if more:
                            feed.split_lo(dve, g + 1, s)

                turns(dve, T, body)

            @block.scalar
            def _(act):
                feed.hi_st.open(act)
                feed.split_hi(act, 0, 0)
                feed.split_hi(act, 0, 1)

                def body(g, more):
                    for s in range(2):
                        for j in (2 * s, 2 * s + 1):
                            relu.wait(act, g, f"tile{j}")
                            t = tile(HID, g * 4 + j)
                            sq.done(act.activation(t, t, ACT.Square), f"tile{j}")
                        if more:
                            feed.split_hi(act, g + 1, s)

                turns(act, T, body)


def store_stage(nc, PS, C, X, H, out):
    S = X.shape[2]
    D = out.shape[1]
    T, K = S // P, D // P
    with stage(nc, "turned", "kept", "written") as (turned, kept, written):
        rows = H[:, :, :].rearrange("p k n -> p (k n)").rearrange("p (c f) -> p c f", c=T)
        with nc.Block() as block:

            @block.tensor
            def _(pe):
                for c in range(T):
                    for half in range(2):
                        for k in range(4):
                            last = pe.transpose(PS[:, 2 * c + half, k * P:(k + 1) * P], X[:, 4 * half + k, c * P:(c + 1) * P], C[:, IDENT, :])
                        last.then_inc(turned, 1)

            @block.vector
            def _(dve):
                for c in range(T):
                    for half in range(2):
                        dve.wait_ge(turned, 2 * c + half + 1)
                        dve.tensor_copy(rows[:, c, half * 512:(half + 1) * 512], PS[:, 2 * c + half, :]).then_inc(kept, 1)

            @block.sync
            def _(sp):
                for c in range(T):
                    sp.wait_ge(kept, 2 * c + 2)
                    sp.dma_start(out[c * P:(c + 1) * P, :], rows[:, c, :]).then_inc(written, 16)
                sp.wait_ge(written, 16 * T)


def second_block(nc, PS, C, A, X, H, PAR, ROWS, RS, new_in, dump, out):
    flat = lambda t: t[:, :, :].rearrange("p a n -> p (a n)")
    vec = lambda n: A[n].rearrange("l (m p) -> (l m) p", p=P)
    loads = [(FINAL, A["final_norm"].rearrange("(m p) -> m p", p=P)), (NORM1, vec("norm1_g_2")), (NORM2, vec("norm2_g_2")),
             (BGATE, vec("b_gate_2")), (SCONV, A["sconv_w_2"][0].rearrange("t (m p) -> (t m) p", p=P)),
             (CONFB, vec("conf_conv_b_2")), (CLNG, vec("conf_ln_g_2")), (CLNB, vec("conf_ln_b_2")),
             (PE_, A["nsa_cmp_pe_2"][0].rearrange("t (j a) d -> (t j) (a d)", a=2)),
             (P, A["conf_conv_w_2"][0].rearrange("t (m p) -> (t m) p", p=P))]
    extra = []
    for half in range(2):
        cols = slice(64 * half, 64 * half + 64)
        extra += [(ROWS[QG:QG + 1, 0, cols], A["nsa_q_norm_g_2"]), (ROWS[KG:KG + 3, 0, cols], A["nsa_k_norm_g_2"][0])]
    params_stage(nc, PS, C, ROWS, PAR, loads, 2, extra)
    par = PAR[:, 0, :]
    for dst, first in ((X, FINAL), (H, NORM1)):
        with ExitStack() as w:
            rms_stage(nc, PS, C, X, dst, par[:, first:first + 8], RS[:, 0, :], 1e-6, new_in(w), split=False)
    dump("xn", flat(H))
    with ExitStack() as mid:
        new = new_in(mid)
        Y = new("Y", [P, 8, 512])
        with ExitStack() as br:
            new = new_in(br)
            b = {n: new(n, s) for n, s in dict(
                GU=[P, 2, 512], GV=[P, 4, UNIT], Q=[P, 2, 512], KC=[P, 4, 512], K=[P, 2, 512], V=[P, 2, 512], CB=[P, 2, 512],
                ZP=[P, 2, 542], SC=[P, 2, 512], SP=[P, 2, 514], SBB=[P, 2, 512], NG=[P, 4, 12], KCM=[P, N_CMP], VCM=[P, P]).items()}
            with ExitStack() as w:
                new = new_in(w)
                early = Early(nc, w, new, 8, UNIT, lambda raw, s: [(raw[:, s], k_tiles(A["w_in_2"][0])[:, :, (GU, GV_)[s]:(GU, GV_)[s] + UNIT])])
                second_proj_stage(nc, PS, A, H, b, new, early)
            with ExitStack() as w:
                gmlp_stage(nc, PS, C, A, b, Y, new_in(w))
            conv_branches_stage(nc, PS, C, PAR, b, Y, RS)
            with ExitStack() as w:
                nsa_prep_stage(nc, PS, C, A, PAR, b, new_in(w))
            with ExitStack() as w:
                attention_stage(nc, PS, C, b, Y, new_in(w))
        dump("y", flat(Y))
        new = new_in(mid)
        M = new("M", [P, 8, 512])
        slabs = early_slabs(nc, mid, new, A["w_out_2"][0])
        with ExitStack() as w:
            new = new_in(w)
            early = Early(nc, w, new, 10, P, lambda raw, s: gate_pieces(A, raw, s, 0))
            gate_stage(nc, PS, A, H, PAR, Y, M, new, early, slabs)
        dump("mixed", flat(M))
        with ExitStack() as w:
            slab_stage(nc, PS, A["w_out_2"][0], M, X, new_in(w), slabs)
    dump("x1", flat(X))
    with ExitStack() as ffn:
        new = new_in(ffn)
        HID = new("HID", [P, 32, 512])
        with ExitStack() as w:
            new = new_in(w)
            early = Early(nc, w, new, 8, UNIT, lambda raw, s: [(raw[:, s], k_tiles(A["w_mlp1_2"][0])[:, :, s * UNIT:(s + 1) * UNIT])])
            pair = split_pair(new)
            with ExitStack() as w2:
                rms_stage(nc, PS, C, X, pair, par[:, NORM2:NORM2 + 8], RS[:, 0, :], 1e-6, new_in(w2), early=early)
            mlp_up_stage(nc, PS, A, pair, HID, new, early)
        with ExitStack() as w:
            new = new_in(w)
            slab_stage(nc, PS, A["w_mlp2_2"][0], HID, X, new, early_slabs(nc, w, new, A["w_mlp2_2"][0]))
    store_stage(nc, PS, C, X, H, out)


def params_stage(nc, PS, C, ROWS, PAR, loads, n_tiles, extra=()):
    with stage(nc, "cleared", "rows_in", "turned", "kept") as (cleared, rows_in, turned, kept):
        with nc.Block() as block:

            @block.sync
            def _(sp):
                sp.wait_ge(cleared, 1)
                for at, src in loads:
                    n = src.shape[0]
                    sp.dma_start(ROWS[at % P:at % P + n, at // P, :], src).then_inc(rows_in, 16)
                for dst, src in extra:
                    sp.dma_start(dst, src).then_inc(rows_in, 16)
                sp.wait_ge(rows_in, 16 * (len(loads) + len(extra)))

            @block.tensor
            def _(pe):
                pe.wait_ge(rows_in, 16 * (len(loads) + len(extra)))
                for n in range(n_tiles):
                    pe.transpose(PS[:, n, 0:P], ROWS[:, n, :], C[:, IDENT, :]).then_inc(turned, 1)

            @block.vector
            def _(dve):
                dve.memset(ROWS[:, :, :], 0.0).then_inc(cleared, 1)
                dve.wait_ge(turned, n_tiles)
                dve.tensor_copy(PAR[:, :, :], PS[:, 0:n_tiles, 0:P]).then_inc(kept, 1)


def at_layer(ap, l):
    axes = " ".join(f"d{n}" for n in range(1, len(ap.shape)))
    first, rest = axes.split(" ", 1) if " " in axes else (axes, "")
    return ap[ds(l, 1)].rearrange(f"l {axes} -> (l {first}) {rest}")


def build(nc, A, out, dumps=None):
    S, D = A["x"].shape[1:]
    K = D // P
    with ExitStack() as top:
        named = {}

        def new_in(ctx):
            def new(name, shape, dt=F32):
                named[name] = named.get(name, 0) + 1
                return ctx.enter_context(nc.sbuf_tensor(f"{name}_{named[name]}", shape, dt))
            return new

        new = new_in(top)
        PS = top.enter_context(nc.psum_tensor("PS", [P, 8, 512], F32))
        C = new("C", [P, N_CONST, P])
        X = new("X", [P, K, S])
        H = new("H", [P, K, S])
        PAR = new("PAR", [P, 2, P])
        ROWS = new("ROWS", [P, 2, P])
        SMALL = new("SMALL", [P, 32])
        RS = new("RS", [P, 2, S])

        def dump(name, ap, l=None):
            if name in (dumps or {}):
                with stage(nc, "dump") as (s,):
                    with nc.Block() as block:
                        @block.sync
                        def _(sp):
                            dst = dumps[name] if l is None else dumps[name][ds(l, 1)].rearrange("l p n -> (l p) n")
                            sp.dma_start(dst, ap).then_inc(s, 16)
                            sp.wait_ge(s, 16)

        with stage(nc, "consts_in") as (consts_in,):
            with nc.Block() as block:

                @block.sync
                def _(sp):
                    sp.dma_start(C[:, :, :], A["consts"]).then_inc(consts_in, 16)
                    sp.wait_ge(consts_in, 16)

        load_norm_stage(nc, PS, C, A["x"].rearrange("b s d -> (b s) d"), X, H)
        mixer_layers(nc, PS, C, A, X, H, PAR, ROWS, SMALL, RS, new_in, dump)
        second_block(nc, PS, C, A, X, H, PAR, ROWS, RS, new_in, dump, out.rearrange("b s d -> (b s) d"))


MIX, FFN, DNN, HGN, BIAS = 60, 68, 76, 77, 66


def mixer_layers(nc, PS, C, A, X, H, PAR, ROWS, SMALL, RS, new_in, dump):
    flat = lambda t: t[:, :, :].rearrange("p a n -> p (a n)")
    with nc.Fori(0, A["w_in"].shape[0]) as l:
        conv = at_layer(A["dn_conv"], l).rearrange("j (m p) -> (j m) p", p=P)
        fconv = at_layer(A["ffn_conv"], l).rearrange("j (m p) -> (j m) p", p=P)
        row = lambda n: A[n][ds(l, 1)].rearrange("l (m p) -> (l m) p", p=P)
        w_in_l = A["w_in"][ds(l, 1)].rearrange("l (k p) n -> p (l k) n", p=P)
        bc = lambda n: A[n][ds(l, 1)].rearrange("l a b -> l (a b)").rearrange("l n -> (l n)").partition_broadcast(P)
        params_stage(nc, PS, C, ROWS, PAR,
                     [(0, conv), (MIX, row("mix_norm")), (FFN, row("ffn_norm")), (DNN, row("dn_norm")), (HGN, row("hg_norm")),
                      (P, fconv), (P + BIAS, row("ffn_conv_bias"))], 2,
                     [(SMALL[:, 0:8], bc("dn_a_log")), (SMALL[:, 8:16], bc("dn_dt_bias")),
                      (SMALL[:, 16:17], A["layer"][ds(l, 1)].partition_broadcast(P))])
        with ExitStack() as mix:
            new = new_in(mix)
            ODN = new("ODN", [P, 4, 512])
            with ExitStack() as dn:
                new = new_in(dn)
                O2 = new("O2", [P, 8, 512])
                QKV = new("QKV", [P, 12, 516])
                Z = new("Z", [P, 4, 512])
                BA = new("BA", [P, 4, 16])
                with ExitStack() as w:
                    new = new_in(w)
                    early = Early(nc, w, new, 8, UNIT, lambda raw, s: [(raw[:, s], w_in_l[:, :, s * UNIT:(s + 1) * UNIT])])
                    with ExitStack() as w2:
                        rms_stage(nc, PS, C, X, H, PAR[:, 0, MIX:MIX + 8], RS[:, 0, :], 1e-6, new_in(w2), split=False, early=early)
                    dump("h", flat(H), l)
                    CONV = new("CONV", [P, 2, 512])
                    WBA = new("WBA", [P, 8, 16])
                    qkv_stage(nc, PS, C, A, l, A["w_in"], H, QKV, CONV, Z, WBA, BA, PAR[:, 0, :], new, early)
                dump("qkv", flat(QKV), l)
                dump("z", flat(Z), l)
                with ExitStack() as w:
                    new = new_in(w)
                    KTOK = new("KTOK", [P, 4, 512])
                    VTOK = new("VTOK", [P, 4, 512])
                    BETA = new("BETA", [P, 4, 8])
                    G = new("G", [P, 4, 8])
                    with ExitStack() as w2:
                        delta_prep_stage(nc, PS, C, l, QKV, BA, SMALL, KTOK, VTOK, BETA, G, new_in(w2))
                    dump("qkv2", flat(QKV), l)
                    dump("beta", flat(BETA), l)
                    dump("g", flat(G), l)
                    delta_stage(nc, PS, C, QKV, KTOK, VTOK, BETA, G, O2, new)
                dump("o2", flat(O2), l)
                with ExitStack() as w:
                    head_norm_stage(nc, PS, C, O2, Z, PAR[:, 0, DNN:DNN + 1], ODN, new_in(w))
                dump("odn", flat(ODN), l)
            OHG = new_in(mix)("OHG", [P, 4, 512])
            with ExitStack() as hg:
                new = new_in(hg)
                LF = new("LF", [P, 8, 512])
                KK = new("KK", [P, 8, 512])
                HI = new("HI", [P, 4, 512])
                HQ = new("HQ", [P, 4, 512])
                LB, OM, logits = flat(OHG)[:, 0:1024], flat(OHG)[:, 1024:2048], HQ[:, :, :].rearrange("p (a b) n -> p a (b n)", a=2)
                with ExitStack() as w:
                    new = new_in(w)
                    first = HGRN_COL + HGRN_ORDER[0] * 512
                    early = Early(nc, w, new, 8, UNIT, lambda raw, s: [(raw[:, s], w_in_l[:, :, first + s * UNIT:first + (s + 1) * UNIT])])
                    lower_bound_stage(nc, A, SMALL, LB, OM, logits, early)
                    hgrn_proj_stage(nc, PS, l, A["w_in"], H, LB, OM, LF, KK, HI, HQ, OHG, new, early)
                dump("lf", flat(LF), l)
                dump("kk", flat(KK), l)
                O2 = new_in(hg)("O2", [P, 8, 512])
                with ExitStack() as w:
                    hgrn_stage(nc, PS, C, LF, KK, HI, HQ, O2, new_in(w))
                dump("ho2", flat(O2), l)
                with ExitStack() as w:
                    head_norm_stage(nc, PS, C, O2, OHG, PAR[:, 0, HGN:HGN + 1], OHG, new_in(w))
                dump("ohg", flat(OHG), l)
            with ExitStack() as br:
                new = new_in(br)
                M = new("M", [P, 8, 512])
                with ExitStack() as w:
                    new = new_in(w)
                    early = Early(nc, w, new, 12, P, lambda raw, s: branch_pieces(A, l, raw, s, 0))
                    branch_stage(nc, PS, l, A, H, ODN, OHG, M, new, early)
                dump("m", flat(M), l)
                with ExitStack() as w:
                    new = new_in(w)
                    slab_stage(nc, PS, at_layer(A["w_out"], l), M, X, new, early_slabs(nc, w, new, at_layer(A["w_out"], l)))
        dump("xm", flat(X), l)
        with ExitStack() as ffn:
            new = new_in(ffn)
            HID = new("HID", [P, 22, 512])
            slabs = early_slabs(nc, ffn, new, at_layer(A["w_down"], l))
            with ExitStack() as w:
                new = new_in(w)
                early = Early(nc, w, new, 8, UNIT, lambda raw, s: [ffn_piece(A, l, raw, s, 0)])
                pair = split_pair(new)
                with ExitStack() as w2:
                    rms_stage(nc, PS, C, X, pair, PAR[:, 0, FFN:FFN + 8], RS[:, 0, :], 1e-6, new_in(w2), early=early)
                ffn_up_stage(nc, PS, l, A, pair, PAR[:, 1, :], HID, new, early, slabs)
            with ExitStack() as w:
                slab_stage(nc, PS, at_layer(A["w_down"], l), HID, X, new_in(w), slabs)
        dump("x", flat(X), l)


INPUTS = ['x', 'mix_norm', 'w_in', 'dn_conv', 'dn_a_log', 'dn_dt_bias', 'dn_norm', 'hg_lb_logits', 'hg_norm',
          'w_branch_dn', 'w_branch_hg', 'w_out', 'ffn_norm', 'w_up', 'ffn_conv', 'ffn_conv_bias', 'w_down',
          'final_norm', 'norm1_g_2', 'w_in_2', 'gmlp_ln_g_2', 'gmlp_ln_b_2', 'gmlp_ws_2', 'gmlp_bs_2',
          'nsa_q_norm_g_2', 'nsa_k_norm_g_2', 'nsa_cmp_pe_2', 'nsa_cmp_w1_2', 'nsa_cmp_w2_2', 'conf_conv_w_2',
          'conf_conv_b_2', 'conf_ln_g_2', 'conf_ln_b_2', 'sconv_w_2', 'w_branch_2', 'w_gate_2', 'b_gate_2', 'w_out_2',
          'norm2_g_2', 'w_mlp1_2', 'w_mlp2_2']


def kernel(**inputs):
    import concourse.bacc as bacc
    from concourse.bass_utils import run_bass_kernel_spmd as run

    nc = bacc.Bacc("TRN2", target_bir_lowering=False, num_devices=1)
    arrays = {n: np.ascontiguousarray(inputs[n]) for n in INPUTS}
    depth = arrays["w_in"].shape[0]
    arrays["consts"] = constant_table(31, 32, 16)
    arrays["layer"] = np.arange(depth, dtype=np.float32).reshape(depth, 1)
    A = {n: nc.dram_tensor(f"in_{n}", a.shape, mybir.dt.from_np(a.dtype), kind="ExternalInput").ap() for n, a in arrays.items()}
    out = nc.dram_tensor("out", (1, 512, 1024), F32, kind="ExternalOutput").ap()
    build(nc, A, out)
    r = run(nc, [{f"in_{n}": a for n, a in arrays.items()}], core_ids=[0])
    return r.results[0]["out"]
```
